# Optimizing a Trainium2 kernel written in Bass

```python
import jax, jax.numpy as jnp
from jax import lax
import numpy as np

D_MODEL = 1024
BATCH = 1
SEQ = 256
DEPTH = 2
DEC_BATCH = 8
DEC_SEQ = 8
PAST_LEN = 2048
PAGE_SIZE = 128

N_MEM = 256
D_A = 512
K_A = 31
D_B = 1024
K_B = 4
H_B = 8
BW_B = D_B // H_B
LRU_C = 8.0
D_C = 512
H_C = 4
DH_C = D_C // H_C
N_BRANCH = 3
D_IN = 2 * D_A + 2 * D_B + D_C + N_BRANCH * D_MODEL
SPLITS = (2 * D_A, 2 * D_A + D_B, 2 * D_A + 2 * D_B, 2 * D_A + 2 * D_B + D_C)
D_FF = 2816
N_EXPERTS = 8
TOP_K = 2
D_FF_E = 2816
N_DENSE = (DEPTH + 1) // 2
N_MOE = DEPTH // 2
ALPHA = (2.0 * DEPTH) ** 0.25
BETA = (8.0 * DEPTH) ** -0.25
LN_EPS = 1e-5

kernel_name = 'hybrid_conv_rglru_memxattn_decoder_step'

def layer_norm(x, g, b):
    xf = x.astype(jnp.float32)
    mu = jnp.mean(xf, axis=-1, keepdims=True)
    var = jnp.mean(jnp.square(xf - mu), axis=-1, keepdims=True)
    y = (xf - mu) * lax.rsqrt(var + LN_EPS) * g.astype(jnp.float32) + b.astype(jnp.float32)
    return y.astype(x.dtype)

def causal_depthwise_conv(x_full, w, b):
    c = x_full.shape[-1]
    y = lax.conv_general_dilated(x_full, w[:, None, :].astype(x_full.dtype), window_strides=(1,),
                                 padding='VALID', dimension_numbers=('NWC', 'WIO', 'NWC'),
                                 feature_group_count=c)
    return y + b

def rg_lru(x, h0, w_a, b_a, w_x, b_x, lam):
    bsz, t, _ = x.shape
    xh = x.reshape(bsz, t, H_B, BW_B)
    r = jax.nn.sigmoid(jnp.einsum('bthi,hij->bthj', xh, w_a).reshape(bsz, t, D_B) + b_a)
    i = jax.nn.sigmoid(jnp.einsum('bthi,hij->bthj', xh, w_x).reshape(bsz, t, D_B) + b_x)
    log_a = -LRU_C * r.astype(jnp.float32) * jax.nn.softplus(-lam.astype(jnp.float32))
    a = jnp.exp(log_a)
    u = jnp.sqrt(-jnp.expm1(2.0 * log_a)) * (i * x).astype(jnp.float32)
    u = u.at[:, 0].add(a[:, 0] * h0.astype(jnp.float32))

    def combine(left, right):
        return (left[0] * right[0], right[0] * left[1] + right[1])

    _, h = lax.associative_scan(combine, (a, u), axis=1)
    return h.astype(x.dtype), h[:, -1].astype(x.dtype)

def token_mixing(x, buf_a, buf_b, h0, mem_k, mem_v,
                 w_in, b_in, w_conv_a, b_conv_a, ln_a_g, ln_a_b, w_a_out,
                 w_conv_b, b_conv_b, w_rg_a, b_rg_a, w_rg_x, b_rg_x, lru_lambda, w_b_out,
                 w_c_out, w_mix_out):
    bsz, t, _ = x.shape
    z = x @ w_in + b_in
    z_a, z_b, z_g, q, z_m = jnp.split(z, SPLITS, axis=-1)
    u = z_a[..., :D_A] * jax.nn.sigmoid(z_a[..., D_A:])
    u_full = jnp.concatenate([buf_a, u], axis=1)
    c_a = causal_depthwise_conv(u_full, w_conv_a, b_conv_a)
    y_a = jax.nn.silu(layer_norm(c_a, ln_a_g, ln_a_b)) @ w_a_out
    xb_full = jnp.concatenate([buf_b, z_b], axis=1)
    c_b = causal_depthwise_conv(xb_full, w_conv_b, b_conv_b)
    h_seq, h_last = rg_lru(c_b, h0, w_rg_a, b_rg_a, w_rg_x, b_rg_x, lru_lambda)
    y_b = (h_seq * jax.nn.gelu(z_g)) @ w_b_out
    qh = q.reshape(bsz, t, H_C, DH_C)
    s = jnp.einsum('bthd,bmhd->bhtm', qh, mem_k, preferred_element_type=jnp.float32) * (DH_C ** -0.5)
    p = jax.nn.softmax(s, axis=-1)
    o = jnp.einsum('bhtm,bmhd->bthd', p.astype(x.dtype), mem_v).reshape(bsz, t, D_C)
    y_c = o @ w_c_out
    g = jax.nn.sigmoid(z_m).reshape(bsz, t, N_BRANCH, D_MODEL)
    merged = g[:, :, 0] * y_a + g[:, :, 1] * y_b + g[:, :, 2] * y_c
    return (merged @ w_mix_out, u_full[:, -(K_A - 1):], xb_full[:, -(K_B - 1):], h_last)

def swiglu(x, w_g, w_u, w_d):
    return (jax.nn.silu(x @ w_g) * (x @ w_u)) @ w_d

def moe_swiglu(x, w_router, b_router, w_gate, w_up, w_down):
    logits = (x @ w_router + b_router).astype(jnp.float32)
    top_v, top_i = lax.top_k(logits, TOP_K)
    probs = jax.nn.softmax(top_v, axis=-1)
    gates = jnp.sum(jax.nn.one_hot(top_i, N_EXPERTS, dtype=jnp.float32) * probs[..., None], axis=-2).astype(x.dtype)
    out = jnp.zeros_like(x)
    for e in range(N_EXPERTS):
        out = out + gates[..., e:e + 1] * swiglu(x, w_gate[e], w_up[e], w_down[e])
    return out

def setup_inputs(seed: int = 0) -> dict:
    key = jax.random.key(seed)
    ks = jax.random.split(key, 40)

    def nrm(k, shape, scale):
        return jax.random.normal(k, shape, jnp.float32) * scale

    u = jax.random.uniform(ks[20], (DEPTH, D_B), jnp.float32, minval=0.9, maxval=0.999)
    s = u ** (1.0 / LRU_C)
    lru_lambda = jnp.log(s) - jnp.log1p(-s)
    return {
        'x_prompt': nrm(ks[0], (BATCH, SEQ, D_MODEL), 1.0),
        'x_sample': nrm(ks[1], (DEC_BATCH, DEC_SEQ, D_MODEL), 1.0),
        'state_conv_a': nrm(ks[2], (DEPTH, DEC_BATCH, K_A - 1, D_A), 0.5),
        'state_conv_b': nrm(ks[3], (DEPTH, DEC_BATCH, K_B - 1, D_B), 1.0),
        'state_rglru': nrm(ks[4], (DEPTH, DEC_BATCH, D_B), 0.5),
        'cache_mem_k': nrm(ks[5], (DEPTH, DEC_BATCH, N_MEM, H_C, DH_C), 1.0),
        'cache_mem_v': nrm(ks[6], (DEPTH, DEC_BATCH, N_MEM, H_C, DH_C), 1.0),
        'mem_prompt': nrm(ks[7], (BATCH, N_MEM, D_MODEL), 1.0),
        'w_in': nrm(ks[8], (DEPTH, D_MODEL, D_IN), D_MODEL ** -0.5),
        'b_in': nrm(ks[9], (DEPTH, D_IN), 0.02),
        'w_conv_a': nrm(ks[10], (DEPTH, K_A, D_A), K_A ** -0.5),
        'b_conv_a': nrm(ks[11], (DEPTH, D_A), 0.02),
        'ln_a_g': 1.0 + nrm(ks[12], (DEPTH, D_A), 0.02),
        'ln_a_b': nrm(ks[13], (DEPTH, D_A), 0.02),
        'w_a_out': nrm(ks[14], (DEPTH, D_A, D_MODEL), D_A ** -0.5),
        'w_conv_b': nrm(ks[15], (DEPTH, K_B, D_B), K_B ** -0.5),
        'b_conv_b': nrm(ks[16], (DEPTH, D_B), 0.02),
        'w_rg_a': nrm(ks[17], (DEPTH, H_B, BW_B, BW_B), BW_B ** -0.5),
        'b_rg_a': nrm(ks[18], (DEPTH, D_B), 0.02),
        'w_rg_x': nrm(ks[19], (DEPTH, H_B, BW_B, BW_B), BW_B ** -0.5),
        'b_rg_x': nrm(ks[21], (DEPTH, D_B), 0.02),
        'lru_lambda': lru_lambda,
        'w_b_out': nrm(ks[22], (DEPTH, D_B, D_MODEL), D_B ** -0.5),
        'w_mem_kv': nrm(ks[23], (DEPTH, D_MODEL, 2 * D_C), D_MODEL ** -0.5),
        'w_c_out': nrm(ks[24], (DEPTH, D_C, D_MODEL), D_C ** -0.5),
        'w_mix_out': nrm(ks[25], (DEPTH, D_MODEL, D_MODEL), BETA * D_MODEL ** -0.5),
        'ln1_g': 1.0 + nrm(ks[26], (DEPTH, D_MODEL), 0.02),
        'ln1_b': nrm(ks[27], (DEPTH, D_MODEL), 0.02),
        'w_ff_gate': nrm(ks[28], (N_DENSE, D_MODEL, D_FF), D_MODEL ** -0.5),
        'w_ff_up': nrm(ks[29], (N_DENSE, D_MODEL, D_FF), D_MODEL ** -0.5),
        'w_ff_down': nrm(ks[30], (N_DENSE, D_FF, D_MODEL), BETA * D_FF ** -0.5),
        'w_router': nrm(ks[31], (N_MOE, D_MODEL, N_EXPERTS), D_MODEL ** -0.5),
        'b_router': nrm(ks[32], (N_MOE, N_EXPERTS), 0.01),
        'w_e_gate': nrm(ks[33], (N_MOE, N_EXPERTS, D_MODEL, D_FF_E), D_MODEL ** -0.5),
        'w_e_up': nrm(ks[34], (N_MOE, N_EXPERTS, D_MODEL, D_FF_E), D_MODEL ** -0.5),
        'w_e_down': nrm(ks[35], (N_MOE, N_EXPERTS, D_FF_E, D_MODEL), BETA * D_FF_E ** -0.5),
        'ln2_g': 1.0 + nrm(ks[36], (DEPTH, D_MODEL), 0.02),
        'ln2_b': nrm(ks[37], (DEPTH, D_MODEL), 0.02),
    }

def reference(x_prompt, x_sample, state_conv_a, state_conv_b, state_rglru, cache_mem_k, cache_mem_v,
              mem_prompt, w_in, b_in, w_conv_a, b_conv_a, ln_a_g, ln_a_b, w_a_out,
              w_conv_b, b_conv_b, w_rg_a, b_rg_a, w_rg_x, b_rg_x, lru_lambda, w_b_out,
              w_mem_kv, w_c_out, w_mix_out, ln1_g, ln1_b, w_ff_gate, w_ff_up, w_ff_down,
              w_router, b_router, w_e_gate, w_e_up, w_e_down, ln2_g, ln2_b):

    def run_layer(l, x, buf_a, buf_b, h0, mem_k, mem_v):
        mix, nb_a, nb_b, h_last = token_mixing(
            x, buf_a, buf_b, h0, mem_k, mem_v,
            w_in[l], b_in[l], w_conv_a[l], b_conv_a[l], ln_a_g[l], ln_a_b[l], w_a_out[l],
            w_conv_b[l], b_conv_b[l], w_rg_a[l], b_rg_a[l], w_rg_x[l], b_rg_x[l], lru_lambda[l], w_b_out[l],
            w_c_out[l], w_mix_out[l])
        x = layer_norm(ALPHA * x + mix, ln1_g[l], ln1_b[l])
        j = l // 2
        if l % 2 == 0:
            f = swiglu(x, w_ff_gate[j], w_ff_up[j], w_ff_down[j])
        else:
            f = moe_swiglu(x, w_router[j], b_router[j], w_e_gate[j], w_e_up[j], w_e_down[j])
        x = layer_norm(ALPHA * x + f, ln2_g[l], ln2_b[l])
        return x, nb_a, nb_b, h_last

    b_p = x_prompt.shape[0]
    n_mem = mem_prompt.shape[1]
    y_p = x_prompt
    y_s = x_sample
    p_conv_a, p_conv_b, p_h, p_mk, p_mv = [], [], [], [], []
    s_conv_a, s_conv_b, s_h = [], [], []
    for l in range(DEPTH):
        kv = mem_prompt @ w_mem_kv[l]
        mk = kv[..., :D_C].reshape(b_p, n_mem, H_C, DH_C)
        mv = kv[..., D_C:].reshape(b_p, n_mem, H_C, DH_C)
        zero_a = jnp.zeros((b_p, K_A - 1, D_A), x_prompt.dtype)
        zero_b = jnp.zeros((b_p, K_B - 1, D_B), x_prompt.dtype)
        zero_h = jnp.zeros((b_p, D_B), x_prompt.dtype)
        y_p, na, nb, nh = run_layer(l, y_p, zero_a, zero_b, zero_h, mk, mv)
        p_conv_a.append(na)
        p_conv_b.append(nb)
        p_h.append(nh)
        p_mk.append(mk)
        p_mv.append(mv)
        y_s, na, nb, nh = run_layer(l, y_s, state_conv_a[l], state_conv_b[l], state_rglru[l],
                                    cache_mem_k[l], cache_mem_v[l])
        s_conv_a.append(na)
        s_conv_b.append(nb)
        s_h.append(nh)

    return (y_p, y_s, jnp.stack(p_conv_a), jnp.stack(p_conv_b), jnp.stack(p_h), jnp.stack(p_mk), jnp.stack(p_mv),
            jnp.stack(s_conv_a), jnp.stack(s_conv_b), jnp.stack(s_h))


_drawn_inputs = setup_inputs


def setup_inputs(seed=0):
    import zlib

    import numpy as np

    out = dict(_drawn_inputs(seed))
    spreads = {}
    factors = {'b_conv_a': 3.523,
     'ln_a_g': 7.351,
     'ln_a_b': 5.709,
     'b_rg_a': 8.0,
     'b_rg_x': 7.439,
     'b_router': 6.237,
     'cache_mem_k': 3.426,
     'cache_mem_v': 2.96}
    for name, (base, spread) in spreads.items():
        noise = np.random.default_rng([zlib.crc32(name.encode()), seed]).standard_normal(out[name].shape)
        drawn = base * np.exp(spread * noise) if base else spread * noise
        out[name] = __import__('jax').numpy.asarray(drawn.astype(out[name].dtype))
    for name, factor in factors.items():
        out[name] = (out[name] * factor).astype(out[name].dtype)
    return out
```

```python
from contextlib import ExitStack

import concourse.bass as bass
from concourse import mybir

F32 = mybir.dt.float32
I32 = mybir.dt.int32
U32 = mybir.dt.uint32
ALU = mybir.AluOpType
ACT = mybir.ActivationFunctionType
AX = mybir.AxisListType

P = 128
DEPTH = 2
D = 1024
KT = D // P
SEQ, DEC, DSEQ = 256, 8, 8
NSAMP = DEC * DSEQ
T = SEQ + NSAMP
TOK = [(0, 128), (128, 128), (256, 64)]
N_MEM = 256
D_A, K_A = 512, 31
D_B, K_B = 1024, 4
D_C, H_C = 512, 4
JA, JB, JC = D_A // P, D_B // P, D_C // P
D_IN = 2 * D_A + 2 * D_B + D_C + 3 * D
D_FF = 2816
FT = D_FF // P
NE = 8
CAP = T // 2
ALPHA = (2.0 * DEPTH) ** 0.25
EPS = 1e-5
QSCALE = float(P) ** -0.5

LN_STEPS = len(TOK)
HIST = 1 + JB + 2 + JA
SLOTS = 11
UNIT = 1024
BANKS = 8
SEG_A = K_A - 1 + DSEQ
SEG_B = K_B - 1 + DSEQ
LEN_A = K_A - 1 + SEQ + DEC * SEG_A
LEN_B = K_B - 1 + SEQ + DEC * SEG_B

_c = 0
COL = {}
for _name, _n in (("b_in", D_IN // P), ("w_conv_a", JA * K_A), ("b_conv_a", JA), ("ln_a_g", JA), ("ln_a_b", JA),
                  ("w_conv_b", JB * K_B), ("b_conv_b", JB), ("b_rg_a", JB), ("b_rg_x", JB), ("lam", JB)):
    COL[_name] = _c
    _c += _n
NCOL = _c
ZA_U, ZA_G, ZB, ZG, ZQ, ZM = 0, JA, 2 * JA, 2 * JA + JB, 2 * JA + 2 * JB, 2 * JA + 2 * JB + JC


class Tile:

    def __init__(self, bank, use):
        self.bank, self.use, self.done = bank, use, None


class Plan:

    def __init__(self):
        self.steps = 0
        self.tiles = {}
        self.unit_done = []
        self.unit_of = {}

    def tile(self, *key):
        n = len(self.tiles)
        self.tiles[key] = Tile(n % BANKS, n // BANKS)

    def step(self, closes=(), unit=None):
        self.steps += 1
        for key in closes:
            if key not in self.tiles:
                self.tile(*key)
            self.tiles[key].done = self.steps
        if unit is not None:
            self.unit_of[unit] = len(self.unit_done)
            self.unit_done.append(self.steps)


def make_plan():
    p = Plan()
    for l in range(DEPTH):
        for n in range(JB):
            p.step([(l, "zb", n)], (l, "zb", n))
        for n in range(2 * JA):
            p.step([(l, "za", n)], (l, "za", n))
        for n in range(JC):
            p.step([(l, "q", n)], (l, "q", n))
        for n in range(H_C):
            p.step([(l, "k", n)], (l, "k", n))
        for m in range(2):
            p.tile(l, "v", m)
        for c in range(4):
            p.step([(l, "v", m) for m in range(2)] if c == 3 else [], (l, "v", c))
        for n in range(8):
            p.step([(l, "ps", n)])
        for b in range(DEC):
            if b % 4 == 0:
                p.tile(l, "ss", b // 4)
            p.step([(l, "ss", b // 4)] if b % 4 == 3 else [], (l, "ck", b))
        p.step([(l, "mean", 0)])
        for n in range(JB):
            p.step([(l, "zg", n)], (l, "zg", n))
        p.step([(l, "var", 0)])
        for n in range(H_C + 1):
            p.step([(l, "pt", n)])
        for h in range(H_C):
            p.tile(l, "o", h)
        for b in range(DEC):
            p.step([(l, "o", h) for h in range(H_C)] if b == DEC - 1 else [], (l, "cv", b))
        for n in range(2 * JB):
            p.step([(l, "rg", n)], (l, "rg", n // JB) if n % JB == JB - 1 else None)
        for br, y in ((0, "ya"), (2, "yc")):
            for n in range(0, KT, 2):
                p.step([(l, "g", br, n)], (l, "g", br, n))
                p.step([(l, "g", br, n + 1)], (l, "g", br, n + 1))
                p.step([(l, y, n)])
                p.step([(l, y, n + 1)], (l, y, n // 2))
        for n in range(KT):
            p.step([(l, "g", 1, n)], (l, "g", 1, n))
            p.step([(l, "yb", n)], (l, "yb", n))
        for n in range(6):
            p.tile(l, "mix", n)
        for k in range(KT):
            p.step([(l, "mix", n) for n in range(6)] if k == KT - 1 else [], (l, "mix", k))
        for k in range(KT):
            p.step([(l, "xt", k)])
        if l % 2 == 0:
            for f in range(0, FT, 2):
                for w in "gu":
                    for n in (f, f + 1):
                        p.step([(l, w, n)], (l, w, n))
            for n in range(6):
                p.tile(l, "down", n)
            for f in range(FT):
                p.step([(l, "down", n) for n in range(6)] if f == FT - 1 else [], (l, "down", f))
            for k in range(KT):
                p.step([(l, "xt2", k)])
    p.step([("router",)])
    p.step([("pos",)])
    for n in range(4):
        p.step([("gather0", n)])
    first, first_unit, first_tile = p.steps, len(p.unit_done), len(p.tiles)
    for f in range(0, FT, 2):
        for w in "gu":
            p.tile("e", w, f // 2)
            for n in (f, f + 1):
                p.step([("e", w, f // 2)] if n == f + 1 else [], ("e", w, n))
    for n in range(4):
        p.step([("e", "gather", n)])
    for n in range(4):
        p.tile("e", "down", n)
    for f in range(FT):
        p.step([("e", "down", n) for n in range(4)] if f == FT - 1 else [], ("e", "down", f))
    for n in range(2):
        p.step([("e", "pt", n)])
    for n in range(4):
        p.step([("e", "yt", n)])
    for n in range(12):
        p.step([("e", "y", n)])
    p.per_steps = p.steps - first
    p.per_units = len(p.unit_done) - first_unit
    p.loop_unit = first_unit
    per_tiles = len(p.tiles) - first_tile
    assert per_tiles % BANKS == 0 and p.per_units % SLOTS == 0
    p.per_use = per_tiles // BANKS
    p.per_slot = p.per_units // SLOTS
    return p


def trunk(nc, x0, x0T, memT, chan, rows, hist, stream, router_w, router_b, experts,
          y, o_a, o_b, o_h, o_k, o_v):
    plan = make_plan()
    n_units = plan.loop_unit
    assert stream.shape[0] == n_units

    with ExitStack() as ctx:
        def sb(name, shape, dt=F32):
            return ctx.enter_context(nc.sbuf_tensor(name, shape, dt))

        def sem(name):
            return ctx.enter_context(nc.semaphore(name))

        psum = ctx.enter_context(nc.psum_tensor("psum", [P, BANKS, 512], F32))
        ring = sb("ring", [P, SLOTS, UNIT])
        x = sb("x", [P, 3, D])
        xT = sb("xT", [P, KT, T])
        mem = sb("mem", [P, KT, N_MEM])
        lnp = sb("lnp", [P, 4, D])
        par = sb("par", [P, DEPTH, NCOL])
        ident = sb("ident", [P, P])
        ones = sb("ones", [P, P])
        upper = sb("upper", [P, P])
        iota = sb("iota", [P, CAP])
        small = sb("small", [P, 256])
        tails = sb("tails", [P, 288])
        stat = sb("stat", [P, 50])
        spl = sb("spl", [P, DEPTH * JB])
        nvi = sb("nvi", [P, 1], I32)

        arena = sb("arena", [P, 28248])
        off = [0]

        def cut(n, a=None):
            at = off[0]
            off[0] += n
            v = arena[:, at:at + n]
            return v.rearrange("p (a b) -> p a b", a=a) if a else v

        ig_flat = arena[:, 0:JB * T]
        ua = arena[:, 0:JA * LEN_A].rearrange("p (a b) -> p a b", a=JA)
        ig = cut(JB * T, JB)
        w_flat = arena[:, off[0]:off[0] + JB * T]
        w_b = w_flat.rearrange("p (a b) -> p a b", a=JB)
        zb = cut(JB * LEN_B, JB)
        sg = cut(JA * T, JA)
        ca = cut(JA * T, JA)
        cb = cut(JB * T, JB)
        qT = cut(JC * T, JC)
        qpad = cut(DEC * P, DEC)
        kT = cut(H_C * N_MEM, H_C)
        vm = cut(2 * D_C, 2)
        pp = arena[:, off[0]:off[0] + 2560].rearrange("p (a b) -> p a b", a=10)
        mg = cut(KT * T, KT)
        pT = arena[:, off[0]:off[0] + 2560].rearrange("p (a b) -> p a b", a=5)
        aa = cut(JB * T, JB)
        oT = cut(JC * T, JC)
        rr = cut(JB * T, JB)
        gg_flat = arena[:, off[0]:off[0] + JB * T]
        gg = cut(JB * T, JB)
        sa_flat = arena[:, off[0]:off[0] + JA * T]
        sa = cut(JA * T, JA)
        gt = cut(2 * T, 2)
        hist_a = gg_flat[:, 0:JA * DEC * (K_A - 1)].rearrange("p (a b c) -> p a b c", a=JA, b=DEC)
        tail_a = sa_flat[:, 0:JA * 9 * (K_A - 1)].rearrange("p (a b c) -> p a b c", a=JA, b=9)
        hist_b = small[:, 0:192].rearrange("p (a b c) -> p a b c", a=JB, b=DEC)
        h0 = small[:, 192:256].rearrange("p (a b) -> p a b", a=JB)
        tail_b = tails[:, 0:216].rearrange("p (a b c) -> p a b c", a=JB, b=9)
        tail_h = tails[:, 216:288].rearrange("p (a b) -> p a b", a=JB)
        off[0] = 0
        hT = cut(FT * T, FT)
        dsig = cut(2 * T, 2)
        dlin = cut(2 * T, 2)
        off[0] = 0
        yacc = cut(3 * D, 3)
        xe = cut(KT * CAP, KT)
        he = cut(FT * CAP, FT)
        ye = cut(KT * CAP, KT)
        y0 = cut(D)
        y1 = cut(D)
        pg0 = cut(T)
        pg1 = cut(T)
        pick = cut(3 * CAP, 3)
        pickg = cut(3 * CAP, 3)
        esig = cut(2 * 2 * CAP, 2)
        elin = cut(2 * 2 * CAP, 2)
        wr = cut(KT * NE, KT)
        brow = cut(NE)
        lg = cut(3 * NE, 3)
        top = cut(3 * 8, 3)
        topf = cut(3 * 2, 3)
        gate2 = cut(3 * 2, 3)
        den = cut(3)
        m1 = cut(3 * NE, 3)
        m2 = cut(3 * NE, 3)
        hit = cut(3 * NE, 3)
        gates = cut(3 * (2 * NE), 3)
        slot = cut(3 * (2 * NE + 1), 3)
        nmax = cut(2)
        eps_c = sb("eps_c", [P, 1])
        stats = sb("stats", [P, 3, 2, 6])
        mv = sb("mv", [P, 3, 4])
        lamw = sb("lamw", [P, 6, DEPTH, JB])
        topi = sb("topi", [P, 3, 8], U32)

        slot_full = [sem(f"slot_full{s}") for s in range(SLOTS)]
        mm_done = sem("mm_done")
        evac = [sem(f"evac{b}") for b in range(BANKS)]
        x_in, xt_in, mem_in, par_in = sem("x_in"), sem("xt_in"), sem("mem_in"), sem("par_in")
        ln_in = [sem("ln1_in"), sem("ln2_in")]
        hist_in, hist_small_in = sem("hist_in"), sem("hist_small_in")
        router_in = sem("router_in")
        kv_out, tail_a_out, tail_b_out, h_out, y_out = (sem("kv_out"), sem("tail_a_out"), sem("tail_b_out"),
                                                        sem("h_out"), sem("y_out"))
        const_step, const_ready = sem("const_step"), sem("const_ready")
        pool_step = sem("pool_step")
        hist_ready = sem("hist_ready")
        tails_ready = sem("tails_ready")
        htail_ready = sem("htail_ready")
        dve_step = sem("dve_step")
        spl_exp, spl_ready = sem("spl_exp"), sem("spl_ready")
        spl_ask = sem("spl_ask")
        eps_ready, bn_done, sa_lin, mg_part = sem("eps_ready"), sem("bn_done"), sem("sa_lin"), sem("mg_part")
        yacc_ready, lg_zero, pos_read = sem("yacc_ready"), sem("lg_zero"), sem("pos_read")
        glu_done = sem("glu_done")
        conv_b_done = sem("conv_b_done")
        conv_a_tap = sem("conv_a_tap")
        negmax = sem("negmax")
        probs = sem("probs")
        dev_ready, sq_ready = sem("dev_ready"), sem("sq_ready")
        lna_norm, lna_sig, lna_done = sem("lna_norm"), sem("lna_sig"), sem("lna_done")
        tanh_done = sem("tanh_done")
        a2_ready, root_ready = sem("a2_ready"), sem("root_ready")
        h_ready, hg_ready = sem("h_ready"), sem("hg_ready")
        var_ready, std_ready, x_ready = sem("var_ready"), sem("std_ready"), sem("x_ready")
        top_ready, exp_ready = sem("top_ready"), sem("exp_ready")
        hit_ready, nv_ready, pick_ready, pickg_ready = (sem("hit_ready"), sem("nv_ready"), sem("pick_ready"),
                                                        sem("pickg_ready"))
        mg_ready = sem("mg_ready")
        dsig_ready, esig_ready = sem("dsig_ready"), sem("esig_ready")

        def tile_of(*key):
            return plan.tiles[key]

        def bank(*key):
            return psum[:, plan.tiles[key].bank, :]

        def filled(eng, *key, i=None):
            v = plan.tiles[key].done
            eng.wait_ge(mm_done, v if i is None else i * plan.per_steps + v)

        def emptied(eng, *key, i=None):
            t = plan.tiles[key]
            eng.wait_ge(evac[t.bank], t.use + 1 if i is None else i * plan.per_use + (t.use + 1))

        def frees(ins, *key):
            ins.then_inc(evac[plan.tiles[key].bank], 1)

        def take(eng, *key, i=None):
            t = plan.tiles[key]
            if i is not None:
                eng.wait_ge(evac[t.bank], i * plan.per_use + t.use)
            elif t.use:
                eng.wait_ge(evac[t.bank], t.use)

        def weights(eng, *key, i=None):
            u = plan.unit_of[key]
            v = 16 * (u // SLOTS + 1)
            eng.wait_ge(slot_full[u % SLOTS], v if i is None else i * (16 * plan.per_slot) + v)
            return ring[:, u % SLOTS, :]

        def samp(v):
            return v.rearrange("p (b t) -> p b t", b=DEC)

        def seg_a(j, k, n):
            return ua[:, j, K_A - 1 + SEQ:LEN_A].rearrange("p (b s) -> p b s", b=DEC)[:, :, k:k + n]

        def seg_b(j, k, n):
            return zb[:, j, K_B - 1 + SEQ:LEN_B].rearrange("p (b s) -> p b s", b=DEC)[:, :, k:k + n]

        def col(l, name, n=0, w=1):
            c = COL[name] + n
            return par[:, l, c:c + w]

        def pair(v, n):
            return v[:, 2 * n:2 * n + 2].rearrange("p a b -> p (a b)")

        def xe_pair(n):
            return pair(xe, n)

        def ye_pair(n):
            return pair(ye, n)

        def he_pair(n):
            return pair(he, n)

        def layer_norm_std(act, n):
            act.wait_ge(eps_ready, 1)
            for t, (_, r) in enumerate(TOK):
                act.wait_ge(var_ready, 3 * n + t + 1)
                act.activation(mv[0:r, t, 2:3], mv[0:r, t, 1:2], ACT.Sqrt, bias=eps_c[0:r, 0:1])\
                   .then_inc(std_ready, 1)

        block = ctx.enter_context(nc.Block())

        @block.sync
        def _(sp):
            for u in range(n_units + SLOTS):
                s = u % SLOTS
                if u >= SLOTS:
                    sp.wait_ge(mm_done, plan.unit_done[u - SLOTS])
                src = stream[u] if u < n_units else experts[u - n_units]
                sp.dma_start(ring[:, s, :], src).then_inc(slot_full[s], 16)

            def expert(i, e):
                for k in range(plan.per_units):
                    u = plan.loop_unit + k
                    sp.wait_ge(mm_done, i * plan.per_steps + plan.unit_done[u])
                    sp.dma_start(ring[:, u % SLOTS, :], experts[e * plan.per_units + (SLOTS + k)])\
                        .then_inc(slot_full[u % SLOTS], 16)

            with sp.Fori(0, NE) as i:
                expert(i, i)
            sp.wait_ge(nv_ready, 1)
            nv = sp.value_load(nvi[0:1, 0:1], min_val=NE, max_val=2 * NE)
            with sp.If(nv > NE):
                with sp.Fori(NE, 2 * NE) as i:
                    expert(i, i - NE)

        @block.gpsimd
        def _(pool):
            pool.dma_start(xT[:], x0T).then_inc(xt_in, 16)
            pool.dma_start(par[:], chan.rearrange("l p c -> p l c")).then_inc(par_in, 16)
            pool.dma_start(mem[:], memT).then_inc(mem_in, 16)
            pool.memset(ones[:], 1.0).then_inc(const_step, 1)
            pool.memset(ident[:], 0.0).then_inc(const_step, 1)
            pool.iota(iota[:], pattern=[[1, CAP]], base=0, channel_multiplier=0,
                      allow_small_or_imprecise_dtypes=True).then_inc(const_ready, 1)
            pool.wait_ge(const_step, 2)
            pool.affine_select(out=ident[:], in_=ident[:], compare_op=ALU.not_equal, fill=1.0, base=0,
                               pattern=[[-1, P]], channel_multiplier=1).then_inc(const_ready, 1)
            pool.affine_select(out=upper[:], in_=ones[:], compare_op=ALU.is_gt, fill=0.0, base=0,
                               pattern=[[1, P]], channel_multiplier=-1).then_inc(const_ready, 1)
            for l in range(DEPTH):
                if l:
                    pool.wait_ge(x_ready, LN_STEPS * 2 * l)
                for n in range(2):
                    pool.dma_start(lnp[:, 2 * n:2 * n + 2, :], rows[l, 2 * n:2 * n + 2].partition_broadcast(P))\
                        .then_inc(ln_in[n], 16)
                pool.dma_start(small[:], hist[l, :, JA * DEC * (K_A - 1):]).then_inc(hist_small_in, 16)
                pool.dma_start(gg_flat[:, 0:JA * DEC * (K_A - 1)], hist[l, :, 0:JA * DEC * (K_A - 1)])\
                    .then_inc(hist_in, 16)
                if l == 0:
                    for t, (r0, n) in enumerate(TOK):
                        pool.dma_start(x[0:n, t, :], x0[r0:r0 + n]).then_inc(x_in, 16)
                pool.memset(zb[:, :, 0:K_B - 1], 0.0).then_inc(hist_ready, 1)
                pool.wait_ge(hist_small_in, 16 * (l + 1))
                for j in range(JB):
                    pool.tensor_copy(seg_b(j, 0, K_B - 1), hist_b[:, j]).then_inc(hist_ready, 1)
                pool.memset(ua[:, :, 0:K_A - 1], 0.0).then_inc(hist_ready, 1)
                pool.memset(qpad[:], 0.0).then_inc(hist_ready, 1)
                pool.wait_ge(hist_in, 16 * (l + 1))
                for j in range(JA):
                    pool.tensor_copy(seg_a(j, 0, K_A - 1), hist_a[:, j]).then_inc(hist_ready, 1)
                for j in range(JB):
                    emptied(pool, l, "zb", j)
                pool.wait_ge(hist_ready, (l + 1) * HIST)
                if l:
                    pool.wait_ge(tail_b_out, 16 * l)
                    pool.wait_ge(h_out, 16 * l)
                for j in range(JB):
                    pool.tensor_copy(tail_b[:, j, 0, :], zb[:, j, SEQ:SEQ + K_B - 1]).then_inc(tails_ready, 1)
                    pool.tensor_copy(tail_b[:, j, 1:9, :], seg_b(j, DSEQ, K_B - 1)).then_inc(tails_ready, 1)
                pool.wait_ge(glu_done, 2 * JA * (l + 1))
                for j in range(JA):
                    pool.tensor_copy(tail_a[:, j, 0, :], ua[:, j, SEQ:SEQ + K_A - 1]).then_inc(tails_ready, 1)
                    pool.tensor_copy(tail_a[:, j, 1:9, :], seg_a(j, DSEQ, K_A - 1)).then_inc(tails_ready, 1)
                pool.wait_ge(tails_ready, 2 * (JA + JB) * (l + 1))
                pool.dma_start(o_b[l], tails[:, 0:216]).then_inc(tail_b_out, 16)
                pool.dma_start(o_a[l], sa_flat[:, 0:JA * 9 * (K_A - 1)]).then_inc(tail_a_out, 16)
                for n in range(H_C):
                    emptied(pool, l, "k", n)
                for n in range(2):
                    emptied(pool, l, "v", n)
                pool.dma_start(o_k[l], kT[:]).then_inc(kv_out, 16)
                pool.dma_start(o_v[l], vm[:]).then_inc(kv_out, 16)
                pool.wait_ge(h_ready, l + 1)
                pool.tensor_copy(tail_h[:, :, 0:1], cb[:, :, SEQ - 1:SEQ]).then_inc(htail_ready, 1)
                pool.tensor_copy(tail_h[:, :, 1:9], cb[:, :, SEQ + DSEQ - 1:T:DSEQ]).then_inc(htail_ready, 1)
                pool.wait_ge(htail_ready, 2 * (l + 1))
                pool.dma_start(o_h[l], tails[:, 216:288]).then_inc(h_out, 16)
            pool.wait_ge(x_ready, LN_STEPS * (2 * DEPTH - 1))
            pool.wait_ge(kv_out, 32 * DEPTH)
            pool.wait_ge(tail_a_out, 16 * DEPTH)
            pool.dma_start(wr[:], router_w).then_inc(router_in, 16)
            pool.dma_start(brow, router_b.partition_broadcast(P)).then_inc(router_in, 16)
            pool.wait_ge(x_ready, LN_STEPS * 2 * DEPTH)
            for t, (r0, n) in enumerate(TOK):
                pool.dma_start(y[r0:r0 + n], yacc[0:n, t, :]).then_inc(y_out, 16)
            pool.wait_ge(y_out, 48)
            pool.wait_ge(h_out, 16 * DEPTH)
            pool.wait_ge(kv_out, 32 * DEPTH)
            pool.wait_ge(tail_a_out, 16 * DEPTH)
            pool.wait_ge(tail_b_out, 16 * DEPTH)
            nv = pool.value_load(nvi[0:1, 0:1], min_val=NE, max_val=2 * NE)
            for s in range(SLOTS):
                before = len(range(s, n_units + SLOTS, SLOTS))
                pool.wait_ge(slot_full[s], nv * (16 * plan.per_slot) + 16 * before)

        @block.scalar
        def _(act):
            def ident_bias(out, in_, bias):
                return act.activation(out, in_, ACT.Identity, bias=bias)

            act.wait_ge(spl_ask, 1)
            act.activation(lamw[:, 1], lamw[:, 0], ACT.Exp).then_inc(spl_exp, 1)
            for l in range(DEPTH):
                for n in range(JB):
                    filled(act, l, "zb", n)
                    b = col(l, "b_in", ZB + n)
                    ident_bias(zb[:, n, K_B - 1:K_B - 1 + SEQ], bank(l, "zb", n)[:, 0:SEQ], b)
                    frees(ident_bias(seg_b(n, K_B - 1, DSEQ), samp(bank(l, "zb", n)[:, SEQ:T]), b), l, "zb", n)
                for n in range(JA):
                    filled(act, l, "za", 2 * n + 1)
                    frees(act.activation(sg[:, n], bank(l, "za", 2 * n + 1)[:, 0:T], ACT.Sigmoid,
                                         bias=col(l, "b_in", ZA_G + n)), l, "za", 2 * n + 1)
                act.wait_ge(hist_ready, HIST * l + 1 + JB + 2)
                for n in range(JC):
                    filled(act, l, "q", n)
                    b = col(l, "b_in", ZQ + n)
                    ident_bias(qpad[:, :, 40 * n:40 * n + DSEQ], samp(bank(l, "q", n)[:, SEQ:T]), b)
                    frees(ident_bias(qT[:, n], bank(l, "q", n)[:, 0:T], b), l, "q", n)
                for n in range(H_C):
                    filled(act, l, "k", n)
                    frees(act.copy(kT[:, n], bank(l, "k", n)[:, 0:N_MEM]), l, "k", n)
                for n in range(2):
                    filled(act, l, "v", n)
                    frees(act.copy(vm[:, n], bank(l, "v", n)), l, "v", n)
                for n in range(10):
                    key = (l, "ps", n) if n < 8 else (l, "ss", n - 8)
                    act.wait_ge(negmax, 10 * l + n + 1)
                    frees(act.activation(pp[:, n], bank(*key)[:, 0:N_MEM], ACT.Exp, bias=stat[:, 20 + n:21 + n],
                                         scale=QSCALE, accum_out=stat[:, 30 + n:31 + n]), *key)
                act.wait_ge(hist_ready, HIST * (l + 1))
                for n in range(JB):
                    filled(act, l, "zg", n)
                    frees(act.activation(gg[:, n], bank(l, "zg", n)[:, 0:T], ACT.Gelu_apprx_tanh,
                                         bias=col(l, "b_in", ZG + n)), l, "zg", n)
                filled(act, l, "var", 0)
                frees(act.activation(gt[:, 0], bank(l, "var", 0)[:, 0:T], ACT.Sqrt, scale=1.0 / D_A,
                                     bias=eps_c[:, 0:1]), l, "var", 0)
                for n in range(H_C + 1):
                    filled(act, l, "pt", n)
                    frees(act.copy(pT[:, n], bank(l, "pt", n)), l, "pt", n)
                act.wait_ge(lna_norm, l + 1)
                for n in range(JA):
                    act.activation(sg[:, n], ca[:, n], ACT.Sigmoid, scale=col(l, "ln_a_g", n),
                                   bias=col(l, "ln_a_b", n)).then_inc(lna_sig, 1)
                for n in range(H_C):
                    filled(act, l, "o", n)
                    frees(act.copy(oT[:, n], bank(l, "o", n)[:, 0:T]), l, "o", n)
                act.wait_ge(spl_ready, 1)
                for n in range(JB):
                    filled(act, l, "rg", n)
                    frees(act.activation(rr[:, n], bank(l, "rg", n)[:, 0:T], ACT.Sigmoid,
                                         bias=col(l, "b_rg_a", n)), l, "rg", n)
                for n in range(JB):
                    emptied(act, l, "rg", n)
                    act.activation(rr[:, n], rr[:, n], ACT.Tanh,
                                   scale=spl[:, JB * l + n:JB * l + n + 1]).then_inc(tanh_done, 1)
                act.wait_ge(conv_a_tap, K_A * (l + 1))
                act.wait_ge(tails_ready, 2 * (JA + JB) * (l + 1))
                for n in range(JB):
                    filled(act, l, "rg", JB + n)
                    frees(act.activation(ig[:, n], bank(l, "rg", JB + n)[:, 0:T], ACT.Sigmoid,
                                         bias=col(l, "b_rg_x", n)), l, "rg", JB + n)
                q = 0
                before = []
                for br, yk in ((0, "ya"), (2, "yc"), (1, "yb")):
                    for n in range(KT):
                        if br == 0 and n == 2:
                            act.wait_ge(a2_ready, l + 1)
                            act.activation(rr[:], rr[:], ACT.Sqrt).then_inc(root_ready, 1)
                        filled(act, l, "g", br, n)
                        if q >= 2:
                            emptied(act, *before[q - 2])
                        frees(act.activation(gt[:, q % 2], bank(l, "g", br, n)[:, 0:T], ACT.Sigmoid,
                                             bias=col(l, "b_in", ZM + KT * br + n)), l, "g", br, n)
                        before.append((l, yk, n))
                        q += 1
                layer_norm_std(act, 2 * l)
                for k in range(KT):
                    filled(act, l, "xt", k)
                    frees(act.copy(xT[:, k], bank(l, "xt", k)[:, 0:T]), l, "xt", k)
                if l % 2 == 0:
                    for f in range(FT):
                        filled(act, l, "g", f)
                        if f >= 2:
                            emptied(act, l, "g", f - 2)
                        act.activation(dsig[:, f % 2], bank(l, "g", f)[:, 0:T], ACT.Sigmoid).then_inc(dsig_ready, 1)
                    layer_norm_std(act, 2 * l + 1)
                    for k in range(KT):
                        filled(act, l, "xt2", k)
                        frees(act.copy(xT[:, k], bank(l, "xt2", k)[:, 0:T]), l, "xt2", k)
            act.wait_ge(top_ready, 1)
            act.activation(gate2[:, :, 1], gate2[:, :, 0], ACT.Exp).then_inc(exp_ready, 1)
            for n in range(4):
                filled(act, "gather0", n)
                frees(act.copy(xe_pair(n), bank("gather0", n)[:, 0:2 * CAP]), "gather0", n)
            act.wait_ge(nv_ready, 1)
            nv = act.value_load(nvi[0:1, 0:1], min_val=NE, max_val=2 * NE)
            with act.Fori(0, nv) as i:
                for f in range(FT // 2):
                    filled(act, "e", "g", f, i=i)
                    if f >= 2:
                        emptied(act, "e", "g", f - 2, i=i)
                    act.activation(esig[:, f % 2], bank("e", "g", f)[:, 0:2 * CAP], ACT.Sigmoid)\
                        .then_inc(esig_ready, 1)
                for n in range(4):
                    filled(act, "e", "gather", n, i=i)
                    frees(act.copy(xe_pair(n), bank("e", "gather", n)[:, 0:2 * CAP]), "e", "gather", n)
                for n in range(4):
                    filled(act, "e", "down", n, i=i)
                    frees(act.copy(ye_pair(n), bank("e", "down", n)[:, 0:2 * CAP]), "e", "down", n)
                filled(act, "e", "pt", 0, i=i)
                frees(act.copy(pg0, bank("e", "pt", 0)[:, 0:T]), "e", "pt", 0)
                filled(act, "e", "pt", 1, i=i)
                frees(act.copy(pg1[0:CAP - P], bank("e", "pt", 1)[0:CAP - P, 0:T]), "e", "pt", 1)
                for n in range(2):
                    filled(act, "e", "yt", n, i=i)
                    frees(act.copy(y0[:, 512 * n:512 * n + 512], bank("e", "yt", n)), "e", "yt", n)
                for n in range(2):
                    filled(act, "e", "yt", 2 + n, i=i)
                    frees(act.copy(y1[0:CAP - P, 512 * n:512 * n + 512], bank("e", "yt", 2 + n)[0:CAP - P]),
                          "e", "yt", 2 + n)
            layer_norm_std(act, 2 * DEPTH - 1)

        @block.vector
        def _(dve):
            steps = [0]

            def link(ins):
                steps[0] += 1
                ins.then_inc(dve_step, 1)
                dve.wait_ge(dve_step, steps[0])

            def mac(out, in0, scalar, in1):
                return dve.scalar_tensor_tensor(out=out, in0=in0, scalar=scalar, in1=in1, op0=ALU.mult, op1=ALU.add)

            def over(v, n):
                return v.unsqueeze(1).to_broadcast([P, n, v.shape[-1]])

            def layer_norm(n, v):
                dve.wait_ge(ln_in[n % 2], 16 * (n // 2 + 1))
                for t, (_, r) in enumerate(TOK):
                    for c in range(2):
                        dve.bn_stats(stats[0:r, t, c], v[0:r, t, 512 * c:512 * c + 512]).then_inc(bn_done, 1)
                dve.wait_ge(bn_done, 6 * (n + 1))
                for t, (_, r) in enumerate(TOK):
                    dve.bn_aggr(mv[0:r, t, 0:2], stats[0:r, t]).then_inc(var_ready, 1)
                for t, (_, r) in enumerate(TOK):
                    dve.wait_ge(std_ready, 3 * n + t + 1)
                    link(dve.reciprocal(mv[0:r, t, 2:3], mv[0:r, t, 2:3]))
                    link(dve.tensor_scalar(v[0:r, t, :], v[0:r, t, :], mv[0:r, t, 0:1], mv[0:r, t, 2:3],
                                           ALU.subtract, ALU.mult))
                    link(dve.tensor_tensor(v[0:r, t, :], v[0:r, t, :], lnp[0:r, 2 * (n % 2), :], ALU.mult))
                    dve.tensor_tensor(v[0:r, t, :], v[0:r, t, :], lnp[0:r, 2 * (n % 2) + 1, :], ALU.add)\
                       .then_inc(x_ready, 1)
                dve.wait_ge(x_ready, 3 * (n + 1))

            def residual(l, name):
                for n in range(6):
                    t, c = n // 2, n % 2
                    r = TOK[t][1]
                    filled(dve, l, name, n)
                    frees(dve.scalar_tensor_tensor(out=x[0:r, t, 512 * c:512 * c + 512],
                                                   in0=x[0:r, t, 512 * c:512 * c + 512], scalar=ALPHA,
                                                   in1=bank(l, name, n)[0:r], op0=ALU.mult, op1=ALU.add),
                          l, name, n)
                for n in range(6):
                    emptied(dve, l, name, n)

            dve.memset(eps_c[:], EPS).then_inc(eps_ready, 1)
            dve.wait_ge(par_in, 16)
            lam = par[:, :, COL["lam"]:COL["lam"] + JB]
            link(dve.tensor_scalar(lamw[:, 2], lam, -1.0, None, ALU.mult))
            dve.tensor_tensor(lamw[:, 0], lam, lamw[:, 2], ALU.min).then_inc(spl_ask, 1)
            dve.wait_ge(spl_exp, 1)
            link(dve.tensor_scalar(lamw[:, 0], lamw[:, 1], 2.0, None, ALU.add))
            link(dve.reciprocal(lamw[:, 0], lamw[:, 0]))
            link(dve.tensor_tensor(lamw[:, 0], lamw[:, 0], lamw[:, 1], ALU.mult))
            link(dve.tensor_tensor(lamw[:, 3], lamw[:, 0], lamw[:, 0], ALU.mult))
            link(dve.tensor_scalar(lamw[:, 4], lamw[:, 3], 1.0 / 17, 1.0 / 15, ALU.mult, ALU.add))
            for k in (13, 11, 9, 7, 5, 3, 1):
                link(dve.tensor_tensor(lamw[:, 4], lamw[:, 4], lamw[:, 3], ALU.mult))
                link(dve.tensor_scalar(lamw[:, 4], lamw[:, 4], 1.0 / k, None, ALU.add))
            link(dve.tensor_tensor(lamw[:, 4], lamw[:, 4], lamw[:, 0], ALU.mult))
            link(dve.tensor_scalar(lamw[:, 4], lamw[:, 4], 2.0, None, ALU.mult))
            link(dve.tensor_scalar(lamw[:, 2], lamw[:, 2], 0.0, None, ALU.max))
            link(dve.tensor_tensor(lamw[:, 4], lamw[:, 4], lamw[:, 2], ALU.add))
            dve.tensor_scalar(spl[:].rearrange("p (l j) -> p l j", l=DEPTH), lamw[:, 4], -4.0, None, ALU.mult)\
               .then_inc(spl_ready, 1)

            for l in range(DEPTH):
                dve.wait_ge(hist_ready, HIST * l + 1 + JB)
                for j0 in range(0, JB, 2):
                    for j in (j0, j0 + 1):
                        emptied(dve, l, "zb", j)
                    for k in range(K_B):
                        for j in (j0, j0 + 1):
                            w = col(l, "w_conv_b", K_B * j + k)
                            for out, in_ in ((cb[:, j, 0:SEQ], zb[:, j, k:k + SEQ]),
                                             (samp(cb[:, j, SEQ:T]), seg_b(j, k, DSEQ))):
                                if k == 0:
                                    ins = dve.tensor_scalar(out, in_, w, col(l, "b_conv_b", j), ALU.mult, ALU.add)
                                else:
                                    ins = mac(out, in_, w, out)
                        if k < K_B - 1:
                            link(ins)
                        else:
                            ins.then_inc(conv_b_done, 1)
                dve.wait_ge(hist_ready, HIST * (l + 1))
                for j in range(JA):
                    filled(dve, l, "za", 2 * j)
                    emptied(dve, l, "za", 2 * j + 1)
                    b = col(l, "b_in", ZA_U + j)
                    z = bank(l, "za", 2 * j)
                    dve.scalar_tensor_tensor(out=ua[:, j, K_A - 1:K_A - 1 + SEQ], in0=z[:, 0:SEQ], scalar=b,
                                             in1=sg[:, j, 0:SEQ], op0=ALU.add, op1=ALU.mult).then_inc(glu_done, 1)
                    dve.wait_ge(glu_done, 2 * (JA * l + j) + 1)
                    dve.scalar_tensor_tensor(out=seg_a(j, K_A - 1, DSEQ), in0=samp(z[:, SEQ:T]), scalar=b,
                                             in1=samp(sg[:, j, SEQ:T]), op0=ALU.add, op1=ALU.mult)\
                       .then_inc(glu_done, 1)
                    dve.wait_ge(glu_done, 2 * (JA * l + j + 1))
                    frees(dve.tensor_scalar(ca[:, j, 0:SEQ], ua[:, j, 0:SEQ], col(l, "w_conv_a", K_A * j),
                                            col(l, "b_conv_a", j), ALU.mult, ALU.add), l, "za", 2 * j)
                    ins = dve.tensor_scalar(samp(ca[:, j, SEQ:T]), seg_a(j, 0, DSEQ), col(l, "w_conv_a", K_A * j),
                                            col(l, "b_conv_a", j), ALU.mult, ALU.add)
                ins.then_inc(conv_a_tap, 1)
                for k in range(1, K_A):
                    dve.wait_ge(conv_a_tap, K_A * l + k)
                    for j in range(JA):
                        w = col(l, "w_conv_a", K_A * j + k)
                        mac(ca[:, j, 0:SEQ], ua[:, j, k:k + SEQ], w, ca[:, j, 0:SEQ])
                        ins = mac(samp(ca[:, j, SEQ:T]), seg_a(j, k, DSEQ), w, samp(ca[:, j, SEQ:T]))
                    ins.then_inc(conv_a_tap, 1)
                for n in range(10):
                    key = (l, "ps", n) if n < 8 else (l, "ss", n - 8)
                    filled(dve, *key)
                    link(dve.reduce_max(stat[:, 10 + n:11 + n], bank(*key)[:, 0:N_MEM], AX.X))
                    dve.tensor_scalar(stat[:, 20 + n:21 + n], stat[:, 10 + n:11 + n], -QSCALE, None, ALU.mult)\
                       .then_inc(negmax, 1)
                filled(dve, l, "mean", 0)
                frees(mac(ca[:], over(bank(l, "mean", 0)[:, 0:T], JA), -1.0 / D_A, ca[:]), l, "mean", 0)
                emptied(dve, l, "mean", 0)
                dve.tensor_tensor(sg[:], ca[:], ca[:], ALU.mult).then_inc(dev_ready, 1)
                for n in range(10):
                    emptied(dve, *((l, "ps", n) if n < 8 else (l, "ss", n - 8)))
                link(dve.reciprocal(stat[:, 40:50], stat[:, 30:40]))
                for n in range(10):
                    dve.tensor_scalar(pp[:, n], pp[:, n], stat[:, 40 + n:41 + n], None, ALU.mult).then_inc(probs, 1)
                emptied(dve, l, "var", 0)
                link(dve.reciprocal(gt[:, 0], gt[:, 0]))
                dve.tensor_tensor(ca[:], ca[:], over(gt[:, 0], JA), ALU.mult).then_inc(lna_norm, 1)
                dve.wait_ge(lna_norm, l + 1)
                dve.wait_ge(tail_a_out, 16 * (l + 1))
                for j in range(JA):
                    dve.tensor_scalar(sa[:, j], ca[:, j], col(l, "ln_a_g", j), col(l, "ln_a_b", j),
                                      ALU.mult, ALU.add).then_inc(sa_lin, 1)
                for j in range(JA):
                    dve.wait_ge(sa_lin, JA * l + j + 1)
                    dve.wait_ge(lna_sig, JA * l + j + 1)
                    dve.tensor_tensor(sa[:, j], sa[:, j], sg[:, j], ALU.mult).then_inc(lna_done, 1)
                dve.wait_ge(tanh_done, JB * (l + 1))
                link(dve.tensor_scalar(w_b, rr[:], -1.0, 1.0, ALU.mult, ALU.add))
                link(dve.reciprocal(w_b, w_b))
                for half in range(2):
                    h = slice(4 * half, 4 * half + 4)
                    dve.scalar_tensor_tensor(out=aa[:, h], in0=rr[:, h], scalar=1.0, in1=w_b[:, h],
                                             op0=ALU.add, op1=ALU.mult)
                    ins = dve.scalar_tensor_tensor(out=w_b[:, h], in0=rr[:, h], scalar=-2.0, in1=w_b[:, h],
                                                   op0=ALU.mult, op1=ALU.mult)
                link(ins)
                for half in range(2):
                    h = slice(4 * half, 4 * half + 4)
                    ins = dve.scalar_tensor_tensor(out=rr[:, h], in0=aa[:, h], scalar=1.0, in1=w_b[:, h],
                                                   op0=ALU.add, op1=ALU.mult)
                ins.then_inc(a2_ready, 1)
                for n in range(JB):
                    emptied(dve, l, "rg", JB + n)
                link(dve.tensor_tensor(ig[:], ig[:], cb[:], ALU.mult))
                for n in range(KT):
                    filled(dve, l, "ya", n)
                    emptied(dve, l, "g", 0, n)
                    frees(dve.tensor_tensor(mg[:, n], bank(l, "ya", n)[:, 0:T], gt[:, n % 2], ALU.mult), l, "ya", n)
                    if n == 1:
                        dve.wait_ge(root_ready, l + 1)
                        link(dve.tensor_tensor(ig[:], ig[:], rr[:], ALU.mult))
                        first = slice(SEQ, T, DSEQ)
                        link(dve.tensor_tensor(h0[:], h0[:], aa[:, :, first], ALU.mult))
                        link(dve.tensor_tensor(ig[:, :, first], ig[:, :, first], h0[:], ALU.add))
                        dve.memset(aa[:, :, first], 0.0)
                        link(dve.memset(aa[:, :, 0:1], 0.0))
                        dve.tensor_tensor_scan(cb[:].rearrange("p a b -> p (a b)"), aa[:].rearrange("p a b -> p (a b)"),
                                               ig_flat, 0.0, ALU.mult, ALU.add).then_inc(h_ready, 1)
                        dve.wait_ge(h_ready, l + 1)
                        dve.tensor_tensor(gg[:], gg[:], cb[:], ALU.mult).then_inc(hg_ready, 1)
                for br, yk, q0 in ((2, "yc", KT), (1, "yb", 2 * KT)):
                    for n in range(KT):
                        filled(dve, l, yk, n)
                        emptied(dve, l, "g", br, n)
                        frees(dve.tensor_tensor(sg[:, n % 2], bank(l, yk, n)[:, 0:T], gt[:, (q0 + n) % 2], ALU.mult),
                              l, yk, n)
                        emptied(dve, l, yk, n)
                        ins = dve.tensor_tensor(mg[:, n], mg[:, n], sg[:, n % 2], ALU.add)
                        if br == 1:
                            ins.then_inc(mg_ready, 1)
                        else:
                            ins.then_inc(mg_part, 1)
                    if br == 2:
                        dve.wait_ge(mg_part, KT * (l + 1))
                residual(l, "mix")
                dve.wait_ge(kv_out, 32 * (l + 1))
                dve.wait_ge(h_out, 16 * (l + 1))
                layer_norm(2 * l, x)
                if l % 2 == 0:
                    for f in range(FT):
                        dve.wait_ge(dsig_ready, f + 1)
                        frees(dve.tensor_tensor(dlin[:, f % 2], bank(l, "g", f)[:, 0:T], dsig[:, f % 2], ALU.mult),
                              l, "g", f)
                        emptied(dve, l, "g", f)
                        filled(dve, l, "u", f)
                        frees(dve.tensor_tensor(hT[:, f], bank(l, "u", f)[:, 0:T], dlin[:, f % 2], ALU.mult),
                              l, "u", f)
                    residual(l, "down")
                    layer_norm(2 * l + 1, x)

            for t, (_, r) in enumerate(TOK):
                dve.tensor_scalar(yacc[0:r, t, :], x[0:r, t, :], ALPHA, None, ALU.mult).then_inc(yacc_ready, 1)
            dve.memset(lg[:], 0.0).then_inc(lg_zero, 1)
            dve.memset(slot[:], -1.0).then_inc(lg_zero, 1)
            dve.wait_ge(lg_zero, 2)
            dve.wait_ge(router_in, 32)
            filled(dve, "router")
            for t, (_, r) in enumerate(TOK):
                ins = dve.tensor_tensor(lg[0:r, t, :], bank("router")[0:r, NE * t:NE * t + NE], brow[0:r], ALU.add)
            frees(ins, "router")
            emptied(dve, "router")
            for t in range(3):
                ins = dve.max(top[:, t, :], lg[:, t, :])
            link(ins)
            for t in range(3):
                ins = dve.max_index(topi[:, t, :], top[:, t, :], lg[:, t, :])
            link(ins)
            dve.tensor_copy(topf[:], topi[:, :, 0:2]).then_inc(lg_zero, 1)
            dve.tensor_tensor(gate2[:, :, 0:1], top[:, :, 1:2], top[:, :, 0:1], ALU.subtract).then_inc(top_ready, 1)
            dve.wait_ge(lg_zero, 3)
            lanes = over(iota[:, 0:NE], 3)
            dve.tensor_tensor(m1[:], lanes, topf[:, :, 0:1].to_broadcast([P, 3, NE]), ALU.is_equal)
            link(dve.tensor_tensor(m2[:], lanes, topf[:, :, 1:2].to_broadcast([P, 3, NE]), ALU.is_equal))
            dve.tensor_tensor(hit[:], m1[:], m2[:], ALU.add).then_inc(hit_ready, 1)
            dve.wait_ge(exp_ready, 1)
            link(dve.tensor_scalar(den[:], gate2[:, :, 1], 1.0, None, ALU.add))
            link(dve.reciprocal(gate2[:, :, 0], den[:]))
            link(dve.tensor_tensor(gate2[:, :, 1], gate2[:, :, 1], gate2[:, :, 0], ALU.mult))
            dve.tensor_tensor(m1[:], m1[:], gate2[:, :, 0:1].to_broadcast([P, 3, NE]), ALU.mult)
            link(dve.tensor_tensor(m2[:], m2[:], gate2[:, :, 1:2].to_broadcast([P, 3, NE]), ALU.mult))
            for r in range(2):
                ins = dve.tensor_tensor(gates[:, :, NE * r:NE * r + NE], m1[:], m2[:], ALU.add)
            link(ins)
            filled(dve, "pos")
            for t, (_, r) in enumerate(TOK):
                dve.tensor_scalar(m1[0:r, t, :], bank("pos")[0:r, NE * t:NE * t + NE], 1.0, None, ALU.add)\
                   .then_inc(pos_read, 1)
            frees(dve.reduce_max(nmax[:, 0:1], bank("pos")[:, 3 * NE:4 * NE], AX.X), "pos")
            dve.wait_ge(pos_read, 3)
            emptied(dve, "pos")
            link(dve.tensor_scalar(nmax[:, 1:2], nmax[:, 0:1], float(CAP), float(NE), ALU.is_gt, ALU.mult))
            dve.tensor_scalar(nvi[:], nmax[:, 1:2], float(NE), None, ALU.add).then_inc(nv_ready, 1)
            for t, (_, r) in enumerate(TOK):
                ins = dve.tensor_tensor(m1[0:r, t, :], m1[0:r, t, :], hit[0:r, t, :], ALU.mult)
            link(ins)
            for t, (_, r) in enumerate(TOK):
                dve.tensor_scalar(slot[0:r, t, 0:NE], m1[0:r, t, :], -1.0, None, ALU.add)
                ins = dve.tensor_scalar(slot[0:r, t, NE:2 * NE], m1[0:r, t, :], -1.0 - CAP, None, ALU.add)
            link(ins)
            for t, (_, r) in enumerate(TOK):
                dve.tensor_scalar(pick[0:r, t, :], iota[0:r, :], slot[0:r, t, 0:1], None, ALU.is_equal)\
                   .then_inc(pick_ready, 1)

            dve.wait_ge(nv_ready, 1)
            dve.wait_ge(yacc_ready, 3)
            nv = dve.value_load(nvi[0:1, 0:1], min_val=NE, max_val=2 * NE)
            with dve.Fori(0, nv) as i:
                for f in range(FT // 2):
                    dve.wait_ge(esig_ready, i * (FT // 2) + (f + 1))
                    frees(dve.tensor_tensor(elin[:, f % 2], bank("e", "g", f)[:, 0:2 * CAP], esig[:, f % 2],
                                            ALU.mult), "e", "g", f)
                    emptied(dve, "e", "g", f, i=i)
                    filled(dve, "e", "u", f, i=i)
                    frees(dve.tensor_tensor(he_pair(f), bank("e", "u", f)[:, 0:2 * CAP], elin[:, f % 2],
                                            ALU.mult), "e", "u", f)
                    if f == 0:
                        for t, (_, r) in enumerate(TOK):
                            dve.tensor_scalar(pick[0:r, t, :], iota[0:r, :], slot[0:r, t, bass.ds(i + 1, 1)], None,
                                              ALU.is_equal).then_inc(pick_ready, 1)
                        for t, (_, r) in enumerate(TOK):
                            dve.tensor_scalar(pickg[0:r, t, :], iota[0:r, :], slot[0:r, t, bass.ds(i, 1)],
                                              gates[0:r, t, bass.ds(i, 1)], ALU.is_equal, ALU.mult)\
                               .then_inc(pickg_ready, 1)
                for n in range(12):
                    t, c = n // 4, n % 4
                    r = TOK[t][1]
                    filled(dve, "e", "y", n, i=i)
                    frees(dve.tensor_tensor(yacc[0:r, t, 256 * c:256 * c + 256], bank("e", "y", n)[0:r, 0:256],
                                            yacc[0:r, t, 256 * c:256 * c + 256], ALU.add), "e", "y", n)
                for n in range(4, 12):
                    emptied(dve, "e", "y", n, i=i)
            layer_norm(2 * DEPTH - 1, yacc)

        @block.tensor
        def _(pe):
            def product(out, lhs, rhs, k, n, **kw):
                return pe.matmul(out, lhs, rhs, start=(k == 0), stop=(k == n - 1), **kw)

            def step(ins):
                ins.then_inc(mm_done, 1)

            def blocks(key, src, n, width, kt=KT, unit=None):
                w = (weights(pe, *key) if unit is None else unit).rearrange("p (k n) -> p k n", n=P)
                take(pe, *key)
                for k in range(kt):
                    ins = product(bank(*key)[:, 0:width], w[:, k], src[:, k], k, kt)
                step(ins)

            def rows_of(key, k, nk, src, tiles=6):
                w = weights(pe, *key)
                if k == 0:
                    for n in range(tiles):
                        take(pe, key[0], key[1], n)
                for n in range(tiles):
                    r0, r = TOK[n // 2]
                    c = 512 * (n % 2)
                    ins = product(bank(key[0], key[1], n)[0:r], src[:, r0:r0 + r], w[:, c:c + 512], k, nk)
                step(ins)

            def turn_x(l, name, n):
                pe.wait_ge(x_ready, 3 * n)
                for k in range(KT):
                    take(pe, l, name, k)
                    for t, (r0, r) in enumerate(TOK):
                        ins = pe.transpose(bank(l, name, k)[:, r0:r0 + r], x[0:r, t, P * k:P * k + P],
                                           ident[0:r, 0:r])
                    step(ins)

            pe.wait_ge(const_ready, 3)
            pe.wait_ge(xt_in, 16)
            for l in range(DEPTH):
                if l:
                    for k in range(KT):
                        emptied(pe, l - 1, "xt2", k)
                for n in range(JB):
                    blocks((l, "zb", n), xT, n, T)
                for n in range(2 * JA):
                    blocks((l, "za", n), xT, n, T)
                for n in range(JC):
                    blocks((l, "q", n), xT, n, T)
                pe.wait_ge(mem_in, 16)
                for n in range(H_C):
                    blocks((l, "k", n), mem, n, N_MEM)
                for c in range(4):
                    w = weights(pe, l, "v", c)
                    if c == 0:
                        for m in range(2):
                            take(pe, l, "v", m)
                    for m in range(2):
                        for k in range(2):
                            ins = product(bank(l, "v", m), mem[:, 2 * c + k, P * m:P * m + P],
                                          w[:, 512 * k:512 * k + 512], 2 * c + k, KT)
                    step(ins)
                for n in range(JC):
                    emptied(pe, l, "q", n)
                    emptied(pe, l, "k", n)
                for n in range(8):
                    h, t = n // 2, n % 2
                    take(pe, l, "ps", n)
                    step(pe.matmul(bank(l, "ps", n)[:, 0:N_MEM], qT[:, h, P * t:P * t + P], kT[:, h],
                                   start=True, stop=True))
                for b in range(DEC):
                    w = weights(pe, l, "ck", b)
                    if b % 4 == 0:
                        take(pe, l, "ss", b // 4)
                    for h in range(H_C):
                        ins = product(bank(l, "ss", b // 4)[32 * (b % 4):32 * (b % 4) + 32, 0:N_MEM],
                                      qpad[:, b, 32 * h:32 * h + 32], w[:, N_MEM * h:N_MEM * h + N_MEM], h, H_C)
                    step(ins)
                pe.wait_ge(conv_a_tap, K_A * (l + 1))
                take(pe, l, "mean", 0)
                for j in range(JA):
                    ins = product(bank(l, "mean", 0)[:, 0:T], ones[:], ca[:, j], j, JA)
                step(ins)
                for n in range(JB):
                    blocks((l, "zg", n), xT, n, T)
                pe.wait_ge(dev_ready, l + 1)
                take(pe, l, "var", 0)
                for j in range(JA):
                    ins = product(bank(l, "var", 0)[:, 0:T], ones[:], sg[:, j], j, JA)
                step(ins)
                for n in range(H_C + 1):
                    take(pe, l, "pt", n)
                    pe.wait_ge(probs, 10 * l + 2 * n + 2)
                    for m in range(2):
                        for t in range(2):
                            c = 2 * P * m + P * t
                            ins = pe.transpose(bank(l, "pt", n)[:, c:c + P], pp[:, 2 * n + t, P * m:P * m + P],
                                               ident[:])
                    step(ins)
                for n in range(H_C + 1):
                    emptied(pe, l, "pt", n)
                for m in range(2):
                    emptied(pe, l, "v", m)
                for b in range(DEC):
                    w = weights(pe, l, "cv", b).rearrange("p (m c) -> p m c", m=2)
                    if b == 0:
                        for h in range(H_C):
                            take(pe, l, "o", h)
                            for m in range(2):
                                product(bank(l, "o", h)[:, 0:SEQ], vm[:, m, P * h:P * h + P],
                                        pT[:, h, N_MEM * m:N_MEM * m + SEQ], m, 2)
                    for h in range(H_C):
                        for m in range(2):
                            c = 2 * P * m + 32 * b + DSEQ * h
                            ins = product(bank(l, "o", h)[:, SEQ + DSEQ * b:SEQ + DSEQ * b + DSEQ],
                                          w[:, m, P * h:P * h + P], pT[:, H_C, c:c + DSEQ], m, 2)
                    step(ins)
                pe.wait_ge(conv_b_done, 4 * (l + 1))
                for n in range(2 * JB):
                    if n % JB == 0:
                        w = weights(pe, l, "rg", n // JB)
                    take(pe, l, "rg", n)
                    j = n % JB
                    step(pe.matmul(bank(l, "rg", n)[:, 0:T], w[:, P * j:P * j + P], cb[:, j], start=True, stop=True))
                for br, yk, src in ((0, "ya", sa), (2, "yc", oT)):
                    for n in range(0, KT, 2):
                        blocks((l, "g", br, n), xT, n, T)
                        blocks((l, "g", br, n + 1), xT, n, T)
                        if n == 0 and br == 0:
                            pe.wait_ge(lna_done, JA * (l + 1))
                        if n == 0 and br == 2:
                            for h in range(H_C):
                                emptied(pe, l, "o", h)
                        w = weights(pe, l, yk, n // 2)
                        for m in range(2):
                            blocks((l, yk, n + m), src, n, T, kt=4, unit=w[:, 512 * m:512 * m + 512])
                for n in range(KT):
                    blocks((l, "g", 1, n), xT, n, T)
                    if n == 0:
                        pe.wait_ge(hg_ready, l + 1)
                    blocks((l, "yb", n), gg, n, T)
                for k in range(KT):
                    pe.wait_ge(mg_ready, KT * l + k + 1)
                    rows_of((l, "mix", k), k, KT, mg[:, k])
                turn_x(l, "xt", 2 * l + 1)
                for k in range(KT):
                    emptied(pe, l, "xt", k)
                if l % 2 == 0:
                    for f in range(0, FT, 2):
                        for w in "gu":
                            for n in (f, f + 1):
                                blocks((l, w, n), xT, n, T)
                    for f in range(FT):
                        emptied(pe, l, "u", f)
                        rows_of((l, "down", f), f, FT, hT[:, f])
                    turn_x(l, "xt2", 2 * l + 2)
            pe.wait_ge(router_in, 32)
            take(pe, "router")
            for t, (r0, r) in enumerate(TOK):
                for k in range(KT):
                    ins = product(bank("router")[0:r, NE * t:NE * t + NE], xT[:, k, r0:r0 + r], wr[:, k], k, KT)
            step(ins)
            take(pe, "pos")
            pe.wait_ge(hit_ready, 1)
            for t, (r0, r) in enumerate(TOK):
                for s in range(t + 1):
                    rs = TOK[s][1]
                    product(bank("pos")[0:r, NE * t:NE * t + NE], (upper if s == t else ones)[0:rs, 0:r],
                            hit[0:rs, s], s, t + 1)
            for s in range(3):
                rs = TOK[s][1]
                ins = product(bank("pos")[:, 3 * NE:4 * NE], ones[0:rs, :], hit[0:rs, s], s, 3)
            step(ins)

            def gather(key, i=None):
                for n in range(4):
                    take(pe, *key, n, i=i)
                    for m in range(2):
                        k = 2 * n + m
                        for t, (_, r) in enumerate(TOK):
                            ins = product(bank(*key, n)[:, CAP * m:CAP * m + CAP], x[0:r, t, P * k:P * k + P],
                                          pick[0:r, t, :], t, 3)
                    step(ins)

            pe.wait_ge(pick_ready, 3)
            gather(("gather0",))
            for n in range(4):
                emptied(pe, "gather0", n)
            pe.wait_ge(nv_ready, 1)
            nv = pe.value_load(nvi[0:1, 0:1], min_val=NE, max_val=2 * NE)
            with pe.Fori(0, nv) as i:
                for f in range(0, FT, 2):
                    for w in "gu":
                        take(pe, "e", w, f // 2, i=i)
                        for n in (f, f + 1):
                            u = weights(pe, "e", w, n, i=i).rearrange("p (k n) -> p k n", n=P)
                            for k in range(KT):
                                ins = product(bank("e", w, f // 2)[:, CAP * (n - f):CAP * (n - f) + CAP],
                                              u[:, k], xe[:, k], k, KT)
                            step(ins)
                pe.wait_ge(pick_ready, i * 3 + 6)
                gather(("e", "gather"), i=i)
                for f in range(FT):
                    u = weights(pe, "e", "down", f, i=i)
                    if f == 0:
                        for n in range(4):
                            take(pe, "e", "down", n, i=i)
                    if f % 2 == 0:
                        emptied(pe, "e", "u", f // 2, i=i)
                    for n in range(KT):
                        ins = pe.matmul(bank("e", "down", n // 2)[:, CAP * (n % 2):CAP * (n % 2) + CAP],
                                        u[:, P * n:P * n + P], he[:, f], start=(f == 0 and n % 2 == 0),
                                        stop=(f == FT - 1), skip_group_check=True)
                    step(ins)
                pe.wait_ge(pickg_ready, i * 3 + 3)
                for n in range(2):
                    c, w = (0, P) if n == 0 else (P, CAP - P)
                    take(pe, "e", "pt", n, i=i)
                    for t, (r0, r) in enumerate(TOK):
                        ins = pe.transpose(bank("e", "pt", n)[0:w, r0:r0 + r], pickg[0:r, t, c:c + w],
                                           ident[0:r, 0:r])
                    step(ins)
                for n in range(4):
                    c, w = (0, P) if n < 2 else (P, CAP - P)
                    take(pe, "e", "yt", n, i=i)
                    for m in range(4):
                        k = 4 * (n % 2) + m
                        if n < 2 and m % 2 == 0:
                            emptied(pe, "e", "down", k // 2, i=i)
                        ins = pe.transpose(bank("e", "yt", n)[0:w, P * m:P * m + P], ye[:, k, c:c + w], ident[:])
                    step(ins)
                for n in range(2):
                    emptied(pe, "e", "pt", n, i=i)
                for n in range(4):
                    emptied(pe, "e", "yt", n, i=i)
                for n in range(12):
                    t, c = n // 4, 256 * (n % 4)
                    r0, r = TOK[t]
                    take(pe, "e", "y", n, i=i)
                    pe.matmul(bank("e", "y", n)[0:r, 0:256], pg0[:, r0:r0 + r], y0[:, c:c + 256],
                              start=True, stop=False)
                    step(pe.matmul(bank("e", "y", n)[0:r, 0:256], pg1[0:CAP - P, r0:r0 + r],
                                   y1[0:CAP - P, c:c + 256], start=False, stop=True))
                for n in range(4):
                    emptied(pe, "e", "gather", n, i=i)

    return nc


def _blocks(w):
    k, n = w.shape
    return w.reshape(k // P, P, n // P, P).transpose(2, 1, 0, 3).reshape(n // P, P, k)


def _halves(w):
    return w.reshape(4, P, 4, 2, P).transpose(2, 1, 3, 0, 4).reshape(4, P, UNIT)


def _ffn(gate, up, down):
    import numpy as np

    g, u = (_blocks(a).reshape(FT // 2, 2, P, UNIT) for a in (gate, up))
    return np.concatenate([np.concatenate([g, u], 1).reshape(2 * FT, P, UNIT), down.reshape(FT, P, UNIT)])


def _mix_units(a, l):
    import numpy as np

    win = _blocks(a["w_in"][l])
    za = np.stack([win[ZA_U:ZA_U + JA], win[ZA_G:ZA_G + JA]], 1).reshape(2 * JA, P, UNIT)
    kv = a["w_mem_kv"][l]
    v = kv[:, D_C:].reshape(4, 2, P, D_C).transpose(0, 2, 1, 3).reshape(4, P, UNIT)
    ck = a["cache_mem_k"][l].transpose(0, 3, 2, 1).reshape(DEC, P, UNIT)
    cv = a["cache_mem_v"][l].reshape(DEC, 2, P, D_C).transpose(0, 2, 1, 3).reshape(DEC, P, UNIT)
    rg = [a[n][l].transpose(1, 0, 2).reshape(1, P, UNIT) for n in ("w_rg_a", "w_rg_x")]
    parts = [win[ZB:ZB + JB], za, win[ZQ:ZQ + JC], _blocks(kv[:, :D_C]), v, ck, win[ZG:ZG + JB], cv, *rg]
    for br, name in ((0, "w_a_out"), (2, "w_c_out")):
        g = win[ZM + KT * br:ZM + KT * br + KT].reshape(4, 2, P, UNIT)
        parts.append(np.concatenate([g, _halves(a[name][l])[:, None]], 1).reshape(12, P, UNIT))
    parts.append(np.stack([win[ZM + KT:ZM + 2 * KT], _blocks(a["w_b_out"][l])], 1).reshape(2 * KT, P, UNIT))
    parts.append(a["w_mix_out"][l].reshape(KT, P, UNIT))
    return np.concatenate(parts)


def _channels(v):
    import numpy as np

    v = np.moveaxis(v, -1, 1)
    return v.reshape(DEPTH, v.shape[1] // P, P, -1).transpose(0, 2, 1, 3).reshape(DEPTH, P, -1)


def kernel(**inputs):
    import numpy as np
    import concourse.bacc as bacc
    from concourse.bass_utils import run_bass_kernel_spmd as run

    a = {k: np.asarray(v) for k, v in inputs.items()}
    x0 = np.concatenate([a["x_prompt"].reshape(SEQ, D), a["x_sample"].reshape(NSAMP, D)])
    feature = lambda v: np.ascontiguousarray(v.T.reshape(KT, P, -1).transpose(1, 0, 2))
    experts = np.concatenate([_ffn(a["w_e_gate"][0, e], a["w_e_up"][0, e], a["w_e_down"][0, e]) for e in range(NE)])
    arrays = {
        "x0": x0,
        "x0T": feature(x0),
        "memT": feature(a["mem_prompt"][0]),
        "chan": np.concatenate([_channels(a[n]) for n in COL if n != "lam"] + [_channels(a["lru_lambda"])], 2),
        "rows": np.stack([a["ln1_g"], a["ln1_b"], a["ln2_g"], a["ln2_b"]], 1),
        "hist": np.concatenate([_channels(a["state_conv_a"]), _channels(a["state_conv_b"]),
                                _channels(a["state_rglru"])], 2),
        "stream": np.concatenate([_mix_units(a, 0), _ffn(a["w_ff_gate"][0], a["w_ff_up"][0], a["w_ff_down"][0]),
                                  _mix_units(a, 1)]),
        "router_w": np.ascontiguousarray(a["w_router"][0].reshape(KT, P, NE).transpose(1, 0, 2)),
        "router_b": a["b_router"][0],
        "experts": np.concatenate([experts, experts[:SLOTS]]),
    }
    outs = {"y": (T, D), "o_a": (DEPTH, P, JA * 9 * (K_A - 1)), "o_b": (DEPTH, P, JB * 9 * (K_B - 1)),
            "o_h": (DEPTH, P, JB * 9), "o_k": (DEPTH, P, H_C, N_MEM), "o_v": (DEPTH, P, 2, D_C)}
    nc = bacc.Bacc("TRN2", target_bir_lowering=False, num_devices=1)
    args = [nc.dram_tensor(n, v.shape, F32, kind="ExternalInput").ap() for n, v in arrays.items()]
    args += [nc.dram_tensor(n, s, F32, kind="ExternalOutput").ap() for n, s in outs.items()]
    trunk(nc, *args)
    r = run(nc, [arrays], core_ids=[0]).results[0]
    ca = r["o_a"].reshape(DEPTH, P, JA, 9, K_A - 1).transpose(0, 3, 4, 2, 1).reshape(DEPTH, 9, K_A - 1, D_A)
    cb = r["o_b"].reshape(DEPTH, P, JB, 9, K_B - 1).transpose(0, 3, 4, 2, 1).reshape(DEPTH, 9, K_B - 1, D_B)
    h = r["o_h"].reshape(DEPTH, P, JB, 9).transpose(0, 3, 2, 1).reshape(DEPTH, 9, D_B)
    mk = r["o_k"].transpose(0, 3, 2, 1).reshape(DEPTH, 1, N_MEM, H_C, P)
    mv = r["o_v"].transpose(0, 2, 1, 3).reshape(DEPTH, 1, N_MEM, H_C, P)
    y = r["y"]
    return (y[:SEQ].reshape(1, SEQ, D), y[SEQ:].reshape(DEC, DSEQ, D), ca[:, :1], cb[:, :1], h[:, :1], mk, mv,
            ca[:, 1:], cb[:, 1:], h[:, 1:])
```

```python
from contextlib import ExitStack

import concourse.bass as bass
from concourse import mybir

F32 = mybir.dt.float32
F32R = mybir.dt.float32r
I32 = mybir.dt.int32
U32 = mybir.dt.uint32
ALU = mybir.AluOpType
ACT = mybir.ActivationFunctionType
AX = mybir.AxisListType

P = 128
DEPTH = 2
D = 1024
KT = D // P
SEQ, DEC, DSEQ = 256, 8, 8
NSAMP = DEC * DSEQ
T = SEQ + NSAMP
TOK = [0, 128, T - 128]
DUP = 64
N_MEM = 256
D_A, K_A = 512, 31
D_B, K_B = 1024, 4
D_C, H_C = 512, 4
JA, JB, JC = D_A // P, D_B // P, D_C // P
D_IN = 2 * D_A + 2 * D_B + D_C + 3 * D
D_FF = 2816
FT = D_FF // P
NE = 8
CAP = T // 2
SMALL = 96
ALPHA = (2.0 * DEPTH) ** 0.25
EPS = 1e-5
QSCALE = float(P) ** -0.5

LN_STEPS = len(TOK)
HIST = 1 + JB + 2 + JA
SLOTS = 6
E_SLOTS = 11
SPLITS = 3
AHEAD = 2
UNIT = 1024
SBUF_FIRST, SBUF_END = 16512, 229344
BANKS = 8
Y_TILES = [(t, c, 256) for t in range(3) for c in range(0, D, 256)]
SEG_A = K_A - 1 + DSEQ
SEG_B = K_B - 1 + DSEQ
LEN_A = K_A - 1 + SEQ + DEC * SEG_A
LEN_B = K_B - 1 + SEQ + DEC * SEG_B

_c = 0
COL = {}
for _name, _n in (("b_in", D_IN // P), ("w_conv_a", JA * K_A), ("b_conv_a", JA), ("ln_a_g", JA), ("ln_a_b", JA),
                  ("w_conv_b", JB * K_B), ("b_conv_b", JB), ("b_rg_a", JB), ("b_rg_x", JB), ("lam", JB)):
    COL[_name] = _c
    _c += _n
NCOL = _c
ZA_U, ZA_G, ZB, ZG, ZQ, ZM = 0, JA, 2 * JA, 2 * JA + JB, 2 * JA + 2 * JB, 2 * JA + 2 * JB + JC


class Tile:

    def __init__(self, bank, use):
        self.bank, self.use, self.done = bank, use, None


class Plan:

    def __init__(self):
        self.steps = 0
        self.tiles = {}
        self.unit_done = []
        self.unit_of = {}
        self.split = {}

    def tile(self, *key):
        n = len(self.tiles)
        self.tiles[key] = Tile(n % BANKS, n // BANKS)

    def step(self, closes=(), unit=None, split=False):
        self.steps += 1
        for key in closes:
            if key not in self.tiles:
                self.tile(*key)
            self.tiles[key].done = self.steps
        if unit is not None:
            self.unit_of[unit] = len(self.unit_done)
            if split:
                self.split[len(self.unit_done)] = len(self.split)
            self.unit_done.append(self.steps)


def make_plan():
    p = Plan()
    for l in range(DEPTH):
        for n in range(JB):
            p.step([(l, "zb", n)], (l, "zb", n))
        for n in range(2 * JA):
            p.step([(l, "za", n)], (l, "za", n))
        for n in range(JC):
            p.step([(l, "q", n)], (l, "q", n))
        for n in range(H_C):
            p.step([(l, "k", n)], (l, "k", n))
        for m in range(2):
            p.tile(l, "v", m)
        for c in range(4):
            p.step([(l, "v", m) for m in range(2)] if c == 3 else [], (l, "v", c))
        for n in range(8):
            p.step([(l, "ps", n)])
        for b in range(DEC):
            if b % 4 == 0:
                p.tile(l, "ss", b // 4)
            p.step([(l, "ss", b // 4)] if b % 4 == 3 else [], (l, "ck", b))
        p.step([(l, "mean", 0)])
        for n in range(JB):
            p.step([(l, "zg", n)], (l, "zg", n))
        p.step([(l, "var", 0)])
        for n in range(H_C + 1):
            p.step([(l, "pt", n)])
        for h in range(H_C):
            p.tile(l, "o", h)
        for b in range(DEC):
            p.step([(l, "o", h) for h in range(H_C)] if b == DEC - 1 else [], (l, "cv", b))
        for n in range(2 * JB):
            p.step([(l, "rg", n)], (l, "rg", n // JB) if n % JB == JB - 1 else None)
        for br, y in ((0, "ya"), (2, "yc")):
            for n in range(0, KT, 2):
                p.step([(l, "g", br, n)], (l, "g", br, n))
                p.step([(l, "g", br, n + 1)], (l, "g", br, n + 1))
                p.step([(l, y, n)])
                p.step([(l, y, n + 1)], (l, y, n // 2))
        for n in range(KT):
            p.step([(l, "g", 1, n)], (l, "g", 1, n))
            p.step([(l, "yb", n)], (l, "yb", n))
        for n in range(6):
            p.tile(l, "mix", n)
        for k in range(KT):
            p.step([(l, "mix", n) for n in range(6)] if k == KT - 1 else [], (l, "mix", k))
        for k in range(KT):
            p.step([(l, "xt", k)])
        if l % 2 == 0:
            for f in range(0, FT, 2):
                for w in "gu":
                    for n in (f, f + 1):
                        p.step([(l, w, n)], (l, w, n), split=True)
            for n in range(6):
                p.tile(l, "down", n)
            for f in range(FT):
                p.step([(l, "down", n) for n in range(6)] if f == FT - 1 else [], (l, "down", f), split=True)
            for k in range(KT):
                p.step([(l, "xt2", k)])
    p.step([("router",)])
    p.step([("pos",)])
    for n in range(4):
        p.step([("gather0", n)])
    first, first_unit, first_tile = p.steps, len(p.unit_done), len(p.tiles)
    for f in range(0, FT, 2):
        for w in "gu":
            p.tile("e", w, f // 2)
            for n in (f, f + 1):
                p.step([("e", w, f // 2)] if n == f + 1 else [], ("e", w, n))
        if f == 0:
            for n in range(2):
                p.step([("e", "pt", n)])
    for n in range(4):
        p.step([("e", "gather", n)])
    for n in range(4):
        p.tile("e", "down", n)
    for f in range(FT):
        p.step([("e", "down", n) for n in range(4)] if f == FT - 1 else [], ("e", "down", f))
    for n in range(4):
        p.step([("e", "yt", n)])
    for n in range(len(Y_TILES)):
        p.step([("e", "y", n)])
    p.per_steps = p.steps - first
    p.per_units = len(p.unit_done) - first_unit
    p.loop_unit = first_unit
    per_tiles = len(p.tiles) - first_tile
    assert per_tiles % BANKS == 0 and p.per_units % E_SLOTS == 0
    p.per_use = per_tiles // BANKS
    p.per_slot = p.per_units // E_SLOTS
    return p


def trunk(nc, x0, x0T, memT, chan, rows, hist, stream, router_w, router_b, experts,
          y, o_a, o_b, o_h, o_k, o_v):
    plan = make_plan()
    n_units = plan.loop_unit
    assert stream.shape[0] == n_units

    with ExitStack() as ctx:
        sbuf_at = [SBUF_FIRST]

        def place(name, shape, at, dt=F32):
            return nc.alloc_sbuf_tensor_at(name, shape, dt, offset=at)

        def sb(name, shape, dt=F32):
            n = 4
            for d in shape[1:]:
                n *= d
            at = sbuf_at[0]
            sbuf_at[0] += (n + 31) // 32 * 32
            assert sbuf_at[0] <= SBUF_END, name
            return place(name, shape, at, dt)

        def sem(name):
            return ctx.enter_context(nc.semaphore(name))

        psum = ctx.enter_context(nc.psum_tensor("psum", [P, BANKS, 512], F32))
        ring_at = sbuf_at[0]
        ring = sb("ring", [P, SLOTS + 2 * SPLITS, UNIT])
        wh = place("wh", [P, SPLITS, UNIT], ring_at + 4 * UNIT * SLOTS, F32R)
        wl = place("wl", [P, SPLITS, UNIT], ring_at + 4 * UNIT * (SLOTS + SPLITS), F32R)
        x = sb("x", [P, 3, D])
        xT = sb("xT", [P, KT, T])
        mem = sb("mem", [P, KT, N_MEM])
        lnp = sb("lnp", [P, 2, D])
        par = sb("par", [P, DEPTH, NCOL])
        ident = sb("ident", [P, P])
        ones = sb("ones", [P, P])
        upper = sb("upper", [P, P])
        iota = sb("iota", [P, CAP])
        small = sb("small", [P, 256])
        tails = sb("tails", [P, 288])
        stat = sb("stat", [P, 50])
        spl = sb("spl", [P, DEPTH * JB])
        nvi = sb("nvi", [P, 1], I32)
        big = sb("big", [P, 2 * NE], I32)

        ARENA = 28248
        arena_at = sbuf_at[0]
        arena = sb("arena", [P, ARENA])
        off = [0]

        def cut(n, a=None):
            at = off[0]
            off[0] += n
            assert off[0] <= ARENA
            v = arena[:, at:at + n]
            return v.rearrange("p (a b) -> p a b", a=a) if a else v

        def cut_r(name, n, a):
            v = place(name, [P, a, n // a], arena_at + 4 * off[0], F32R)
            off[0] += n
            assert off[0] <= ARENA
            return v

        ig_flat = arena[:, 0:JB * T]
        ua = arena[:, 0:JA * LEN_A].rearrange("p (a b) -> p a b", a=JA)
        ig = cut(JB * T, JB)
        w_flat = arena[:, off[0]:off[0] + JB * T]
        w_b = w_flat.rearrange("p (a b) -> p a b", a=JB)
        zb = cut(JB * LEN_B, JB)
        sg = cut(JA * T, JA)
        ca = cut(JA * T, JA)
        cb = cut(JB * T, JB)
        qT = cut(JC * T, JC)
        qpad = cut(DEC * P, DEC)
        kT = cut(H_C * N_MEM, H_C)
        vm = cut(2 * D_C, 2)
        pp = arena[:, off[0]:off[0] + 2560].rearrange("p (a b) -> p a b", a=10)
        mg = cut(KT * T, KT)
        pT = arena[:, off[0]:off[0] + 2560].rearrange("p (a b) -> p a b", a=5)
        aa = cut(JB * T, JB)
        oT = cut(JC * T, JC)
        rr = cut(JB * T, JB)
        gg_flat = arena[:, off[0]:off[0] + JB * T]
        gg = cut(JB * T, JB)
        sa_flat = arena[:, off[0]:off[0] + JA * T]
        sa = cut(JA * T, JA)
        gt = cut(2 * T, 2)
        hist_a = gg_flat[:, 0:JA * DEC * (K_A - 1)].rearrange("p (a b c) -> p a b c", a=JA, b=DEC)
        tail_a = sa_flat[:, 0:JA * 9 * (K_A - 1)].rearrange("p (a b c) -> p a b c", a=JA, b=9)
        hist_b = small[:, 0:192].rearrange("p (a b c) -> p a b c", a=JB, b=DEC)
        h0 = small[:, 192:256].rearrange("p (a b) -> p a b", a=JB)
        tail_b = tails[:, 0:216].rearrange("p (a b c) -> p a b c", a=JB, b=9)
        tail_h = tails[:, 216:288].rearrange("p (a b) -> p a b", a=JB)
        off[0] = 0
        hTh, hTl = cut_r("hTh", FT * T, FT), cut_r("hTl", FT * T, FT)
        xTh, xTl = cut_r("xTh", KT * T, KT), cut_r("xTl", KT * T, KT)
        dsig = cut(2 * T, 2)
        dlin = cut(2 * T, 2)
        dh = cut(2 * T, 2)
        off[0] = 0
        yacc = cut(3 * D, 3)
        xe = cut(KT * CAP, KT)
        he = cut(FT * CAP, FT)
        ye = cut(KT * CAP, KT)
        ys = cut(2 * D, 2)
        pg = cut(2 * T, 2)
        pick = cut(3 * CAP, 3)
        esig = cut(4 * CAP, 4)
        elin = cut(4 * CAP, 4)
        wr = cut(KT * NE, KT)
        brow = cut(NE)
        lg = cut(3 * NE, 3)
        top = cut(3 * 8, 3)
        topf = cut(3 * 2, 3)
        gate2 = cut(3 * 2, 3)
        den = cut(3)
        m1 = cut(3 * NE, 3)
        m2 = cut(3 * NE, 3)
        hit = cut(3 * NE, 3)
        gates = cut(3 * (2 * NE), 3)
        slot = cut(3 * (2 * NE + 1), 3)
        count = cut(NE)
        nmax = cut(2)
        eps_c = sb("eps_c", [P, 1])
        stats = sb("stats", [P, 3, 2, 6])
        mv = sb("mv", [P, 3, 4])
        lamw = sb("lamw", [P, 6, DEPTH, JB])
        topi = sb("topi", [P, 3, 8], U32)

        slot_full = [sem(f"slot_full{s}") for s in range(E_SLOTS)]
        mm_done = sem("mm_done")
        evac = [sem(f"evac{b}") for b in range(BANKS)]
        x_in, xt_in, mem_in, par_in = sem("x_in"), sem("xt_in"), sem("mem_in"), sem("par_in")
        ln_in = sem("ln_in")
        hi_done, lo_done = sem("hi_done"), sem("lo_done")
        xth_ready = sem("xth_ready")
        dhh_ready, dhl_ready = sem("dhh_ready"), sem("dhl_ready")
        hist_in, hist_small_in = sem("hist_in"), sem("hist_small_in")
        router_in = sem("router_in")
        kv_out, tail_a_out, tail_b_out, h_out, y_out = (sem("kv_out"), sem("tail_a_out"), sem("tail_b_out"),
                                                        sem("h_out"), sem("y_out"))
        const_step, const_ready = sem("const_step"), sem("const_ready")
        pool_step = sem("pool_step")
        hist_ready = sem("hist_ready")
        tails_ready = sem("tails_ready")
        htail_ready = sem("htail_ready")
        dve_step = sem("dve_step")
        spl_exp, spl_ready = sem("spl_exp"), sem("spl_ready")
        spl_ask = sem("spl_ask")
        eps_ready, bn_done, sa_lin, mg_part = sem("eps_ready"), sem("bn_done"), sem("sa_lin"), sem("mg_part")
        yacc_ready, lg_zero, pos_read = sem("yacc_ready"), sem("lg_zero"), sem("pos_read")
        glu_done = sem("glu_done")
        conv_b_done = sem("conv_b_done")
        conv_a_tap = sem("conv_a_tap")
        negmax = sem("negmax")
        probs = sem("probs")
        dev_ready, sq_ready = sem("dev_ready"), sem("sq_ready")
        lna_norm, lna_sig, lna_done = sem("lna_norm"), sem("lna_sig"), sem("lna_done")
        tanh_done = sem("tanh_done")
        a2_ready, root_ready = sem("a2_ready"), sem("root_ready")
        h_ready, hg_ready = sem("h_ready"), sem("hg_ready")
        var_ready, std_ready, x_ready = sem("var_ready"), sem("std_ready"), sem("x_ready")
        top_ready, exp_ready = sem("top_ready"), sem("exp_ready")
        hit_ready, nv_ready, pick_ready = sem("hit_ready"), sem("nv_ready"), sem("pick_ready")
        mg_ready = sem("mg_ready")
        dsig_ready, esig_ready = sem("dsig_ready"), sem("esig_ready")

        def tile_of(*key):
            return plan.tiles[key]

        def bank(*key):
            return psum[:, plan.tiles[key].bank, :]

        def turn_slot(k):
            k %= E_SLOTS
            return (n_units + k) % SLOTS if k < SLOTS else k

        stream_loads = [len(range(s, n_units, SLOTS)) if s < SLOTS else 0 for s in range(E_SLOTS)]

        def filled(eng, *key, i=None):
            v = plan.tiles[key].done
            eng.wait_ge(mm_done, v if i is None else i * plan.per_steps + v)

        def emptied_before(eng, *key, i):
            t = plan.tiles[key]
            eng.wait_ge(evac[t.bank], i * plan.per_use + (t.use + 1 - plan.per_use))

        def emptied(eng, *key, i=None):
            t = plan.tiles[key]
            eng.wait_ge(evac[t.bank], t.use + 1 if i is None else i * plan.per_use + (t.use + 1))

        def frees(ins, *key):
            ins.then_inc(evac[plan.tiles[key].bank], 1)

        def take(eng, *key, i=None):
            t = plan.tiles[key]
            if i is not None:
                eng.wait_ge(evac[t.bank], i * plan.per_use + t.use)
            elif t.use:
                eng.wait_ge(evac[t.bank], t.use)

        def weights(eng, *key, i=None):
            u = plan.unit_of[key]
            if i is None:
                slot_wait(eng, u)
                return ring[:, u % SLOTS, :]
            k = u - plan.loop_unit
            s = turn_slot(k)
            eng.wait_ge(slot_full[s], i * (16 * plan.per_slot) + 16 * (stream_loads[s] + k // E_SLOTS + 1))
            return ring[:, s, :]

        def slot_wait(eng, u):
            eng.wait_ge(slot_full[u % SLOTS], 16 * (u // SLOTS + 1))

        def parts(eng, *key):
            q = plan.split[plan.unit_of[key]]
            eng.wait_ge(lo_done, q + 1)
            return wh[:, q % SPLITS, :], wl[:, q % SPLITS, :]

        split_steps = [plan.unit_done[u] for u in plan.split]

        def make_hi(act, u):
            q = plan.split[u]
            slot_wait(act, u)
            if q >= SPLITS:
                act.wait_ge(mm_done, split_steps[q - SPLITS])
            act.copy(wh[:, q % SPLITS, :], ring[:, u % SLOTS, :]).then_inc(hi_done, 1)

        def make_lo(pool, u):
            q = plan.split[u]
            pool.wait_ge(hi_done, q + 1)
            pool.tensor_tensor(wl[:, q % SPLITS, :], ring[:, u % SLOTS, :], wh[:, q % SPLITS, :].bitcast(F32),
                               ALU.subtract).then_inc(lo_done, 1)

        def units_by(step):
            return sum(done <= step for done in plan.unit_done)

        def samp(v):
            return v.rearrange("p (b t) -> p b t", b=DEC)

        def seg_a(j, k, n):
            return ua[:, j, K_A - 1 + SEQ:LEN_A].rearrange("p (b s) -> p b s", b=DEC)[:, :, k:k + n]

        def seg_b(j, k, n):
            return zb[:, j, K_B - 1 + SEQ:LEN_B].rearrange("p (b s) -> p b s", b=DEC)[:, :, k:k + n]

        def col(l, name, n=0, w=1):
            c = COL[name] + n
            return par[:, l, c:c + w]

        def pair(v, n, cap=CAP):
            return v[:, 2 * n:2 * n + 2, 0:cap]

        def bank_pair(*key, cap=CAP):
            return bank(*key)[:, 0:2 * CAP].rearrange("p (a b) -> p a b", a=2)[:, :, 0:cap]

        def yt_place(n, cap):
            if cap <= P:
                return cap, 0, 256 * n, 256
            return (P if n < 2 else cap - P), n // 2, 512 * (n % 2), 512

        def pt_place(n, cap):
            if cap <= P:
                return cap, 0, P * n, (P if n == 0 else T - P)
            return (P if n == 0 else cap - P), n, 0, T

        def turns(eng, turn):
            eng.wait_ge(nv_ready, 1)
            nv = eng.value_load(nvi[0:1, 0:1], min_val=NE, max_val=2 * NE)
            with eng.Fori(0, nv) as i:
                large = eng.value_load(big[0:1, bass.ds(i, 1)], min_val=0, max_val=1)
                with eng.If(large > 0):
                    turn(i, CAP)
                with eng.Else():
                    turn(i, SMALL)
            return nv

        def layer_norm_std(act, n):
            act.wait_ge(eps_ready, 1)
            for t in range(3):
                act.wait_ge(var_ready, 3 * n + t + 1)
                act.activation(mv[:, t, 2:3], mv[:, t, 1:2], ACT.Sqrt, bias=eps_c[:, 0:1])\
                   .then_inc(std_ready, 1)

        block = ctx.enter_context(nc.Block())

        @block.sync
        def _(sp):
            for u in range(n_units):
                if u - SLOTS in plan.split:
                    sp.wait_ge(lo_done, plan.split[u - SLOTS] + 1)
                elif u >= SLOTS:
                    sp.wait_ge(mm_done, plan.unit_done[u - SLOTS])
                sp.dma_start(ring[:, u % SLOTS, :], stream[u]).then_inc(slot_full[u % SLOTS], 16)
            for k in range(E_SLOTS):
                if k < SLOTS:
                    sp.wait_ge(mm_done, plan.unit_done[n_units + k - SLOTS])
                elif k == SLOTS:
                    sp.wait_ge(mm_done, split_steps[-1])
                sp.dma_start(ring[:, turn_slot(k), :], experts[k]).then_inc(slot_full[turn_slot(k)], 16)

            def expert(i, e):
                for k in range(plan.per_units):
                    sp.wait_ge(mm_done, i * plan.per_steps + plan.unit_done[plan.loop_unit + k])
                    sp.dma_start(ring[:, turn_slot(k), :], experts[e * plan.per_units + (E_SLOTS + k)])\
                        .then_inc(slot_full[turn_slot(k)], 16)

            with sp.Fori(0, NE) as i:
                expert(i, i)
            sp.wait_ge(nv_ready, 1)
            nv = sp.value_load(nvi[0:1, 0:1], min_val=NE, max_val=2 * NE)
            with sp.If(nv > NE):
                with sp.Fori(NE, 2 * NE) as i:
                    expert(i, i - NE)

        @block.gpsimd
        def _(pool):
            pool.dma_start(xT[:], x0T).then_inc(xt_in, 16)
            pool.dma_start(par[:], chan.rearrange("l p c -> p l c")).then_inc(par_in, 16)
            pool.dma_start(mem[:], memT).then_inc(mem_in, 16)
            pool.memset(ones[:], 1.0).then_inc(const_step, 1)
            pool.memset(ident[:], 0.0).then_inc(const_step, 1)
            pool.iota(iota[:], pattern=[[1, CAP]], base=0, channel_multiplier=0,
                      allow_small_or_imprecise_dtypes=True).then_inc(const_ready, 1)
            pool.wait_ge(const_step, 2)
            pool.affine_select(out=ident[:], in_=ident[:], compare_op=ALU.not_equal, fill=1.0, base=0,
                               pattern=[[-1, P]], channel_multiplier=1).then_inc(const_ready, 1)
            pool.affine_select(out=upper[:], in_=ones[:], compare_op=ALU.is_gt, fill=0.0, base=0,
                               pattern=[[1, P]], channel_multiplier=-1).then_inc(const_ready, 1)
            for l in range(DEPTH):
                if l:
                    pool.wait_ge(x_ready, LN_STEPS * 2 * l)
                pool.dma_start(lnp[:], rows[l, 0:2].partition_broadcast(P)).then_inc(ln_in, 16)
                pool.dma_start(small[:], hist[l, :, JA * DEC * (K_A - 1):]).then_inc(hist_small_in, 16)
                pool.dma_start(gg_flat[:, 0:JA * DEC * (K_A - 1)], hist[l, :, 0:JA * DEC * (K_A - 1)])\
                    .then_inc(hist_in, 16)
                if l == 0:
                    for t, r0 in enumerate(TOK):
                        pool.dma_start(x[:, t, :], x0[r0:r0 + P]).then_inc(x_in, 16)
                pool.memset(zb[:, :, 0:K_B - 1], 0.0).then_inc(hist_ready, 1)
                pool.wait_ge(hist_small_in, 16 * (l + 1))
                for j in range(JB):
                    pool.tensor_copy(seg_b(j, 0, K_B - 1), hist_b[:, j]).then_inc(hist_ready, 1)
                pool.memset(ua[:, :, 0:K_A - 1], 0.0).then_inc(hist_ready, 1)
                pool.memset(qpad[:], 0.0).then_inc(hist_ready, 1)
                pool.wait_ge(hist_in, 16 * (l + 1))
                for j in range(JA):
                    pool.tensor_copy(seg_a(j, 0, K_A - 1), hist_a[:, j]).then_inc(hist_ready, 1)
                for j in range(JB):
                    emptied(pool, l, "zb", j)
                pool.wait_ge(hist_ready, (l + 1) * HIST)
                if l:
                    pool.wait_ge(tail_b_out, 16 * l)
                    pool.wait_ge(h_out, 16 * l)
                for j in range(JB):
                    pool.tensor_copy(tail_b[:, j, 0, :], zb[:, j, SEQ:SEQ + K_B - 1]).then_inc(tails_ready, 1)
                    pool.tensor_copy(tail_b[:, j, 1:9, :], seg_b(j, DSEQ, K_B - 1)).then_inc(tails_ready, 1)
                pool.wait_ge(glu_done, 2 * JA * (l + 1))
                for j in range(JA):
                    pool.tensor_copy(tail_a[:, j, 0, :], ua[:, j, SEQ:SEQ + K_A - 1]).then_inc(tails_ready, 1)
                    pool.tensor_copy(tail_a[:, j, 1:9, :], seg_a(j, DSEQ, K_A - 1)).then_inc(tails_ready, 1)
                pool.wait_ge(tails_ready, 2 * (JA + JB) * (l + 1))
                pool.dma_start(o_b[l], tails[:, 0:216]).then_inc(tail_b_out, 16)
                pool.dma_start(o_a[l], sa_flat[:, 0:JA * 9 * (K_A - 1)]).then_inc(tail_a_out, 16)
                for n in range(H_C):
                    emptied(pool, l, "k", n)
                for n in range(2):
                    emptied(pool, l, "v", n)
                pool.dma_start(o_k[l], kT[:]).then_inc(kv_out, 16)
                pool.dma_start(o_v[l], vm[:]).then_inc(kv_out, 16)
                pool.wait_ge(h_ready, l + 1)
                pool.tensor_copy(tail_h[:, :, 0:1], cb[:, :, SEQ - 1:SEQ]).then_inc(htail_ready, 1)
                pool.tensor_copy(tail_h[:, :, 1:9], cb[:, :, SEQ + DSEQ - 1:T:DSEQ]).then_inc(htail_ready, 1)
                pool.wait_ge(htail_ready, 2 * (l + 1))
                pool.dma_start(o_h[l], tails[:, 216:288]).then_inc(h_out, 16)
                def next_rows():
                    pool.wait_ge(x_ready, LN_STEPS * (2 * l + 1))
                    pool.dma_start(lnp[:], rows[l, 2:4].partition_broadcast(P)).then_inc(ln_in, 16)
                if l % 2 == 0:
                    for n, u in enumerate(plan.split):
                        if u < n_units:
                            make_lo(pool, u)
                            if n == 8:
                                next_rows()
                else:
                    next_rows()
            pool.wait_ge(kv_out, 32 * DEPTH)
            pool.wait_ge(tail_a_out, 16 * DEPTH)
            pool.dma_start(wr[:], router_w).then_inc(router_in, 16)
            pool.dma_start(brow, router_b.partition_broadcast(P)).then_inc(router_in, 16)
            pool.wait_ge(x_ready, LN_STEPS * 2 * DEPTH)
            for t, r in ((0, 0), (1, 0), (2, DUP)):
                pool.dma_start(y[TOK[t] + r:TOK[t] + P], yacc[r:P, t, :]).then_inc(y_out, 16)
            pool.wait_ge(y_out, 48)
            pool.wait_ge(h_out, 16 * DEPTH)
            pool.wait_ge(kv_out, 32 * DEPTH)
            pool.wait_ge(tail_a_out, 16 * DEPTH)
            pool.wait_ge(tail_b_out, 16 * DEPTH)
            nv = pool.value_load(nvi[0:1, 0:1], min_val=NE, max_val=2 * NE)
            for s in range(E_SLOTS):
                pool.wait_ge(slot_full[s], nv * (16 * plan.per_slot) + 16 * (stream_loads[s] + 1))

        @block.scalar
        def _(act):
            def ident_bias(out, in_, bias):
                return act.activation(out, in_, ACT.Identity, bias=bias)

            queue = list(plan.split)

            def split_for(step):
                while queue and queue[0] < units_by(step) + AHEAD:
                    make_hi(act, queue.pop(0))

            act.wait_ge(spl_ask, 1)
            act.activation(lamw[:, 1], lamw[:, 0], ACT.Exp).then_inc(spl_exp, 1)
            for l in range(DEPTH):
                for n in range(JB):
                    filled(act, l, "zb", n)
                    b = col(l, "b_in", ZB + n)
                    ident_bias(zb[:, n, K_B - 1:K_B - 1 + SEQ], bank(l, "zb", n)[:, 0:SEQ], b)
                    frees(ident_bias(seg_b(n, K_B - 1, DSEQ), samp(bank(l, "zb", n)[:, SEQ:T]), b), l, "zb", n)
                for n in range(JA):
                    filled(act, l, "za", 2 * n + 1)
                    frees(act.activation(sg[:, n], bank(l, "za", 2 * n + 1)[:, 0:T], ACT.Sigmoid,
                                         bias=col(l, "b_in", ZA_G + n)), l, "za", 2 * n + 1)
                act.wait_ge(hist_ready, HIST * l + 1 + JB + 2)
                for n in range(JC):
                    filled(act, l, "q", n)
                    b = col(l, "b_in", ZQ + n)
                    ident_bias(qpad[:, :, 40 * n:40 * n + DSEQ], samp(bank(l, "q", n)[:, SEQ:T]), b)
                    frees(ident_bias(qT[:, n], bank(l, "q", n)[:, 0:T], b), l, "q", n)
                for n in range(H_C):
                    filled(act, l, "k", n)
                    frees(act.copy(kT[:, n], bank(l, "k", n)[:, 0:N_MEM]), l, "k", n)
                for n in range(2):
                    filled(act, l, "v", n)
                    frees(act.copy(vm[:, n], bank(l, "v", n)), l, "v", n)
                for n in range(10):
                    key = (l, "ps", n) if n < 8 else (l, "ss", n - 8)
                    act.wait_ge(negmax, 10 * l + n + 1)
                    frees(act.activation(pp[:, n], bank(*key)[:, 0:N_MEM], ACT.Exp, bias=stat[:, 20 + n:21 + n],
                                         scale=QSCALE, accum_out=stat[:, 30 + n:31 + n]), *key)
                act.wait_ge(hist_ready, HIST * (l + 1))
                for n in range(JB):
                    filled(act, l, "zg", n)
                    frees(act.activation(gg[:, n], bank(l, "zg", n)[:, 0:T], ACT.Gelu_apprx_tanh,
                                         bias=col(l, "b_in", ZG + n)), l, "zg", n)
                filled(act, l, "var", 0)
                frees(act.activation(gt[:, 0], bank(l, "var", 0)[:, 0:T], ACT.Sqrt, scale=1.0 / D_A,
                                     bias=eps_c[:, 0:1]), l, "var", 0)
                for n in range(H_C + 1):
                    filled(act, l, "pt", n)
                    frees(act.copy(pT[:, n], bank(l, "pt", n)), l, "pt", n)
                act.wait_ge(lna_norm, l + 1)
                for n in range(JA):
                    act.activation(sg[:, n], ca[:, n], ACT.Sigmoid, scale=col(l, "ln_a_g", n),
                                   bias=col(l, "ln_a_b", n)).then_inc(lna_sig, 1)
                for n in range(H_C):
                    filled(act, l, "o", n)
                    frees(act.copy(oT[:, n], bank(l, "o", n)[:, 0:T]), l, "o", n)
                act.wait_ge(spl_ready, 1)
                for n in range(JB):
                    filled(act, l, "rg", n)
                    frees(act.activation(rr[:, n], bank(l, "rg", n)[:, 0:T], ACT.Sigmoid,
                                         bias=col(l, "b_rg_a", n)), l, "rg", n)
                for n in range(JB):
                    emptied(act, l, "rg", n)
                    act.activation(rr[:, n], rr[:, n], ACT.Tanh,
                                   scale=spl[:, JB * l + n:JB * l + n + 1]).then_inc(tanh_done, 1)
                act.wait_ge(conv_a_tap, K_A * (l + 1))
                act.wait_ge(tails_ready, 2 * (JA + JB) * (l + 1))
                for n in range(JB):
                    filled(act, l, "rg", JB + n)
                    frees(act.activation(ig[:, n], bank(l, "rg", JB + n)[:, 0:T], ACT.Sigmoid,
                                         bias=col(l, "b_rg_x", n)), l, "rg", JB + n)
                q = 0
                before = []
                for br, yk in ((0, "ya"), (2, "yc"), (1, "yb")):
                    for n in range(KT):
                        if br == 0 and n == 2:
                            act.wait_ge(a2_ready, l + 1)
                            act.activation(rr[:], rr[:], ACT.Sqrt).then_inc(root_ready, 1)
                        filled(act, l, "g", br, n)
                        if q >= 2:
                            emptied(act, *before[q - 2])
                        frees(act.activation(gt[:, q % 2], bank(l, "g", br, n)[:, 0:T], ACT.Sigmoid,
                                             bias=col(l, "b_in", ZM + KT * br + n)), l, "g", br, n)
                        before.append((l, yk, n))
                        q += 1
                layer_norm_std(act, 2 * l)
                if l % 2 == 0:
                    split_for(tile_of(l, "xt", 0).done)
                    for k in range(KT):
                        filled(act, l, "xt", k)
                        act.copy(xTh[:, k], bank(l, "xt", k)[:, 0:T]).then_inc(xth_ready, 1)
                    for f in range(FT):
                        split_for(tile_of(l, "g", f).done)
                        filled(act, l, "g", f)
                        if f >= 2:
                            emptied(act, l, "g", f - 2)
                        act.activation(dsig[:, f % 2], bank(l, "g", f)[:, 0:T], ACT.Sigmoid).then_inc(dsig_ready, 1)
                        if f:
                            split_for(tile_of(l, "u", f - 1).done)
                            emptied(act, l, "u", f - 1)
                            act.copy(hTh[:, f - 1], dh[:, (f - 1) % 2]).then_inc(dhh_ready, 1)
                    split_for(tile_of(l, "u", FT - 1).done)
                    emptied(act, l, "u", FT - 1)
                    act.copy(hTh[:, FT - 1], dh[:, (FT - 1) % 2]).then_inc(dhh_ready, 1)
                    split_for(tile_of(l, "down", 0).done)
                    layer_norm_std(act, 2 * l + 1)
                    for k in range(KT):
                        filled(act, l, "xt2", k)
                        frees(act.copy(xT[:, k], bank(l, "xt2", k)[:, 0:T]), l, "xt2", k)
                else:
                    for k in range(KT):
                        filled(act, l, "xt", k)
                        frees(act.copy(xT[:, k], bank(l, "xt", k)[:, 0:T]), l, "xt", k)
            act.wait_ge(top_ready, 1)
            act.activation(gate2[:, :, 1], gate2[:, :, 0], ACT.Exp).then_inc(exp_ready, 1)
            for n in range(4):
                filled(act, "gather0", n)
                frees(act.copy(pair(xe, n), bank_pair("gather0", n)), "gather0", n)

            def turn(i, cap):
                for f in range(FT // 2):
                    filled(act, "e", "g", f, i=i)
                    if f >= 2:
                        emptied(act, "e", "g", f - 2, i=i)
                    act.activation(pair(esig, f % 2, cap), bank_pair("e", "g", f, cap=cap), ACT.Sigmoid)\
                        .then_inc(esig_ready, 1)
                for n in range(4):
                    filled(act, "e", "gather", n, i=i)
                    frees(act.copy(pair(xe, n), bank_pair("e", "gather", n)), "e", "gather", n)
                for n in range(4):
                    filled(act, "e", "down", n, i=i)
                    frees(act.copy(pair(ye, n, cap), bank_pair("e", "down", n, cap=cap)), "e", "down", n)
                for n in range(4):
                    filled(act, "e", "yt", n, i=i)
                    r, g, c, w = yt_place(n, cap)
                    frees(act.copy(ys[0:r, g, c:c + w], bank("e", "yt", n)[0:r, 0:w]), "e", "yt", n)

            turns(act, turn)
            layer_norm_std(act, 2 * DEPTH - 1)

        @block.vector
        def _(dve):
            steps = [0]

            def link(ins):
                steps[0] += 1
                ins.then_inc(dve_step, 1)
                dve.wait_ge(dve_step, steps[0])

            def mac(out, in0, scalar, in1):
                return dve.scalar_tensor_tensor(out=out, in0=in0, scalar=scalar, in1=in1, op0=ALU.mult, op1=ALU.add)

            def over(v, n):
                return v.unsqueeze(1).to_broadcast([P, n, v.shape[-1]])

            def layer_norm(n, v):
                dve.wait_ge(ln_in, 16 * (n + 1))
                for t in range(3):
                    for c in range(2):
                        dve.bn_stats(stats[:, t, c], v[:, t, 512 * c:512 * c + 512]).then_inc(bn_done, 1)
                dve.wait_ge(bn_done, 6 * (n + 1))
                for t in range(3):
                    dve.bn_aggr(mv[:, t, 0:2], stats[:, t]).then_inc(var_ready, 1)
                for t in range(3):
                    dve.wait_ge(std_ready, 3 * n + t + 1)
                    link(dve.reciprocal(mv[:, t, 2:3], mv[:, t, 2:3]))
                    link(dve.tensor_scalar(v[:, t, :], v[:, t, :], mv[:, t, 0:1], mv[:, t, 2:3],
                                           ALU.subtract, ALU.mult))
                    link(dve.tensor_tensor(v[:, t, :], v[:, t, :], lnp[:, 0, :], ALU.mult))
                    dve.tensor_tensor(v[:, t, :], v[:, t, :], lnp[:, 1, :], ALU.add).then_inc(x_ready, 1)
                dve.wait_ge(x_ready, 3 * (n + 1))

            def hidden_lo(f):
                dve.wait_ge(dhh_ready, f + 1)
                dve.tensor_tensor(hTl[:, f], dh[:, f % 2], hTh[:, f].bitcast(F32), ALU.subtract)\
                   .then_inc(dhl_ready, 1)

            def residual(l, name):
                for n in range(6):
                    t, c = n // 2, 512 * (n % 2)
                    filled(dve, l, name, n)
                    frees(dve.scalar_tensor_tensor(out=x[:, t, c:c + 512], in0=x[:, t, c:c + 512], scalar=ALPHA,
                                                   in1=bank(l, name, n), op0=ALU.mult, op1=ALU.add), l, name, n)
                for n in range(6):
                    emptied(dve, l, name, n)

            dve.memset(eps_c[:], EPS).then_inc(eps_ready, 1)
            dve.wait_ge(par_in, 16)
            lam = par[:, :, COL["lam"]:COL["lam"] + JB]
            link(dve.tensor_scalar(lamw[:, 2], lam, -1.0, None, ALU.mult))
            dve.tensor_tensor(lamw[:, 0], lam, lamw[:, 2], ALU.min).then_inc(spl_ask, 1)
            dve.wait_ge(spl_exp, 1)
            link(dve.tensor_scalar(lamw[:, 0], lamw[:, 1], 2.0, None, ALU.add))
            link(dve.reciprocal(lamw[:, 0], lamw[:, 0]))
            link(dve.tensor_tensor(lamw[:, 0], lamw[:, 0], lamw[:, 1], ALU.mult))
            link(dve.tensor_tensor(lamw[:, 3], lamw[:, 0], lamw[:, 0], ALU.mult))
            link(dve.tensor_scalar(lamw[:, 4], lamw[:, 3], 1.0 / 17, 1.0 / 15, ALU.mult, ALU.add))
            for k in (13, 11, 9, 7, 5, 3, 1):
                link(dve.tensor_tensor(lamw[:, 4], lamw[:, 4], lamw[:, 3], ALU.mult))
                link(dve.tensor_scalar(lamw[:, 4], lamw[:, 4], 1.0 / k, None, ALU.add))
            link(dve.tensor_tensor(lamw[:, 4], lamw[:, 4], lamw[:, 0], ALU.mult))
            link(dve.tensor_scalar(lamw[:, 4], lamw[:, 4], 2.0, None, ALU.mult))
            link(dve.tensor_scalar(lamw[:, 2], lamw[:, 2], 0.0, None, ALU.max))
            link(dve.tensor_tensor(lamw[:, 4], lamw[:, 4], lamw[:, 2], ALU.add))
            dve.tensor_scalar(spl[:].rearrange("p (l j) -> p l j", l=DEPTH), lamw[:, 4], -4.0, None, ALU.mult)\
               .then_inc(spl_ready, 1)

            for l in range(DEPTH):
                dve.wait_ge(hist_ready, HIST * l + 1 + JB)
                for j0 in range(0, JB, 2):
                    for j in (j0, j0 + 1):
                        emptied(dve, l, "zb", j)
                    for k in range(K_B):
                        for j in (j0, j0 + 1):
                            w = col(l, "w_conv_b", K_B * j + k)
                            for out, in_ in ((cb[:, j, 0:SEQ], zb[:, j, k:k + SEQ]),
                                             (samp(cb[:, j, SEQ:T]), seg_b(j, k, DSEQ))):
                                if k == 0:
                                    ins = dve.tensor_scalar(out, in_, w, col(l, "b_conv_b", j), ALU.mult, ALU.add)
                                else:
                                    ins = mac(out, in_, w, out)
                        if k < K_B - 1:
                            link(ins)
                        else:
                            ins.then_inc(conv_b_done, 1)
                dve.wait_ge(hist_ready, HIST * (l + 1))
                for j in range(JA):
                    filled(dve, l, "za", 2 * j)
                    emptied(dve, l, "za", 2 * j + 1)
                    b = col(l, "b_in", ZA_U + j)
                    z = bank(l, "za", 2 * j)
                    dve.scalar_tensor_tensor(out=ua[:, j, K_A - 1:K_A - 1 + SEQ], in0=z[:, 0:SEQ], scalar=b,
                                             in1=sg[:, j, 0:SEQ], op0=ALU.add, op1=ALU.mult).then_inc(glu_done, 1)
                    dve.wait_ge(glu_done, 2 * (JA * l + j) + 1)
                    dve.scalar_tensor_tensor(out=seg_a(j, K_A - 1, DSEQ), in0=samp(z[:, SEQ:T]), scalar=b,
                                             in1=samp(sg[:, j, SEQ:T]), op0=ALU.add, op1=ALU.mult)\
                       .then_inc(glu_done, 1)
                    dve.wait_ge(glu_done, 2 * (JA * l + j + 1))
                    frees(dve.tensor_scalar(ca[:, j, 0:SEQ], ua[:, j, 0:SEQ], col(l, "w_conv_a", K_A * j),
                                            col(l, "b_conv_a", j), ALU.mult, ALU.add), l, "za", 2 * j)
                    ins = dve.tensor_scalar(samp(ca[:, j, SEQ:T]), seg_a(j, 0, DSEQ), col(l, "w_conv_a", K_A * j),
                                            col(l, "b_conv_a", j), ALU.mult, ALU.add)
                ins.then_inc(conv_a_tap, 1)
                for k in range(1, K_A):
                    dve.wait_ge(conv_a_tap, K_A * l + k)
                    for j in range(JA):
                        w = col(l, "w_conv_a", K_A * j + k)
                        mac(ca[:, j, 0:SEQ], ua[:, j, k:k + SEQ], w, ca[:, j, 0:SEQ])
                        ins = mac(samp(ca[:, j, SEQ:T]), seg_a(j, k, DSEQ), w, samp(ca[:, j, SEQ:T]))
                    ins.then_inc(conv_a_tap, 1)
                for n in range(10):
                    key = (l, "ps", n) if n < 8 else (l, "ss", n - 8)
                    filled(dve, *key)
                    link(dve.reduce_max(stat[:, 10 + n:11 + n], bank(*key)[:, 0:N_MEM], AX.X))
                    dve.tensor_scalar(stat[:, 20 + n:21 + n], stat[:, 10 + n:11 + n], -QSCALE, None, ALU.mult)\
                       .then_inc(negmax, 1)
                filled(dve, l, "mean", 0)
                frees(mac(ca[:], over(bank(l, "mean", 0)[:, 0:T], JA), -1.0 / D_A, ca[:]), l, "mean", 0)
                emptied(dve, l, "mean", 0)
                dve.tensor_tensor(sg[:], ca[:], ca[:], ALU.mult).then_inc(dev_ready, 1)
                for n in range(10):
                    emptied(dve, *((l, "ps", n) if n < 8 else (l, "ss", n - 8)))
                link(dve.reciprocal(stat[:, 40:50], stat[:, 30:40]))
                for n in range(10):
                    dve.tensor_scalar(pp[:, n], pp[:, n], stat[:, 40 + n:41 + n], None, ALU.mult).then_inc(probs, 1)
                emptied(dve, l, "var", 0)
                link(dve.reciprocal(gt[:, 0], gt[:, 0]))
                dve.tensor_tensor(ca[:], ca[:], over(gt[:, 0], JA), ALU.mult).then_inc(lna_norm, 1)
                dve.wait_ge(lna_norm, l + 1)
                dve.wait_ge(tail_a_out, 16 * (l + 1))
                for j in range(JA):
                    dve.tensor_scalar(sa[:, j], ca[:, j], col(l, "ln_a_g", j), col(l, "ln_a_b", j),
                                      ALU.mult, ALU.add).then_inc(sa_lin, 1)
                for j in range(JA):
                    dve.wait_ge(sa_lin, JA * l + j + 1)
                    dve.wait_ge(lna_sig, JA * l + j + 1)
                    dve.tensor_tensor(sa[:, j], sa[:, j], sg[:, j], ALU.mult).then_inc(lna_done, 1)
                dve.wait_ge(tanh_done, JB * (l + 1))
                link(dve.tensor_scalar(w_b, rr[:], -1.0, 1.0, ALU.mult, ALU.add))
                link(dve.reciprocal(w_b, w_b))
                for half in range(2):
                    h = slice(4 * half, 4 * half + 4)
                    dve.scalar_tensor_tensor(out=aa[:, h], in0=rr[:, h], scalar=1.0, in1=w_b[:, h],
                                             op0=ALU.add, op1=ALU.mult)
                    ins = dve.scalar_tensor_tensor(out=w_b[:, h], in0=rr[:, h], scalar=-2.0, in1=w_b[:, h],
                                                   op0=ALU.mult, op1=ALU.mult)
                link(ins)
                for half in range(2):
                    h = slice(4 * half, 4 * half + 4)
                    ins = dve.scalar_tensor_tensor(out=rr[:, h], in0=aa[:, h], scalar=1.0, in1=w_b[:, h],
                                                   op0=ALU.add, op1=ALU.mult)
                ins.then_inc(a2_ready, 1)
                for n in range(JB):
                    emptied(dve, l, "rg", JB + n)
                link(dve.tensor_tensor(ig[:], ig[:], cb[:], ALU.mult))
                for n in range(KT):
                    filled(dve, l, "ya", n)
                    emptied(dve, l, "g", 0, n)
                    frees(dve.tensor_tensor(mg[:, n], bank(l, "ya", n)[:, 0:T], gt[:, n % 2], ALU.mult), l, "ya", n)
                    if n == 1:
                        dve.wait_ge(root_ready, l + 1)
                        link(dve.tensor_tensor(ig[:], ig[:], rr[:], ALU.mult))
                        first = slice(SEQ, T, DSEQ)
                        link(dve.tensor_tensor(h0[:], h0[:], aa[:, :, first], ALU.mult))
                        link(dve.tensor_tensor(ig[:, :, first], ig[:, :, first], h0[:], ALU.add))
                        dve.memset(aa[:, :, first], 0.0)
                        link(dve.memset(aa[:, :, 0:1], 0.0))
                        dve.tensor_tensor_scan(cb[:].rearrange("p a b -> p (a b)"), aa[:].rearrange("p a b -> p (a b)"),
                                               ig_flat, 0.0, ALU.mult, ALU.add).then_inc(h_ready, 1)
                        dve.wait_ge(h_ready, l + 1)
                        dve.tensor_tensor(gg[:], gg[:], cb[:], ALU.mult).then_inc(hg_ready, 1)
                for br, yk, q0 in ((2, "yc", KT), (1, "yb", 2 * KT)):
                    for n in range(KT):
                        filled(dve, l, yk, n)
                        emptied(dve, l, "g", br, n)
                        frees(dve.tensor_tensor(sg[:, n % 2], bank(l, yk, n)[:, 0:T], gt[:, (q0 + n) % 2], ALU.mult),
                              l, yk, n)
                        emptied(dve, l, yk, n)
                        ins = dve.tensor_tensor(mg[:, n], mg[:, n], sg[:, n % 2], ALU.add)
                        if br == 1:
                            ins.then_inc(mg_ready, 1)
                        else:
                            ins.then_inc(mg_part, 1)
                    if br == 2:
                        dve.wait_ge(mg_part, KT * (l + 1))
                residual(l, "mix")
                dve.wait_ge(kv_out, 32 * (l + 1))
                dve.wait_ge(h_out, 16 * (l + 1))
                layer_norm(2 * l, x)
                if l % 2 == 0:
                    for k in range(KT):
                        dve.wait_ge(xth_ready, k + 1)
                        frees(dve.tensor_tensor(xTl[:, k], bank(l, "xt", k)[:, 0:T], xTh[:, k].bitcast(F32),
                                                ALU.subtract), l, "xt", k)
                    for f in range(FT):
                        dve.wait_ge(dsig_ready, f + 1)
                        frees(dve.tensor_tensor(dlin[:, f % 2], bank(l, "g", f)[:, 0:T], dsig[:, f % 2], ALU.mult),
                              l, "g", f)
                        emptied(dve, l, "g", f)
                        filled(dve, l, "u", f)
                        if f >= 2:
                            dve.wait_ge(dhl_ready, f - 1)
                        frees(dve.tensor_tensor(dh[:, f % 2], bank(l, "u", f)[:, 0:T], dlin[:, f % 2], ALU.mult),
                              l, "u", f)
                        emptied(dve, l, "u", f)
                        if f:
                            hidden_lo(f - 1)
                    hidden_lo(FT - 1)
                    residual(l, "down")
                    layer_norm(2 * l + 1, x)

            for t in range(3):
                dve.tensor_scalar(yacc[:, t, :], x[:, t, :], ALPHA, None, ALU.mult).then_inc(yacc_ready, 1)
            dve.memset(slot[:], -1.0).then_inc(lg_zero, 1)
            dve.wait_ge(lg_zero, 1)
            dve.wait_ge(router_in, 32)
            filled(dve, "router")
            for t in range(3):
                ins = dve.tensor_tensor(lg[:, t, :], bank("router")[:, NE * t:NE * t + NE], brow, ALU.add)
            frees(ins, "router")
            emptied(dve, "router")
            for t in range(3):
                ins = dve.max(top[:, t, :], lg[:, t, :])
            link(ins)
            for t in range(3):
                ins = dve.max_index(topi[:, t, :], top[:, t, :], lg[:, t, :])
            link(ins)
            dve.tensor_copy(topf[:], topi[:, :, 0:2]).then_inc(lg_zero, 1)
            dve.tensor_tensor(gate2[:, :, 0:1], top[:, :, 1:2], top[:, :, 0:1], ALU.subtract).then_inc(top_ready, 1)
            dve.wait_ge(lg_zero, 2)
            lanes = over(iota[:, 0:NE], 3)
            dve.tensor_tensor(m1[:], lanes, topf[:, :, 0:1].to_broadcast([P, 3, NE]), ALU.is_equal)
            link(dve.tensor_tensor(m2[:], lanes, topf[:, :, 1:2].to_broadcast([P, 3, NE]), ALU.is_equal))
            link(dve.tensor_tensor(hit[:], m1[:], m2[:], ALU.add))
            dve.memset(hit[0:DUP, 2, :], 0.0).then_inc(hit_ready, 1)
            dve.wait_ge(exp_ready, 1)
            link(dve.tensor_scalar(den[:], gate2[:, :, 1], 1.0, None, ALU.add))
            link(dve.reciprocal(gate2[:, :, 0], den[:]))
            link(dve.tensor_tensor(gate2[:, :, 1], gate2[:, :, 1], gate2[:, :, 0], ALU.mult))
            dve.tensor_tensor(m1[:], m1[:], gate2[:, :, 0:1].to_broadcast([P, 3, NE]), ALU.mult)
            link(dve.tensor_tensor(m2[:], m2[:], gate2[:, :, 1:2].to_broadcast([P, 3, NE]), ALU.mult))
            for r in range(2):
                ins = dve.tensor_tensor(gates[:, :, NE * r:NE * r + NE], m1[:], m2[:], ALU.add)
            link(ins)
            filled(dve, "pos")
            for t in range(3):
                dve.tensor_scalar(m1[:, t, :], bank("pos")[:, NE * t:NE * t + NE], 1.0, None, ALU.add)\
                   .then_inc(pos_read, 1)
            link(dve.tensor_copy(count[:], bank("pos")[:, 3 * NE:4 * NE]))
            frees(dve.reduce_max(nmax[:, 0:1], bank("pos")[:, 3 * NE:4 * NE], AX.X), "pos")
            dve.wait_ge(pos_read, 3)
            emptied(dve, "pos")
            dve.wait_ge(hit_ready, 1)
            for r in range(2):
                link(dve.tensor_scalar(big[:, NE * r:NE * r + NE], count[:], float(SMALL + CAP * r), None,
                                       ALU.is_gt))
            link(dve.tensor_scalar(nmax[:, 1:2], nmax[:, 0:1], float(CAP), float(NE), ALU.is_gt, ALU.mult))
            dve.tensor_scalar(nvi[:], nmax[:, 1:2], float(NE), None, ALU.add).then_inc(nv_ready, 1)
            for t in range(3):
                ins = dve.tensor_tensor(m1[:, t, :], m1[:, t, :], hit[:, t, :], ALU.mult)
            link(ins)
            for t in range(3):
                dve.tensor_scalar(slot[:, t, 0:NE], m1[:, t, :], -1.0, None, ALU.add)
                ins = dve.tensor_scalar(slot[:, t, NE:2 * NE], m1[:, t, :], -1.0 - CAP, None, ALU.add)
            link(ins)
            for t in range(3):
                dve.tensor_scalar(pick[:, t, :], iota[:, :], slot[:, t, 0:1], None, ALU.is_equal)\
                   .then_inc(pick_ready, 1)

            dve.wait_ge(yacc_ready, 3)

            def turn(i, cap):
                for f in range(FT // 2):
                    dve.wait_ge(esig_ready, i * (FT // 2) + (f + 1))
                    frees(dve.tensor_tensor(pair(elin, f % 2, cap), bank_pair("e", "g", f, cap=cap),
                                            pair(esig, f % 2, cap), ALU.mult), "e", "g", f)
                    emptied(dve, "e", "g", f, i=i)
                    filled(dve, "e", "u", f, i=i)
                    frees(dve.tensor_tensor(pair(he, f, cap), bank_pair("e", "u", f, cap=cap),
                                            pair(elin, f % 2, cap), ALU.mult), "e", "u", f)
                    if f == 0:
                        for n in range(2):
                            filled(dve, "e", "pt", n, i=i)
                            r, g, c, w = pt_place(n, cap)
                            frees(dve.tensor_copy(pg[0:r, g, c:c + w], bank("e", "pt", n)[0:r, c:c + w]),
                                  "e", "pt", n)
                        for t in range(3):
                            dve.tensor_scalar(pick[:, t, :], iota[:], slot[:, t, bass.ds(i + 1, 1)], None,
                                              ALU.is_equal).then_inc(pick_ready, 1)
                for n in range(len(Y_TILES) - BANKS, len(Y_TILES)):
                    emptied_before(dve, "e", "y", n, i=i)
                for n, (t, c, w) in enumerate(Y_TILES):
                    filled(dve, "e", "y", n, i=i)
                    frees(dve.scalar_tensor_tensor(out=yacc[:, t, c:c + w], in0=bank("e", "y", n)[:, 0:w],
                                                   scalar=gates[:, t, bass.ds(i, 1)], in1=yacc[:, t, c:c + w],
                                                   op0=ALU.mult, op1=ALU.add), "e", "y", n)

            nv = turns(dve, turn)
            for n in range(len(Y_TILES) - BANKS, len(Y_TILES)):
                emptied_before(dve, "e", "y", n, i=nv)
            layer_norm(2 * DEPTH - 1, yacc)

        @block.tensor
        def _(pe):
            def product(out, lhs, rhs, k, n, **kw):
                return pe.matmul(out, lhs, rhs, start=(k == 0), stop=(k == n - 1), **kw)

            def step(ins):
                ins.then_inc(mm_done, 1)

            def blocks(key, src, n, width, kt=KT, unit=None):
                w = (weights(pe, *key) if unit is None else unit).rearrange("p (k n) -> p k n", n=P)
                take(pe, *key)
                for k in range(kt):
                    ins = product(bank(*key)[:, 0:width], w[:, k], src[:, k], k, kt)
                step(ins)

            def rows_of(key, k, nk, src, tiles=6):
                w = weights(pe, *key)
                if k == 0:
                    for n in range(tiles):
                        take(pe, key[0], key[1], n)
                for n in range(tiles):
                    r0, c = TOK[n // 2], 512 * (n % 2)
                    ins = product(bank(key[0], key[1], n), src[:, r0:r0 + P], w[:, c:c + 512], k, nk)
                step(ins)

            def blocks3(key, hi, lo, n, width):
                h, low = (v.rearrange("p (k n) -> p k n", n=P) for v in parts(pe, *key))
                take(pe, *key)
                for k in range(KT):
                    out = bank(*key)[:, 0:width]
                    pe.matmul(out, h[:, k], hi[:, k], start=(k == 0), stop=False)
                    pe.matmul(out, h[:, k], lo[:, k], start=False, stop=False)
                    ins = pe.matmul(out, low[:, k], hi[:, k], start=False, stop=(k == KT - 1))
                step(ins)

            def rows_of3(key, k, nk, hi, lo, tiles=6):
                h, low = parts(pe, *key)
                if k == 0:
                    for n in range(tiles):
                        take(pe, key[0], key[1], n)
                for t, r0 in enumerate(TOK):
                    for c in range(2):
                        out, cs = bank(key[0], key[1], 2 * t + c), slice(512 * c, 512 * c + 512)
                        pe.matmul(out, hi[:, r0:r0 + P], h[:, cs], start=(k == 0), stop=False)
                        pe.matmul(out, hi[:, r0:r0 + P], low[:, cs], start=False, stop=False)
                        ins = pe.matmul(out, lo[:, r0:r0 + P], h[:, cs], start=False, stop=(k == nk - 1))
                step(ins)

            def turn_x(l, name, n):
                pe.wait_ge(x_ready, 3 * n)
                for k in range(KT):
                    take(pe, l, name, k)
                    for t in (2, 0, 1):
                        ins = pe.transpose(bank(l, name, k)[:, TOK[t]:TOK[t] + P], x[:, t, P * k:P * k + P],
                                           ident[:])
                    step(ins)

            pe.wait_ge(const_ready, 3)
            pe.wait_ge(xt_in, 16)
            for l in range(DEPTH):
                if l:
                    for k in range(KT):
                        emptied(pe, l - 1, "xt2", k)
                for n in range(JB):
                    blocks((l, "zb", n), xT, n, T)
                for n in range(2 * JA):
                    blocks((l, "za", n), xT, n, T)
                for n in range(JC):
                    blocks((l, "q", n), xT, n, T)
                pe.wait_ge(mem_in, 16)
                for n in range(H_C):
                    blocks((l, "k", n), mem, n, N_MEM)
                for c in range(4):
                    w = weights(pe, l, "v", c)
                    if c == 0:
                        for m in range(2):
                            take(pe, l, "v", m)
                    for m in range(2):
                        for k in range(2):
                            ins = product(bank(l, "v", m), mem[:, 2 * c + k, P * m:P * m + P],
                                          w[:, 512 * k:512 * k + 512], 2 * c + k, KT)
                    step(ins)
                for n in range(JC):
                    emptied(pe, l, "q", n)
                    emptied(pe, l, "k", n)
                for n in range(8):
                    h, t = n // 2, n % 2
                    take(pe, l, "ps", n)
                    step(pe.matmul(bank(l, "ps", n)[:, 0:N_MEM], qT[:, h, P * t:P * t + P], kT[:, h],
                                   start=True, stop=True))
                for b in range(DEC):
                    w = weights(pe, l, "ck", b)
                    if b % 4 == 0:
                        take(pe, l, "ss", b // 4)
                    for h in range(H_C):
                        ins = product(bank(l, "ss", b // 4)[32 * (b % 4):32 * (b % 4) + 32, 0:N_MEM],
                                      qpad[:, b, 32 * h:32 * h + 32], w[:, N_MEM * h:N_MEM * h + N_MEM], h, H_C)
                    step(ins)
                pe.wait_ge(conv_a_tap, K_A * (l + 1))
                take(pe, l, "mean", 0)
                for j in range(JA):
                    ins = product(bank(l, "mean", 0)[:, 0:T], ones[:], ca[:, j], j, JA)
                step(ins)
                for n in range(JB):
                    blocks((l, "zg", n), xT, n, T)
                pe.wait_ge(dev_ready, l + 1)
                take(pe, l, "var", 0)
                for j in range(JA):
                    ins = product(bank(l, "var", 0)[:, 0:T], ones[:], sg[:, j], j, JA)
                step(ins)
                for n in range(H_C + 1):
                    take(pe, l, "pt", n)
                    pe.wait_ge(probs, 10 * l + 2 * n + 2)
                    for m in range(2):
                        for t in range(2):
                            c = 2 * P * m + P * t
                            ins = pe.transpose(bank(l, "pt", n)[:, c:c + P], pp[:, 2 * n + t, P * m:P * m + P],
                                               ident[:])
                    step(ins)
                for n in range(H_C + 1):
                    emptied(pe, l, "pt", n)
                for m in range(2):
                    emptied(pe, l, "v", m)
                for b in range(DEC):
                    w = weights(pe, l, "cv", b).rearrange("p (m c) -> p m c", m=2)
                    if b == 0:
                        for h in range(H_C):
                            take(pe, l, "o", h)
                            for m in range(2):
                                product(bank(l, "o", h)[:, 0:SEQ], vm[:, m, P * h:P * h + P],
                                        pT[:, h, N_MEM * m:N_MEM * m + SEQ], m, 2)
                    for h in range(H_C):
                        for m in range(2):
                            c = 2 * P * m + 32 * b + DSEQ * h
                            ins = product(bank(l, "o", h)[:, SEQ + DSEQ * b:SEQ + DSEQ * b + DSEQ],
                                          w[:, m, P * h:P * h + P], pT[:, H_C, c:c + DSEQ], m, 2)
                    step(ins)
                pe.wait_ge(conv_b_done, 4 * (l + 1))
                for n in range(2 * JB):
                    if n % JB == 0:
                        w = weights(pe, l, "rg", n // JB)
                    take(pe, l, "rg", n)
                    j = n % JB
                    step(pe.matmul(bank(l, "rg", n)[:, 0:T], w[:, P * j:P * j + P], cb[:, j], start=True, stop=True))
                for br, yk, src in ((0, "ya", sa), (2, "yc", oT)):
                    for n in range(0, KT, 2):
                        blocks((l, "g", br, n), xT, n, T)
                        blocks((l, "g", br, n + 1), xT, n, T)
                        if n == 0 and br == 0:
                            pe.wait_ge(lna_done, JA * (l + 1))
                        if n == 0 and br == 2:
                            for h in range(H_C):
                                emptied(pe, l, "o", h)
                        w = weights(pe, l, yk, n // 2)
                        for m in range(2):
                            blocks((l, yk, n + m), src, n, T, kt=4, unit=w[:, 512 * m:512 * m + 512])
                for n in range(KT):
                    blocks((l, "g", 1, n), xT, n, T)
                    if n == 0:
                        pe.wait_ge(hg_ready, l + 1)
                    blocks((l, "yb", n), gg, n, T)
                for k in range(KT):
                    pe.wait_ge(mg_ready, KT * l + k + 1)
                    rows_of((l, "mix", k), k, KT, mg[:, k])
                turn_x(l, "xt", 2 * l + 1)
                for k in range(KT):
                    emptied(pe, l, "xt", k)
                if l % 2 == 0:
                    for f in range(0, FT, 2):
                        for w in "gu":
                            for n in (f, f + 1):
                                blocks3((l, w, n), xTh, xTl, n, T)
                    for f in range(FT):
                        pe.wait_ge(dhl_ready, f + 1)
                        rows_of3((l, "down", f), f, FT, hTh[:, f], hTl[:, f])
                    turn_x(l, "xt2", 2 * l + 2)
            pe.wait_ge(router_in, 32)
            take(pe, "router")
            for t, r0 in enumerate(TOK):
                for k in range(KT):
                    ins = product(bank("router")[:, NE * t:NE * t + NE], xT[:, k, r0:r0 + P], wr[:, k], k, KT)
            step(ins)
            take(pe, "pos")
            pe.wait_ge(hit_ready, 1)
            for t in range(3):
                for s in range(t + 1):
                    product(bank("pos")[:, NE * t:NE * t + NE], (upper if s == t else ones)[:], hit[:, s], s, t + 1)
            for s in range(3):
                ins = product(bank("pos")[:, 3 * NE:4 * NE], ones[:], hit[:, s], s, 3)
            step(ins)

            def gather(key, i=None):
                for n in range(4):
                    take(pe, *key, n, i=i)
                    for m in range(2):
                        k = 2 * n + m
                        for t in range(3):
                            ins = product(bank(*key, n)[:, CAP * m:CAP * m + CAP], x[:, t, P * k:P * k + P],
                                          pick[:, t, :], t, 3)
                    step(ins)

            pe.wait_ge(pick_ready, 3)
            gather(("gather0",))
            for n in range(4):
                emptied(pe, "gather0", n)

            def turn(i, cap):
                for n in range(4):
                    emptied_before(pe, "e", "gather", n, i=i)
                for f in range(0, FT, 2):
                    for w in "gu":
                        take(pe, "e", w, f // 2, i=i)
                        for n in (f, f + 1):
                            u = weights(pe, "e", w, n, i=i).rearrange("p (k n) -> p k n", n=P)
                            out = bank("e", w, f // 2)[:, CAP * (n - f):CAP * (n - f) + cap]
                            for k in range(KT):
                                ins = product(out, u[:, k], xe[:, k, 0:cap], k, KT)
                            step(ins)
                    if f == 0:
                        for n in range(2):
                            r, g, c, w = pt_place(n, cap)
                            take(pe, "e", "pt", n, i=i)
                            for t in (2, 0, 1):
                                if c <= TOK[t] < c + w:
                                    ins = pe.transpose(bank("e", "pt", n)[0:r, TOK[t]:TOK[t] + P],
                                                       pick[:, t, P * g:P * g + r], ident[:])
                            step(ins)
                pe.wait_ge(pick_ready, i * 3 + 6)
                gather(("e", "gather"), i=i)
                for f in range(FT):
                    u = weights(pe, "e", "down", f, i=i)
                    if f == 0:
                        for n in range(4):
                            take(pe, "e", "down", n, i=i)
                    if f % 2 == 0:
                        emptied(pe, "e", "u", f // 2, i=i)
                    for n in range(KT):
                        ins = pe.matmul(bank("e", "down", n // 2)[:, CAP * (n % 2):CAP * (n % 2) + cap],
                                        u[:, P * n:P * n + P], he[:, f, 0:cap], start=(f == 0 and n % 2 == 0),
                                        stop=(f == FT - 1), skip_group_check=True)
                    step(ins)
                for n in range(4):
                    r, g, c, w = yt_place(n, cap)
                    take(pe, "e", "yt", n, i=i)
                    for k in range(c // P, (c + w) // P):
                        if k % 2 == 0:
                            emptied(pe, "e", "down", k // 2, i=i)
                        ins = pe.transpose(bank("e", "yt", n)[0:r, P * k - c:P * k - c + P],
                                           ye[:, k, P * g:P * g + r], ident[:])
                    step(ins)
                for n in range(2):
                    emptied(pe, "e", "pt", n, i=i)
                for n in range(4):
                    emptied(pe, "e", "yt", n, i=i)
                for n, (t, c, w) in enumerate(Y_TILES):
                    take(pe, "e", "y", n, i=i)
                    for g in range((cap + P - 1) // P):
                        r = min(cap - P * g, P)
                        ins = pe.matmul(bank("e", "y", n)[:, 0:w], pg[0:r, g, TOK[t]:TOK[t] + P],
                                        ys[0:r, g, c:c + w], start=(g == 0), stop=(P * (g + 1) >= cap))
                    step(ins)

            turns(pe, turn)

    return nc


def _blocks(w):
    k, n = w.shape
    return w.reshape(k // P, P, n // P, P).transpose(2, 1, 0, 3).reshape(n // P, P, k)


def _halves(w):
    return w.reshape(4, P, 4, 2, P).transpose(2, 1, 3, 0, 4).reshape(4, P, UNIT)


def _ffn(gate, up, down):
    import numpy as np

    g, u = (_blocks(a).reshape(FT // 2, 2, P, UNIT) for a in (gate, up))
    return np.concatenate([np.concatenate([g, u], 1).reshape(2 * FT, P, UNIT), down.reshape(FT, P, UNIT)])


def _mix_units(a, l):
    import numpy as np

    win = _blocks(a["w_in"][l])
    za = np.stack([win[ZA_U:ZA_U + JA], win[ZA_G:ZA_G + JA]], 1).reshape(2 * JA, P, UNIT)
    kv = a["w_mem_kv"][l]
    v = kv[:, D_C:].reshape(4, 2, P, D_C).transpose(0, 2, 1, 3).reshape(4, P, UNIT)
    ck = a["cache_mem_k"][l].transpose(0, 3, 2, 1).reshape(DEC, P, UNIT)
    cv = a["cache_mem_v"][l].reshape(DEC, 2, P, D_C).transpose(0, 2, 1, 3).reshape(DEC, P, UNIT)
    rg = [a[n][l].transpose(1, 0, 2).reshape(1, P, UNIT) for n in ("w_rg_a", "w_rg_x")]
    parts = [win[ZB:ZB + JB], za, win[ZQ:ZQ + JC], _blocks(kv[:, :D_C]), v, ck, win[ZG:ZG + JB], cv, *rg]
    for br, name in ((0, "w_a_out"), (2, "w_c_out")):
        g = win[ZM + KT * br:ZM + KT * br + KT].reshape(4, 2, P, UNIT)
        parts.append(np.concatenate([g, _halves(a[name][l])[:, None]], 1).reshape(12, P, UNIT))
    parts.append(np.stack([win[ZM + KT:ZM + 2 * KT], _blocks(a["w_b_out"][l])], 1).reshape(2 * KT, P, UNIT))
    parts.append(a["w_mix_out"][l].reshape(KT, P, UNIT))
    return np.concatenate(parts)


def _channels(v):
    import numpy as np

    v = np.moveaxis(v, -1, 1)
    return v.reshape(DEPTH, v.shape[1] // P, P, -1).transpose(0, 2, 1, 3).reshape(DEPTH, P, -1)


def kernel(**inputs):
    import numpy as np
    import concourse.bacc as bacc
    from concourse.bass_utils import run_bass_kernel_spmd as run

    a = {k: np.asarray(v) for k, v in inputs.items()}
    x0 = np.concatenate([a["x_prompt"].reshape(SEQ, D), a["x_sample"].reshape(NSAMP, D)])
    feature = lambda v: np.ascontiguousarray(v.T.reshape(KT, P, -1).transpose(1, 0, 2))
    experts = np.concatenate([_ffn(a["w_e_gate"][0, e], a["w_e_up"][0, e], a["w_e_down"][0, e]) for e in range(NE)])
    arrays = {
        "x0": x0,
        "x0T": feature(x0),
        "memT": feature(a["mem_prompt"][0]),
        "chan": np.concatenate([_channels(a[n]) for n in COL if n != "lam"] + [_channels(a["lru_lambda"])], 2),
        "rows": np.stack([a["ln1_g"], a["ln1_b"], a["ln2_g"], a["ln2_b"]], 1),
        "hist": np.concatenate([_channels(a["state_conv_a"]), _channels(a["state_conv_b"]),
                                _channels(a["state_rglru"])], 2),
        "stream": np.concatenate([_mix_units(a, 0), _ffn(a["w_ff_gate"][0], a["w_ff_up"][0], a["w_ff_down"][0]),
                                  _mix_units(a, 1)]),
        "router_w": np.ascontiguousarray(a["w_router"][0].reshape(KT, P, NE).transpose(1, 0, 2)),
        "router_b": a["b_router"][0],
        "experts": np.concatenate([experts, experts[:E_SLOTS]]),
    }
    outs = {"y": (T, D), "o_a": (DEPTH, P, JA * 9 * (K_A - 1)), "o_b": (DEPTH, P, JB * 9 * (K_B - 1)),
            "o_h": (DEPTH, P, JB * 9), "o_k": (DEPTH, P, H_C, N_MEM), "o_v": (DEPTH, P, 2, D_C)}
    nc = bacc.Bacc("TRN2", target_bir_lowering=False, num_devices=1)
    args = [nc.dram_tensor(n, v.shape, F32, kind="ExternalInput").ap() for n, v in arrays.items()]
    args += [nc.dram_tensor(n, s, F32, kind="ExternalOutput").ap() for n, s in outs.items()]
    trunk(nc, *args)
    r = run(nc, [arrays], core_ids=[0]).results[0]
    ca = r["o_a"].reshape(DEPTH, P, JA, 9, K_A - 1).transpose(0, 3, 4, 2, 1).reshape(DEPTH, 9, K_A - 1, D_A)
    cb = r["o_b"].reshape(DEPTH, P, JB, 9, K_B - 1).transpose(0, 3, 4, 2, 1).reshape(DEPTH, 9, K_B - 1, D_B)
    h = r["o_h"].reshape(DEPTH, P, JB, 9).transpose(0, 3, 2, 1).reshape(DEPTH, 9, D_B)
    mk = r["o_k"].transpose(0, 3, 2, 1).reshape(DEPTH, 1, N_MEM, H_C, P)
    mv = r["o_v"].transpose(0, 2, 1, 3).reshape(DEPTH, 1, N_MEM, H_C, P)
    y = r["y"]
    return (y[:SEQ].reshape(1, SEQ, D), y[SEQ:].reshape(DEC, DSEQ, D), ca[:, :1], cb[:, :1], h[:, :1], mk, mv,
            ca[:, 1:], cb[:, 1:], h[:, 1:])
```

```python
from contextlib import ExitStack

import concourse.bass as bass
from concourse import mybir

F32 = mybir.dt.float32
F32R = mybir.dt.float32r
I32 = mybir.dt.int32
U32 = mybir.dt.uint32
ALU = mybir.AluOpType
ACT = mybir.ActivationFunctionType
AX = mybir.AxisListType

P = 128
DEPTH = 2
D = 1024
KT = D // P
SEQ, DEC, DSEQ = 256, 8, 8
NSAMP = DEC * DSEQ
T = SEQ + NSAMP
TOK = [0, 128, T - 128]
DUP = 64
N_MEM = 256
D_A, K_A = 512, 31
D_B, K_B = 1024, 4
D_C, H_C = 512, 4
JA, JB, JC = D_A // P, D_B // P, D_C // P
D_IN = 2 * D_A + 2 * D_B + D_C + 3 * D
D_FF = 2816
FT = D_FF // P
NE = 8
CAP = T // 2
SIZES = [96, P, CAP]
ALPHA = (2.0 * DEPTH) ** 0.25
EPS = 1e-5
QSCALE = float(P) ** -0.5

LN_STEPS = len(TOK)
HIST = 1 + JB + 2 + JA
SLOTS = 6
E_SLOTS = 11
SPLITS = 3
AHEAD = 2
UNIT = 1024
SBUF_FIRST, SBUF_END = 16512, 229344
BANKS = 8
TURN = (2, 0, 1)
MAX_TAPS, PROBS_TAP = {15: range(0, 4), 16: range(4, 8), 21: [8], 26: [9]}, 29
BRANCHES = [(2, "yc"), (0, "ya"), (1, "yb")]
Y_TILES = [(t, c, 256) for t in range(3) for c in range(0, D, 256)]
SEG_A = K_A - 1 + DSEQ
SEG_B = K_B - 1 + DSEQ
LEN_A = K_A - 1 + SEQ + DEC * SEG_A
LEN_B = K_B - 1 + SEQ + DEC * SEG_B

_c = 0
COL = {}
for _name, _n in (("b_in", D_IN // P), ("w_conv_a", JA * K_A), ("b_conv_a", JA), ("ln_a_g", JA), ("ln_a_b", JA),
                  ("w_conv_b", JB * K_B), ("b_conv_b", JB), ("b_rg_a", JB), ("b_rg_x", JB), ("ln1_g", JB),
                  ("ln1_b", JB), ("ln2_g", JB), ("ln2_b", JB), ("lam", JB)):
    COL[_name] = _c
    _c += _n
NCOL = _c
ZA_U, ZA_G, ZB, ZG, ZQ, ZM = 0, JA, 2 * JA, 2 * JA + JB, 2 * JA + 2 * JB, 2 * JA + 2 * JB + JC


class Tile:

    def __init__(self, bank, use):
        self.bank, self.use, self.done = bank, use, None


class Plan:

    def __init__(self):
        self.steps = 0
        self.tiles = {}
        self.next_bank = 0
        self.uses = [0] * BANKS
        self.unit_done = []
        self.unit_of = {}
        self.split = {}

    def tile(self, *key, bank=None):
        if bank is None:
            bank = self.next_bank
            self.next_bank = (bank + 1) % BANKS
        self.tiles[key] = Tile(bank, self.uses[bank])
        self.uses[bank] += 1

    def step(self, closes=(), unit=None, split=False):
        self.steps += 1
        for key in closes:
            if key not in self.tiles:
                self.tile(*key)
            self.tiles[key].done = self.steps
        if unit is not None:
            self.unit_of[unit] = len(self.unit_done)
            if split:
                self.split[len(self.unit_done)] = len(self.split)
            self.unit_done.append(self.steps)

    def rows(self, l, name, n_units):
        for n in range(6):
            self.tile(l, name, n)
        for k in range(n_units - 1):
            self.step((), (l, name, k), split=True)
        for t in TURN:
            last = t == TURN[-1]
            self.step([(l, name, 2 * t), (l, name, 2 * t + 1)], (l, name, n_units - 1) if last else None, split=last)

    def raw_unit(self, *key):
        self.unit_of[key] = len(self.unit_done)
        self.unit_done.append(self.steps)


def make_plan():
    p = Plan()
    for l in range(DEPTH):
        for n in range(2 * JA):
            p.step([(l, "za", n)], (l, "za", n), split=True)
        p.raw_unit(l, "mem", 0)
        p.raw_unit(l, "mem", 1)
        for n in range(JC):
            p.step([(l, "q", n)], (l, "q", n), split=True)
        for n in range(H_C):
            p.step([(l, "k", n)], (l, "k", n), split=True)
        for m in range(2):
            p.tile(l, "v", m)
        for c in range(4):
            p.step([(l, "v", m) for m in range(2)] if c == 3 else [], (l, "v", c), split=True)
        for n in range(8):
            p.step([(l, "ps", n)])
        for b in range(DEC):
            if b % 4 == 0:
                p.tile(l, "ss", b // 4)
            p.step([(l, "zb", b)], (l, "zb", b), split=True)
            p.step([(l, "ss", b // 4)] if b % 4 == 3 else [], (l, "ck", b))
        for n in range(JB):
            p.step([(l, "zg", n)], (l, "zg", n), split=True)
        for n in range(H_C + 1):
            p.step([(l, "pt", n)])
        for h in range(H_C):
            p.tile(l, "o", h)
        others = [(p.next_bank + n) % BANKS for n in range(4)]
        p.tile(l, "mean", 0, bank=others[0])
        p.step([(l, "mean", 0)])
        for n in range(KT):
            p.tile(l, "g", 2, n, bank=others[(n + 1) % 4])
        p.tile(l, "var", 0, bank=others[(KT + 1) % 4])
        for br, y in BRANCHES:
            for n in range(KT):
                if br == 2:
                    p.step([(l, "o", h) for h in range(H_C)] if n == DEC - 1 else [], (l, "cv", n))
                p.step([(l, "g", br, n)], (l, "g", br, n), split=True)
            if br == 2:
                p.step([(l, "var", 0)])
            for n in range(KT):
                if y == "yb":
                    p.step([(l, y, n)], (l, y, n), split=True)
                elif n % 2 == 0:
                    p.step([(l, y, n)])
                    p.step([(l, y, n + 1)], (l, y, n // 2), split=True)
            if br == 2:
                for n in range(2 * JB):
                    p.step([(l, "rg", n)], (l, "rg", n // JB) if n % JB == JB - 1 else None)
        p.rows(l, "mix", KT)
        for k in range(KT):
            p.step([(l, "xt", k)])
        if l % 2 == 0:
            for f in range(0, FT, 2):
                for w in "gu":
                    for n in (f, f + 1):
                        p.step([(l, w, n)], (l, w, n), split=True)
            p.rows(l, "down", FT)
            for k in range(KT):
                p.step([(l, "xt2", k)])
    p.step([("router",)])
    p.step([("logits",)])
    p.step([("pos",)])
    for n in range(4):
        p.step([("gather0", n)])
    first, first_unit, first_tile = p.steps, len(p.unit_done), len(p.tiles)
    for f in range(0, FT, 2):
        for w in "gu":
            p.tile("e", w, f // 2)
            for n in (f, f + 1):
                p.step([("e", w, f // 2)] if n == f + 1 else [], ("e", w, n))
        if f == 0:
            for n in range(2):
                p.step([("e", "pt", n)])
    for n in range(4):
        p.step([("e", "gather", n)])
    for n in range(4):
        p.tile("e", "down", n)
    for f in range(FT):
        p.step([("e", "down", n) for n in range(4)] if f == FT - 1 else [], ("e", "down", f))
    for n in range(4):
        p.step([("e", "yt", n)])
    for n in range(len(Y_TILES)):
        p.step([("e", "y", n)])
    p.per_steps = p.steps - first
    p.per_units = len(p.unit_done) - first_unit
    p.loop_unit = first_unit
    per_tiles = len(p.tiles) - first_tile
    assert per_tiles % BANKS == 0 and p.per_units % E_SLOTS == 0
    p.per_use = per_tiles // BANKS
    p.per_slot = p.per_units // E_SLOTS
    return p


def trunk(nc, x0, x0T, chan, rows, hist, stream, router_w, router_b, experts,
          y, o_a, o_b, o_h, o_k, o_v):
    plan = make_plan()
    n_units = plan.loop_unit
    assert stream.shape[0] == n_units

    with ExitStack() as ctx:
        sbuf_at = [SBUF_FIRST]

        def place(name, shape, at, dt=F32):
            return nc.alloc_sbuf_tensor_at(name, shape, dt, offset=at)

        def sb(name, shape, dt=F32):
            n = 4
            for d in shape[1:]:
                n *= d
            at = sbuf_at[0]
            sbuf_at[0] += (n + 31) // 32 * 32
            assert sbuf_at[0] <= SBUF_END, name
            return place(name, shape, at, dt)

        def sem(name):
            return ctx.enter_context(nc.semaphore(name))

        psum = ctx.enter_context(nc.psum_tensor("psum", [P, BANKS, 512], F32))
        ring_at = sbuf_at[0]
        ring = sb("ring", [P, SLOTS + 2 * SPLITS, UNIT])
        wh = place("wh", [P, SPLITS, UNIT], ring_at + 4 * UNIT * SLOTS, F32R)
        wl = place("wl", [P, SPLITS, UNIT], ring_at + 4 * UNIT * (SLOTS + SPLITS), F32R)
        x = sb("x", [P, 3, D])
        xTh = sb("xTh", [P, KT, T], F32R)
        xTl = sb("xTl", [P, KT, T], F32R)
        lnp = sb("lnp", [P, 2, D])
        par = sb("par", [P, DEPTH, NCOL])
        ident = sb("ident", [P, P])
        ones = sb("ones", [P, P])
        upper = sb("upper", [P, P])
        iota = sb("iota", [P, CAP])
        small = sb("small", [P, 256])
        tails = sb("tails", [P, 288])
        stat = sb("stat", [P, 50])
        spl = sb("spl", [P, DEPTH * JB])
        nvi = sb("nvi", [P, 1], I32)
        size = sb("size", [P, 2 * NE], I32)

        ARENA = 28248
        arena_at = sbuf_at[0]
        arena = sb("arena", [P, ARENA])
        off = [0]

        def cut(n, a=None):
            at = off[0]
            off[0] += n
            assert off[0] <= ARENA
            v = arena[:, at:at + n]
            return v.rearrange("p (a b) -> p a b", a=a) if a else v

        def cut_r(name, n, a):
            v = place(name, [P, a, n // a], arena_at + 4 * off[0], F32R)
            off[0] += n
            assert off[0] <= ARENA
            return v

        def share(n, *names):
            at = arena_at + 4 * off[0]
            return [cut(n)] + [place(name, [P, a, c], at, F32R) for name, a, c in names]

        def blocks_of(v, a, n):
            return v[:, 0:a * n].rearrange("p (a b) -> p a b", a=a)

        v, mgh = share(JB * T, ("mgh", KT, T))
        ua, ig, ig_flat = blocks_of(v, JA, LEN_A), blocks_of(v, JB, T), v
        v, hgl = share(JB * LEN_B, ("hgl", JB, T))
        zb, w_b = blocks_of(v, JB, LEN_B), blocks_of(v, JB, T)
        v, sal = share(JA * T, ("sal", JA, T))
        sg = blocks_of(v, JA, T)
        v, sah = share(JA * T, ("sah", JA, T))
        ca = blocks_of(v, JA, T)
        cb = cut(JB * T, JB)
        v, oTl = share(JC * T, ("oTl", JC, T))
        qT, part = blocks_of(v, JC, T), blocks_of(v, 2, T)
        v = cut(DEC * P + H_C * N_MEM + 2 * D_C)
        qpad = blocks_of(v, DEC, P)
        kT = blocks_of(v[:, DEC * P:], H_C, N_MEM)
        vm = blocks_of(v[:, DEC * P + H_C * N_MEM:], 2, D_C)
        gz = blocks_of(v, KT, T)
        v = cut(KT * T)
        pp, mg = blocks_of(v, 10, N_MEM), blocks_of(v, KT, T)
        v, meml, mgl = share(JB * T, ("meml", KT, N_MEM), ("mgl", KT, T))
        pT, aa = blocks_of(v, 5, 2 * N_MEM), blocks_of(v, JB, T)
        v, oTh = share(JC * T, ("oTh", JC, T))
        v, memh, hgh = share(JB * T, ("memh", KT, N_MEM), ("hgh", JB, T))
        rr = blocks_of(v, JB, T)
        gg_flat = cut(JB * T)
        gg = blocks_of(gg_flat, JB, T)
        sa_flat = cut(JA * T)
        sa = blocks_of(sa_flat, JA, T)
        dev = cut(T)
        hist_a = gg_flat[:, 0:JA * DEC * (K_A - 1)].rearrange("p (a b c) -> p a b c", a=JA, b=DEC)
        tail_a = sa_flat[:, 0:JA * 9 * (K_A - 1)].rearrange("p (a b c) -> p a b c", a=JA, b=9)
        hist_b = small[:, 0:192].rearrange("p (a b c) -> p a b c", a=JB, b=DEC)
        h0 = small[:, 192:256].rearrange("p (a b) -> p a b", a=JB)
        tail_b = tails[:, 0:216].rearrange("p (a b c) -> p a b c", a=JB, b=9)
        tail_h = tails[:, 216:288].rearrange("p (a b) -> p a b", a=JB)
        off[0] = 0
        hTh, hTl = cut_r("hTh", FT * T, FT), cut_r("hTl", FT * T, FT)
        dsig = cut(2 * T, 2)
        dlin = cut(2 * T, 2)
        dh = cut(2 * T, 2)
        xaff = cut(3 * T, 3)
        off[0] = 0
        yacc = cut(3 * D, 3)
        xe = cut(KT * CAP, KT)
        he = cut(FT * CAP, FT)
        ye = cut(KT * CAP, KT)
        ys = cut(2 * D, 2)
        pg = cut(2 * T, 2)
        pick = cut(3 * CAP, 3)
        xT = cut(KT * T, KT)
        esig = cut(4 * CAP, 4)
        elin = cut(4 * CAP, 4)
        wr = cut(KT * NE, KT)
        brow = cut(NE)
        lgT = cut(T)
        lg = cut(3 * NE, 3)
        top = cut(3 * 8, 3)
        topf = cut(3 * 2, 3)
        gate2 = cut(3 * 2, 3)
        den = cut(3)
        m1 = cut(3 * NE, 3)
        m2 = cut(3 * NE, 3)
        hit = cut(3 * NE, 3)
        gates = cut(3 * (2 * NE), 3)
        slot = cut(3 * (2 * NE + 1), 3)
        count = cut(NE)
        nmax = cut(2)
        eps_c = sb("eps_c", [P, 1])
        stats = sb("stats", [P, 3, 2, 6])
        mv = sb("mv", [P, 3, 4])
        lamw = sb("lamw", [P, 6, DEPTH, JB])
        topi = sb("topi", [P, 3, 8], U32)

        slot_full = [sem(f"slot_full{s}") for s in range(E_SLOTS)]
        mm_done = sem("mm_done")
        evac = [sem(f"evac{b}") for b in range(BANKS)]
        x_in, xt_in, par_in = sem("x_in"), sem("xt_in"), sem("par_in")
        memh_ready, meml_ready = sem("memh_ready"), sem("meml_ready")
        xtl_ready, xn_ready = sem("xtl_ready"), sem("xn_ready")
        oh_ready = sem("oh_ready")
        sah_ready, sal_ready = sem("sah_ready"), sem("sal_ready")
        hgh_ready, hgl_ready = sem("hgh_ready"), sem("hgl_ready")
        mgh_ready, mgl_ready = sem("mgh_ready"), sem("mgl_ready")
        ln_in = sem("ln_in")
        hi_done, lo_done = sem("hi_done"), sem("lo_done")
        xth_ready = sem("xth_ready")
        dhh_ready, dhl_ready = sem("dhh_ready"), sem("dhl_ready")
        hist_in, hist_small_in = sem("hist_in"), sem("hist_small_in")
        router_in = sem("router_in")
        kv_out, tail_a_out, tail_b_out, h_out, y_out = (sem("kv_out"), sem("tail_a_out"), sem("tail_b_out"),
                                                        sem("h_out"), sem("y_out"))
        const_step, const_ready = sem("const_step"), sem("const_ready")
        hist_ready = sem("hist_ready")
        tails_ready = sem("tails_ready")
        htail_ready = sem("htail_ready")
        dve_step = sem("dve_step")
        spl_exp, spl_ready = sem("spl_exp"), sem("spl_ready")
        spl_ask = sem("spl_ask")
        eps_ready, bn_done, sa_lin, mg_part = sem("eps_ready"), sem("bn_done"), sem("sa_lin"), sem("mg_part")
        yacc_ready, lg_zero, pos_read = sem("yacc_ready"), sem("lg_zero"), sem("pos_read")
        glu_done = sem("glu_done")
        conv_b_done = sem("conv_b_done")
        conv_a_tap = sem("conv_a_tap")
        negmax = sem("negmax")
        probs = sem("probs")
        dev_ready = sem("dev_ready")
        lna_norm, lna_sig, lna_done = sem("lna_norm"), sem("lna_sig"), sem("lna_done")
        a_ready, tanh_done = sem("a_ready"), sem("tanh_done")
        a2_ready, root_ready = sem("a2_ready"), sem("root_ready")
        h_ready, hg_ready = sem("h_ready"), sem("hg_ready")
        xg_ready = sem("xg_ready")
        var_ready, std_ready, x_ready = sem("var_ready"), sem("std_ready"), sem("x_ready")
        top_ready, exp_ready = sem("top_ready"), sem("exp_ready")
        hit_ready, nv_ready, pick_ready = sem("hit_ready"), sem("nv_ready"), sem("pick_ready")
        mg_ready = sem("mg_ready")
        dsig_ready, esig_ready = sem("dsig_ready"), sem("esig_ready")

        def tile_of(*key):
            return plan.tiles[key]

        def bank(*key):
            return psum[:, plan.tiles[key].bank, :]

        mem_units = [plan.unit_of[l, "mem", n] for l in range(DEPTH) for n in range(2)]

        def turn_slot(k):
            k %= E_SLOTS
            return (n_units + k) % SLOTS if k < SLOTS else k

        stream_loads = [len(range(s, n_units, SLOTS)) if s < SLOTS else 0 for s in range(E_SLOTS)]

        def filled(eng, *key, i=None):
            v = plan.tiles[key].done
            eng.wait_ge(mm_done, v if i is None else i * plan.per_steps + v)

        def emptied_before(eng, *key, i):
            t = plan.tiles[key]
            eng.wait_ge(evac[t.bank], i * plan.per_use + (t.use + 1 - plan.per_use))

        def emptied(eng, *key, i=None):
            t = plan.tiles[key]
            eng.wait_ge(evac[t.bank], t.use + 1 if i is None else i * plan.per_use + (t.use + 1))

        def frees(ins, *key):
            ins.then_inc(evac[plan.tiles[key].bank], 1)

        def take(eng, *key, i=None):
            t = plan.tiles[key]
            if i is not None:
                eng.wait_ge(evac[t.bank], i * plan.per_use + t.use)
            elif t.use:
                eng.wait_ge(evac[t.bank], t.use)

        def weights(eng, *key, i=None):
            u = plan.unit_of[key]
            if i is None:
                slot_wait(eng, u)
                return ring[:, u % SLOTS, :]
            k = u - plan.loop_unit
            s = turn_slot(k)
            eng.wait_ge(slot_full[s], i * (16 * plan.per_slot) + 16 * (stream_loads[s] + k // E_SLOTS + 1))
            return ring[:, s, :]

        def slot_wait(eng, u):
            eng.wait_ge(slot_full[u % SLOTS], 16 * (u // SLOTS + 1))

        def parts(eng, *key):
            q = plan.split[plan.unit_of[key]]
            eng.wait_ge(lo_done, q + 1)
            return wh[:, q % SPLITS, :], wl[:, q % SPLITS, :]

        split_steps = [plan.unit_done[u] for u in plan.split]

        def make_hi(act, u):
            q = plan.split[u]
            slot_wait(act, u)
            if q >= SPLITS:
                act.wait_ge(mm_done, split_steps[q - SPLITS])
            act.copy(wh[:, q % SPLITS, :], ring[:, u % SLOTS, :]).then_inc(hi_done, 1)

        def make_lo(pool, u):
            q = plan.split[u]
            pool.wait_ge(hi_done, q + 1)
            pool.tensor_tensor(wl[:, q % SPLITS, :], ring[:, u % SLOTS, :], wh[:, q % SPLITS, :].bitcast(F32),
                               ALU.subtract).then_inc(lo_done, 1)

        def near(u, step):
            return (plan.split[u] < sum(done <= step for done in split_steps) + AHEAD and
                    u < sum(done <= step for done in plan.unit_done) + 2 * AHEAD)

        def samp(v):
            return v.rearrange("p (b t) -> p b t", b=DEC)

        def seg_a(j, k, n):
            return ua[:, j, K_A - 1 + SEQ:LEN_A].rearrange("p (b s) -> p b s", b=DEC)[:, :, k:k + n]

        def seg_b(j, k, n):
            return zb[:, j, K_B - 1 + SEQ:LEN_B].rearrange("p (b s) -> p b s", b=DEC)[:, :, k:k + n]

        def col(l, name, n=0, w=1):
            c = COL[name] + n
            return par[:, l, c:c + w]

        def pair(v, n, cap=CAP):
            return v[:, 2 * n:2 * n + 2, 0:cap]

        def bank_pair(*key, cap=CAP):
            return bank(*key)[:, 0:2 * CAP].rearrange("p (a b) -> p a b", a=2)[:, :, 0:cap]

        def yt_place(n, cap):
            if cap <= P:
                return cap, 0, 256 * n, 256
            return (P if n < 2 else cap - P), n // 2, 512 * (n % 2), 512

        def pt_place(n, cap):
            if cap <= P:
                return cap, 0, P * n, (P if n == 0 else T - P)
            return (P if n == 0 else cap - P), n, 0, T

        def turns(eng, turn):
            eng.wait_ge(nv_ready, 1)
            nv = eng.value_load(nvi[0:1, 0:1], min_val=NE, max_val=2 * NE)
            with eng.Fori(0, nv) as i:
                n = eng.value_load(size[0:1, bass.ds(i, 1)], min_val=0, max_val=2)
                with eng.If(n > 1):
                    turn(i, SIZES[2])
                with eng.Else():
                    with eng.If(n > 0):
                        turn(i, SIZES[1])
                    with eng.Else():
                        turn(i, SIZES[0])
            return nv

        def layer_norm_std(act, n):
            act.wait_ge(eps_ready, 1)
            for m, t in enumerate(TURN):
                act.wait_ge(var_ready, 3 * n + m + 1)
                act.activation(mv[:, t, 2:3], mv[:, t, 1:2], ACT.Sqrt, bias=eps_c[:, 0:1])\
                   .then_inc(std_ready, 1)

        block = ctx.enter_context(nc.Block())

        @block.sync
        def _(sp):
            for u in range(n_units):
                if u - SLOTS in plan.split:
                    sp.wait_ge(lo_done, plan.split[u - SLOTS] + 1)
                elif u - SLOTS in mem_units:
                    sp.wait_ge(meml_ready, mem_units.index(u - SLOTS) + 1)
                elif u >= SLOTS:
                    sp.wait_ge(mm_done, plan.unit_done[u - SLOTS])
                sp.dma_start(ring[:, u % SLOTS, :], stream[u]).then_inc(slot_full[u % SLOTS], 16)
            for k in range(E_SLOTS):
                if k < SLOTS:
                    sp.wait_ge(lo_done, plan.split[n_units + k - SLOTS] + 1)
                elif k == SLOTS:
                    sp.wait_ge(mm_done, split_steps[-1])
                sp.dma_start(ring[:, turn_slot(k), :], experts[k]).then_inc(slot_full[turn_slot(k)], 16)

            def expert(i, e):
                for k in range(plan.per_units):
                    sp.wait_ge(mm_done, i * plan.per_steps + plan.unit_done[plan.loop_unit + k])
                    sp.dma_start(ring[:, turn_slot(k), :], experts[e * plan.per_units + (E_SLOTS + k)])\
                        .then_inc(slot_full[turn_slot(k)], 16)

            with sp.Fori(0, NE) as i:
                expert(i, i)
            sp.wait_ge(nv_ready, 1)
            nv = sp.value_load(nvi[0:1, 0:1], min_val=NE, max_val=2 * NE)
            with sp.If(nv > NE):
                with sp.Fori(NE, 2 * NE) as i:
                    expert(i, i - NE)

        @block.gpsimd
        def _(pool):
            pool.dma_start(cb, x0T).then_inc(xt_in, 16)
            pool.dma_start(par[:], chan.rearrange("l p c -> p l c")).then_inc(par_in, 16)
            pool.memset(ones[:], 1.0).then_inc(const_step, 1)
            pool.memset(ident[:], 0.0).then_inc(const_step, 1)
            pool.iota(iota[:], pattern=[[1, CAP]], base=0, channel_multiplier=0,
                      allow_small_or_imprecise_dtypes=True).then_inc(const_ready, 1)
            pool.wait_ge(const_step, 2)
            pool.affine_select(out=ident[:], in_=ident[:], compare_op=ALU.not_equal, fill=1.0, base=0,
                               pattern=[[-1, P]], channel_multiplier=1).then_inc(const_ready, 1)
            pool.affine_select(out=upper[:], in_=ones[:], compare_op=ALU.is_gt, fill=0.0, base=0,
                               pattern=[[1, P]], channel_multiplier=-1).then_inc(const_ready, 1)
            queue = list(plan.split)

            def split_for(step):
                while queue and near(queue[0], step):
                    make_lo(pool, queue.pop(0))

            for l in range(DEPTH):
                if l:
                    split_for(tile_of(l - 1, "xt2", KT - 1).done)
                    pool.wait_ge(xn_ready, LN_STEPS * 2 * l)
                pool.dma_start(small[:], hist[l, :, JA * DEC * (K_A - 1):]).then_inc(hist_small_in, 16)
                pool.dma_start(gg_flat[:, 0:JA * DEC * (K_A - 1)], hist[l, :, 0:JA * DEC * (K_A - 1)])\
                    .then_inc(hist_in, 16)
                if l == 0:
                    for t, r0 in enumerate(TOK):
                        pool.dma_start(x[:, t, :], x0[r0:r0 + P]).then_inc(x_in, 16)
                split_for(tile_of(l, "za", 0).done)
                pool.memset(zb[:, :, 0:K_B - 1], 0.0).then_inc(hist_ready, 1)
                pool.wait_ge(hist_small_in, 16 * (l + 1))
                for j in range(JB):
                    pool.tensor_copy(seg_b(j, 0, K_B - 1), hist_b[:, j]).then_inc(hist_ready, 1)
                split_for(tile_of(l, "za", 1).done)
                pool.memset(ua[:, :, 0:K_A - 1], 0.0).then_inc(hist_ready, 1)
                pool.memset(qpad[:], 0.0).then_inc(hist_ready, 1)
                split_for(tile_of(l, "za", 2).done)
                pool.wait_ge(hist_in, 16 * (l + 1))
                for j in range(JA):
                    pool.tensor_copy(seg_a(j, 0, K_A - 1), hist_a[:, j]).then_inc(hist_ready, 1)
                split_for(tile_of(l, "za", 4).done)
                if l:
                    pool.wait_ge(x_ready, LN_STEPS * 2 * l)
                pool.dma_start(lnp[:], rows[l, 0:2].partition_broadcast(P)).then_inc(ln_in, 16)
                split_for(tile_of(l, "v", 0).done)
                for n in range(H_C):
                    emptied(pool, l, "k", n)
                for n in range(2):
                    emptied(pool, l, "v", n)
                pool.dma_start(o_k[l], kT).then_inc(kv_out, 16)
                pool.dma_start(o_v[l], vm).then_inc(kv_out, 16)
                pool.wait_ge(glu_done, 2 * JA * (l + 1))
                pool.wait_ge(hist_ready, (l + 1) * HIST)
                for j in range(JA):
                    pool.tensor_copy(tail_a[:, j, 0, :], ua[:, j, SEQ:SEQ + K_A - 1]).then_inc(tails_ready, 1)
                    pool.tensor_copy(tail_a[:, j, 1:9, :], seg_a(j, DSEQ, K_A - 1)).then_inc(tails_ready, 1)
                pool.wait_ge(tails_ready, 2 * (JA + JB) * l + 2 * JA)
                pool.dma_start(o_a[l], sa_flat[:, 0:JA * 9 * (K_A - 1)]).then_inc(tail_a_out, 16)
                split_for(tile_of(l, "zg", 0).done)
                for j in range(JB):
                    emptied(pool, l, "zb", j)
                if l:
                    pool.wait_ge(tail_b_out, 16 * l)
                    pool.wait_ge(h_out, 16 * l)
                for j in range(JB):
                    pool.tensor_copy(tail_b[:, j, 0, :], zb[:, j, SEQ:SEQ + K_B - 1]).then_inc(tails_ready, 1)
                    pool.tensor_copy(tail_b[:, j, 1:9, :], seg_b(j, DSEQ, K_B - 1)).then_inc(tails_ready, 1)
                pool.wait_ge(tails_ready, 2 * (JA + JB) * (l + 1))
                pool.dma_start(o_b[l], tails[:, 0:216]).then_inc(tail_b_out, 16)
                split_for(tile_of(l, "yb", KT - 1).done)
                pool.wait_ge(h_ready, l + 1)
                pool.tensor_copy(tail_h[:, :, 0:1], cb[:, :, SEQ - 1:SEQ]).then_inc(htail_ready, 1)
                pool.tensor_copy(tail_h[:, :, 1:9], cb[:, :, SEQ + DSEQ - 1:T:DSEQ]).then_inc(htail_ready, 1)
                pool.wait_ge(htail_ready, 2 * (l + 1))
                pool.dma_start(o_h[l], tails[:, 216:288]).then_inc(h_out, 16)
                split_for(tile_of(l, "g", 3).done if l % 2 == 0 else tile_of(l, "xt", KT - 1).done)
                if l == DEPTH - 1:
                    pool.wait_ge(xn_ready, LN_STEPS * (2 * l + 1))
                    pool.dma_start(wr[:], router_w).then_inc(router_in, 16)
                    pool.dma_start(brow, router_b.partition_broadcast(P)).then_inc(router_in, 16)
                pool.wait_ge(x_ready, LN_STEPS * (2 * l + 1))
                pool.dma_start(lnp[:], rows[l, 2:4].partition_broadcast(P)).then_inc(ln_in, 16)
            for t, r in ((0, 0), (1, 0), (2, DUP)):
                pool.wait_ge(x_ready, LN_STEPS * (2 * DEPTH - 1) + t + 1)
                pool.dma_start(y[TOK[t] + r:TOK[t] + P], yacc[r:P, t, :]).then_inc(y_out, 16)
            pool.wait_ge(y_out, 48)
            pool.wait_ge(h_out, 16 * DEPTH)
            pool.wait_ge(kv_out, 32 * DEPTH)
            pool.wait_ge(tail_a_out, 16 * DEPTH)
            pool.wait_ge(tail_b_out, 16 * DEPTH)
            nv = pool.value_load(nvi[0:1, 0:1], min_val=NE, max_val=2 * NE)
            for s in range(E_SLOTS):
                pool.wait_ge(slot_full[s], nv * (16 * plan.per_slot) + 16 * (stream_loads[s] + 1))

        @block.scalar
        def _(act):
            def ident_bias(out, in_, bias):
                return act.activation(out, in_, ACT.Identity, bias=bias)

            queue = list(plan.split)

            def split_for(step):
                while queue and near(queue[0], step):
                    make_hi(act, queue.pop(0))

            make_hi(act, queue.pop(0))
            act.wait_ge(xt_in, 16)
            for k in range(KT):
                act.copy(xTh[:, k], cb[:, k]).then_inc(xth_ready, 1)
            split_for(tile_of(0, "za", 0).done)
            act.wait_ge(spl_ask, 1)
            act.activation(lamw[:, 1], lamw[:, 0], ACT.Exp).then_inc(spl_exp, 1)

            def scaled(out, l, name, ln, k):
                return act.activation(out, bank(l, name, k)[:, 0:T], ACT.Identity, scale=col(l, ln + "_g", k),
                                      bias=col(l, ln + "_b", k))

            def made(*key):
                split_for(tile_of(*key).done)
                filled(act, *key)

            for l in range(DEPTH):
                for n in range(JA):
                    if n == 3:
                        for m, u in enumerate(mem_units[2 * l:2 * l + 2]):
                            slot_wait(act, u)
                            act.copy(memh[:, 4 * m:4 * m + 4].rearrange("p a b -> p (a b)"), ring[:, u % SLOTS, :])\
                                .then_inc(memh_ready, 1)
                    made(l, "za", 2 * n + 1)
                    frees(act.activation(sg[:, n], bank(l, "za", 2 * n + 1)[:, 0:T], ACT.Sigmoid,
                                         bias=col(l, "b_in", ZA_G + n)), l, "za", 2 * n + 1)
                split_for(tile_of(l, "q", 0).done)
                act.wait_ge(hist_ready, HIST * l + 1 + JB + 2)
                for n in range(JC):
                    made(l, "q", n)
                    b = col(l, "b_in", ZQ + n)
                    ident_bias(qpad[:, :, 40 * n:40 * n + DSEQ], samp(bank(l, "q", n)[:, SEQ:T]), b)
                    frees(ident_bias(qT[:, n], bank(l, "q", n)[:, 0:T], b), l, "q", n)
                for n in range(H_C):
                    made(l, "k", n)
                    frees(act.copy(kT[:, n], bank(l, "k", n)[:, 0:N_MEM]), l, "k", n)
                for n in range(2):
                    made(l, "v", n)
                    frees(act.copy(vm[:, n], bank(l, "v", n)), l, "v", n)
                def exponentials(n):
                    key = (l, "ps", n) if n < 8 else (l, "ss", n - 8)
                    split_for(tile_of(*key).done)
                    act.wait_ge(negmax, 10 * l + n + 1)
                    frees(act.activation(pp[:, n], bank(*key)[:, 0:N_MEM], ACT.Exp, bias=stat[:, 20 + n:21 + n],
                                         scale=QSCALE, accum_out=stat[:, 30 + n:31 + n]), *key)

                for n in range(8):
                    exponentials(n)
                for n in range(JB):
                    if n == 6:
                        exponentials(8)
                    made(l, "zb", n)
                    b = col(l, "b_in", ZB + n)
                    ident_bias(zb[:, n, K_B - 1:K_B - 1 + SEQ], bank(l, "zb", n)[:, 0:SEQ], b)
                    frees(ident_bias(seg_b(n, K_B - 1, DSEQ), samp(bank(l, "zb", n)[:, SEQ:T]), b), l, "zb", n)
                act.wait_ge(hist_ready, HIST * (l + 1))
                for n in range(JB):
                    if n == 2:
                        exponentials(9)
                    made(l, "zg", n)
                    frees(act.activation(gg[:, n], bank(l, "zg", n)[:, 0:T], ACT.Gelu_apprx_tanh,
                                         bias=col(l, "b_in", ZG + n)), l, "zg", n)
                for n in range(H_C + 1):
                    made(l, "pt", n)
                    frees(act.copy(pT[:, n], bank(l, "pt", n)), l, "pt", n)
                def gates_of(br, n, before):
                    made(l, "g", br, n)
                    if before:
                        emptied(act, l, before, n)
                    frees(act.activation(gz[:, n], bank(l, "g", br, n)[:, 0:T], ACT.Sigmoid,
                                         bias=col(l, "b_in", ZM + KT * br + n)), l, "g", br, n)

                split_for(tile_of(l, "g", 2, 0).done)
                act.wait_ge(kv_out, 32 * (l + 1))
                for n in range(KT):
                    gates_of(2, n, None)
                for n in range(H_C):
                    made(l, "o", n)
                    act.copy(oTh[:, n], bank(l, "o", n)[:, 0:T]).then_inc(oh_ready, 1)
                made(l, "var", 0)
                frees(act.activation(dev, bank(l, "var", 0)[:, 0:T], ACT.Sqrt, scale=1.0 / D_A,
                                     bias=eps_c[:, 0:1]), l, "var", 0)
                split_for(tile_of(l, "yc", 1).done)
                act.wait_ge(lna_norm, l + 1)
                for n in range(JA):
                    act.activation(sg[:, n], ca[:, n], ACT.Sigmoid, scale=col(l, "ln_a_g", n),
                                   bias=col(l, "ln_a_b", n)).then_inc(lna_sig, 1)
                split_for(tile_of(l, "yc", 3).done)
                for n in range(JA):
                    act.wait_ge(lna_done, JA * l + n + 1)
                    act.copy(sah[:, n], sa[:, n]).then_inc(sah_ready, 1)
                split_for(tile_of(l, "yc", KT - 1).done)
                act.wait_ge(spl_ready, 1)
                act.wait_ge(meml_ready, 2 * (l + 1))
                for n in range(JB):
                    made(l, "rg", n)
                    frees(act.activation(rr[:, n], bank(l, "rg", n)[:, 0:T], ACT.Sigmoid,
                                         bias=col(l, "b_rg_a", n)), l, "rg", n)
                act.wait_ge(conv_a_tap, K_A * (l + 1))
                act.wait_ge(tails_ready, 2 * (JA + JB) * (l + 1))
                for n in range(JB):
                    made(l, "rg", JB + n)
                    frees(act.activation(ig[:, n], bank(l, "rg", JB + n)[:, 0:T], ACT.Sigmoid,
                                         bias=col(l, "b_rg_x", n)), l, "rg", JB + n)
                for n in range(JB):
                    emptied(act, l, "rg", n)
                    act.activation(aa[:, n], rr[:, n], ACT.Exp,
                                   scale=spl[:, JB * l + n:JB * l + n + 1]).then_inc(a_ready, 1)
                for n in range(KT):
                    gates_of(0, n, "yc")
                    for m in range(2 * n, min(2 * n + 2, JB)):
                        act.wait_ge(a_ready, JB * l + m + 1)
                        act.activation(rr[:, m], rr[:, m], ACT.Tanh,
                                       scale=spl[:, JB * l + m:JB * l + m + 1]).then_inc(tanh_done, 1)
                    if n == 5:
                        act.wait_ge(a2_ready, l + 1)
                        act.activation(rr, rr, ACT.Sqrt, scale=-1.0).then_inc(root_ready, 1)
                split_for(tile_of(l, "ya", 3).done)
                for n in range(JB):
                    act.wait_ge(hg_ready, JB * l + n + 1)
                    act.copy(hgh[:, n], gg[:, n]).then_inc(hgh_ready, 1)
                for n in range(KT):
                    gates_of(1, n, "ya")
                for n in range(KT):
                    split_for(tile_of(l, "yb", n).done)
                    act.wait_ge(mg_ready, KT * l + n + 1)
                    act.copy(mgh[:, n], mg[:, n]).then_inc(mgh_ready, 1)
                split_for(tile_of(l, "mix", 0).done)
                layer_norm_std(act, 2 * l)
                if l % 2 == 0:
                    split_for(tile_of(l, "xt", 0).done)
                    for k in range(KT):
                        emptied(act, l, "xt", k)
                        act.copy(xTh[:, k], xaff[:, k % 3]).then_inc(xth_ready, 1)
                    for f in range(FT):
                        split_for(tile_of(l, "g", f).done)
                        filled(act, l, "g", f)
                        if f >= 2:
                            emptied(act, l, "g", f - 2)
                        act.activation(dsig[:, f % 2], bank(l, "g", f)[:, 0:T], ACT.Sigmoid).then_inc(dsig_ready, 1)
                        if f:
                            split_for(tile_of(l, "u", f - 1).done)
                            emptied(act, l, "u", f - 1)
                            act.copy(hTh[:, f - 1], dh[:, (f - 1) % 2]).then_inc(dhh_ready, 1)
                    split_for(tile_of(l, "u", FT - 1).done)
                    emptied(act, l, "u", FT - 1)
                    act.copy(hTh[:, FT - 1], dh[:, (FT - 1) % 2]).then_inc(dhh_ready, 1)
                    split_for(tile_of(l, "down", 0).done)
                    layer_norm_std(act, 2 * l + 1)
                    for k in range(KT):
                        emptied(act, l, "xt2", k)
                        act.copy(xTh[:, k], xaff[:, k % 3]).then_inc(xth_ready, 1)
                else:
                    for k in range(KT):
                        filled(act, l, "xt", k)
                        frees(scaled(xT[:, k], l, "xt", "ln1", k), l, "xt", k)
            filled(act, "router")
            frees(act.copy(lgT[0:NE], bank("router")[0:NE, 0:T]), "router")
            act.wait_ge(top_ready, 1)
            act.activation(gate2[:, :, 1], gate2[:, :, 0], ACT.Exp).then_inc(exp_ready, 1)
            for n in range(4):
                filled(act, "gather0", n)
                frees(act.copy(pair(xe, n), bank_pair("gather0", n)), "gather0", n)

            def turn(i, cap):
                for f in range(FT // 2):
                    filled(act, "e", "g", f, i=i)
                    if f >= 2:
                        emptied(act, "e", "g", f - 2, i=i)
                    act.activation(pair(esig, f % 2, cap), bank_pair("e", "g", f, cap=cap), ACT.Sigmoid)\
                        .then_inc(esig_ready, 1)
                for n in range(4):
                    filled(act, "e", "gather", n, i=i)
                    frees(act.copy(pair(xe, n), bank_pair("e", "gather", n)), "e", "gather", n)
                for n in range(4):
                    filled(act, "e", "down", n, i=i)
                    frees(act.copy(pair(ye, n, cap), bank_pair("e", "down", n, cap=cap)), "e", "down", n)
                for n in range(4):
                    filled(act, "e", "yt", n, i=i)
                    r, g, c, w = yt_place(n, cap)
                    frees(act.copy(ys[0:r, g, c:c + w], bank("e", "yt", n)[0:r, 0:w]), "e", "yt", n)

            turns(act, turn)
            layer_norm_std(act, 2 * DEPTH - 1)

        @block.vector
        def _(dve):
            steps = [0]

            def link(ins):
                steps[0] += 1
                ins.then_inc(dve_step, 1)
                dve.wait_ge(dve_step, steps[0])

            def mac(out, in0, scalar, in1):
                return dve.scalar_tensor_tensor(out=out, in0=in0, scalar=scalar, in1=in1, op0=ALU.mult, op1=ALU.add)

            def over(v, n):
                return v.unsqueeze(1).to_broadcast([P, n, v.shape[-1]])

            def normalise(n, v):
                for t in TURN:
                    for c in range(2):
                        dve.bn_stats(stats[:, t, c], v[:, t, 512 * c:512 * c + 512]).then_inc(bn_done, 1)
                for m, t in enumerate(TURN):
                    dve.wait_ge(bn_done, 6 * n + 2 * m + 2)
                    dve.bn_aggr(mv[:, t, 0:2], stats[:, t]).then_inc(var_ready, 1)
                for m, t in enumerate(TURN):
                    dve.wait_ge(std_ready, 3 * n + m + 1)
                    link(dve.reciprocal(mv[:, t, 2:3], mv[:, t, 2:3]))
                    dve.tensor_scalar(v[:, t, :], v[:, t, :], mv[:, t, 0:1], mv[:, t, 2:3],
                                      ALU.subtract, ALU.mult).then_inc(xn_ready, 1)

            def gain_bias(n, v):
                dve.wait_ge(xn_ready, 3 * (n + 1))
                dve.wait_ge(ln_in, 16 * (n + 1))
                for t in range(4):
                    if t < 3:
                        dve.tensor_tensor(v[:, t, :], v[:, t, :], lnp[:, 0, :], ALU.mult).then_inc(xg_ready, 1)
                    if t:
                        dve.wait_ge(xg_ready, 3 * n + t)
                        dve.tensor_tensor(v[:, t - 1, :], v[:, t - 1, :], lnp[:, 1, :], ALU.add)\
                           .then_inc(x_ready, 1)
                dve.wait_ge(x_ready, 3 * (n + 1))

            def turned_lo(l, name, ln, first):
                def low(k):
                    dve.wait_ge(xth_ready, first + k + 1)
                    dve.tensor_tensor(xTl[:, k], xaff[:, k % 3], xTh[:, k].bitcast(F32), ALU.subtract)\
                       .then_inc(xtl_ready, 1)

                for k in range(KT):
                    filled(dve, l, name, k)
                    if k >= 3:
                        dve.wait_ge(xtl_ready, first + k - 2)
                    frees(dve.tensor_scalar(xaff[:, k % 3], bank(l, name, k)[:, 0:T], col(l, ln + "_g", k),
                                            col(l, ln + "_b", k), ALU.mult, ALU.add), l, name, k)
                    if k >= 1:
                        low(k - 1)
                low(KT - 1)

            def residual(l, name):
                for t in TURN:
                    for c in range(2):
                        n = 2 * t + c
                        filled(dve, l, name, n)
                        frees(dve.scalar_tensor_tensor(out=x[:, t, 512 * c:512 * c + 512],
                                                       in0=x[:, t, 512 * c:512 * c + 512], scalar=ALPHA,
                                                       in1=bank(l, name, n), op0=ALU.mult, op1=ALU.add), l, name, n)
                for n in range(6):
                    emptied(dve, l, name, n)

            def hidden_lo(f):
                dve.wait_ge(dhh_ready, f + 1)
                dve.tensor_tensor(hTl[:, f], dh[:, f % 2], hTh[:, f].bitcast(F32), ALU.subtract)\
                   .then_inc(dhl_ready, 1)

            for k in range(KT):
                dve.wait_ge(xth_ready, k + 1)
                dve.tensor_tensor(xTl[:, k], cb[:, k], xTh[:, k].bitcast(F32), ALU.subtract).then_inc(xtl_ready, 1)
            dve.memset(eps_c[:], EPS).then_inc(eps_ready, 1)
            dve.wait_ge(par_in, 16)
            lam = par[:, :, COL["lam"]:COL["lam"] + JB]
            link(dve.tensor_scalar(lamw[:, 2], lam, -1.0, None, ALU.mult))
            dve.tensor_tensor(lamw[:, 0], lam, lamw[:, 2], ALU.min).then_inc(spl_ask, 1)
            dve.wait_ge(spl_exp, 1)
            link(dve.tensor_scalar(lamw[:, 0], lamw[:, 1], 2.0, None, ALU.add))
            link(dve.reciprocal(lamw[:, 0], lamw[:, 0]))
            link(dve.tensor_tensor(lamw[:, 0], lamw[:, 0], lamw[:, 1], ALU.mult))
            link(dve.tensor_tensor(lamw[:, 3], lamw[:, 0], lamw[:, 0], ALU.mult))
            link(dve.tensor_scalar(lamw[:, 4], lamw[:, 3], 1.0 / 17, 1.0 / 15, ALU.mult, ALU.add))
            for k in (13, 11, 9, 7, 5, 3, 1):
                link(dve.tensor_tensor(lamw[:, 4], lamw[:, 4], lamw[:, 3], ALU.mult))
                link(dve.tensor_scalar(lamw[:, 4], lamw[:, 4], 1.0 / k, None, ALU.add))
            link(dve.tensor_tensor(lamw[:, 4], lamw[:, 4], lamw[:, 0], ALU.mult))
            link(dve.tensor_scalar(lamw[:, 4], lamw[:, 4], 2.0, None, ALU.mult))
            link(dve.tensor_scalar(lamw[:, 2], lamw[:, 2], 0.0, None, ALU.max))
            link(dve.tensor_tensor(lamw[:, 4], lamw[:, 4], lamw[:, 2], ALU.add))
            dve.tensor_scalar(spl[:].rearrange("p (l j) -> p l j", l=DEPTH), lamw[:, 4], -8.0, None, ALU.mult)\
               .then_inc(spl_ready, 1)

            for l in range(DEPTH):
                def conv_b(j0):
                    for j in (j0, j0 + 1):
                        emptied(dve, l, "zb", j)
                    for k in range(K_B):
                        for j in (j0, j0 + 1):
                            w = col(l, "w_conv_b", K_B * j + k)
                            for out, in_ in ((cb[:, j, 0:SEQ], zb[:, j, k:k + SEQ]),
                                             (samp(cb[:, j, SEQ:T]), seg_b(j, k, DSEQ))):
                                if k == 0:
                                    ins = dve.tensor_scalar(out, in_, w, col(l, "b_conv_b", j), ALU.mult, ALU.add)
                                else:
                                    ins = mac(out, in_, w, out)
                        if k < K_B - 1:
                            link(ins)
                        else:
                            ins.then_inc(conv_b_done, 1)

                dve.wait_ge(hist_ready, HIST * (l + 1))
                for j in range(JA):
                    if j == 3:
                        for n, u in enumerate(mem_units[2 * l:2 * l + 2]):
                            dve.wait_ge(memh_ready, 2 * l + n + 1)
                            dve.tensor_tensor(meml[:, 4 * n:4 * n + 4].rearrange("p a b -> p (a b)"),
                                              ring[:, u % SLOTS, :],
                                              memh[:, 4 * n:4 * n + 4].rearrange("p a b -> p (a b)").bitcast(F32),
                                              ALU.subtract).then_inc(meml_ready, 1)
                    filled(dve, l, "za", 2 * j)
                    emptied(dve, l, "za", 2 * j + 1)
                    b = col(l, "b_in", ZA_U + j)
                    z = bank(l, "za", 2 * j)
                    dve.scalar_tensor_tensor(out=ua[:, j, K_A - 1:K_A - 1 + SEQ], in0=z[:, 0:SEQ], scalar=b,
                                             in1=sg[:, j, 0:SEQ], op0=ALU.add, op1=ALU.mult).then_inc(glu_done, 1)
                    dve.wait_ge(glu_done, 2 * (JA * l + j) + 1)
                    dve.scalar_tensor_tensor(out=seg_a(j, K_A - 1, DSEQ), in0=samp(z[:, SEQ:T]), scalar=b,
                                             in1=samp(sg[:, j, SEQ:T]), op0=ALU.add, op1=ALU.mult)\
                       .then_inc(glu_done, 1)
                    dve.wait_ge(glu_done, 2 * (JA * l + j + 1))
                    frees(dve.tensor_scalar(ca[:, j, 0:SEQ], ua[:, j, 0:SEQ], col(l, "w_conv_a", K_A * j),
                                            col(l, "b_conv_a", j), ALU.mult, ALU.add), l, "za", 2 * j)
                    ins = dve.tensor_scalar(samp(ca[:, j, SEQ:T]), seg_a(j, 0, DSEQ), col(l, "w_conv_a", K_A * j),
                                            col(l, "b_conv_a", j), ALU.mult, ALU.add)
                ins.then_inc(conv_a_tap, 1)
                for k in range(1, K_A):
                    if k in MAX_TAPS:
                        for n in MAX_TAPS[k]:
                            key = (l, "ps", n) if n < 8 else (l, "ss", n - 8)
                            filled(dve, *key)
                            link(dve.reduce_max(stat[:, 10 + n:11 + n], bank(*key)[:, 0:N_MEM], AX.X))
                            dve.tensor_scalar(stat[:, 20 + n:21 + n], stat[:, 10 + n:11 + n], -QSCALE, None,
                                              ALU.mult).then_inc(negmax, 1)
                    if k == PROBS_TAP:
                        for n in range(2, 10):
                            emptied(dve, *((l, "ps", n) if n < 8 else (l, "ss", n - 8)))
                        link(dve.reciprocal(stat[:, 40:50], stat[:, 30:40]))
                        for n in range(10):
                            dve.tensor_scalar(pp[:, n], pp[:, n], stat[:, 40 + n:41 + n], None, ALU.mult)\
                               .then_inc(probs, 1)
                    dve.wait_ge(conv_a_tap, K_A * l + k)
                    for j in range(JA):
                        w = col(l, "w_conv_a", K_A * j + k)
                        mac(ca[:, j, 0:SEQ], ua[:, j, k:k + SEQ], w, ca[:, j, 0:SEQ])
                        ins = mac(samp(ca[:, j, SEQ:T]), seg_a(j, k, DSEQ), w, samp(ca[:, j, SEQ:T]))
                    ins.then_inc(conv_a_tap, 1)
                conv_b(0)
                conv_b(2)
                filled(dve, l, "mean", 0)
                dve.wait_ge(conv_a_tap, K_A * (l + 1))
                frees(mac(ca[:], over(bank(l, "mean", 0)[:, 0:T], JA), -1.0 / D_A, ca[:]), l, "mean", 0)
                emptied(dve, l, "mean", 0)
                dve.tensor_tensor(sg[:], ca[:], ca[:], ALU.mult).then_inc(dev_ready, 1)
                conv_b(4)
                conv_b(6)
                for n in range(H_C):
                    dve.wait_ge(oh_ready, H_C * l + n + 1)
                    frees(dve.tensor_tensor(oTl[:, n], bank(l, "o", n)[:, 0:T], oTh[:, n].bitcast(F32),
                                            ALU.subtract), l, "o", n)
                emptied(dve, l, "var", 0)
                link(dve.reciprocal(dev, dev))
                dve.tensor_tensor(ca[:], ca[:], over(dev, JA), ALU.mult).then_inc(lna_norm, 1)
                dve.wait_ge(lna_norm, l + 1)
                dve.wait_ge(tail_a_out, 16 * (l + 1))
                for j in range(JA):
                    dve.tensor_scalar(sa[:, j], ca[:, j], col(l, "ln_a_g", j), col(l, "ln_a_b", j),
                                      ALU.mult, ALU.add).then_inc(sa_lin, 1)
                for j in range(JA):
                    dve.wait_ge(sa_lin, JA * l + j + 1)
                    dve.wait_ge(lna_sig, JA * l + j + 1)
                    dve.tensor_tensor(sa[:, j], sa[:, j], sg[:, j], ALU.mult).then_inc(lna_done, 1)
                for j in range(JA):
                    dve.wait_ge(sah_ready, JA * l + j + 1)
                    dve.wait_ge(lna_done, JA * l + j + 1)
                    dve.tensor_tensor(sal[:, j], sa[:, j], sah[:, j].bitcast(F32), ALU.subtract)\
                       .then_inc(sal_ready, 1)
                for n in range(KT):
                    filled(dve, l, "yc", n)
                    emptied(dve, l, "g", 2, n)
                    frees(dve.tensor_tensor(mg[:, n], bank(l, "yc", n)[:, 0:T], gz[:, n], ALU.mult), l, "yc", n)

                def add_gated(br, yk, n, done):
                    filled(dve, l, yk, n)
                    emptied(dve, l, "g", br, n)
                    frees(dve.tensor_tensor(part[:, n % 2], bank(l, yk, n)[:, 0:T], gz[:, n], ALU.mult), l, yk, n)
                    emptied(dve, l, yk, n)
                    dve.tensor_tensor(mg[:, n], mg[:, n], part[:, n % 2], ALU.add).then_inc(done, 1)

                dve.wait_ge(a_ready, JB * (l + 1))
                link(dve.tensor_tensor(w_b, aa, aa, ALU.mult))
                dve.wait_ge(tanh_done, JB * (l + 1))
                for half in range(2):
                    h = slice(4 * half, 4 * half + 4)
                    ins = dve.scalar_tensor_tensor(out=rr[:, h], in0=w_b[:, h], scalar=1.0, in1=rr[:, h],
                                                   op0=ALU.add, op1=ALU.mult)
                ins.then_inc(a2_ready, 1)
                for n in range(JB):
                    emptied(dve, l, "rg", JB + n)
                link(dve.tensor_tensor(ig, ig, cb, ALU.mult))
                dve.wait_ge(root_ready, l + 1)
                link(dve.tensor_tensor(ig, ig, rr, ALU.mult))
                first = slice(SEQ, T, DSEQ)
                link(dve.tensor_tensor(h0[:], h0[:], aa[:, :, first], ALU.mult))
                link(dve.tensor_tensor(ig[:, :, first], ig[:, :, first], h0[:], ALU.add))
                dve.memset(aa[:, :, first], 0.0)
                link(dve.memset(aa[:, :, 0:1], 0.0))
                dve.tensor_tensor_scan(cb.rearrange("p a b -> p (a b)"), aa.rearrange("p a b -> p (a b)"),
                                       ig_flat, 0.0, ALU.mult, ALU.add).then_inc(h_ready, 1)
                dve.wait_ge(h_ready, l + 1)
                for n in range(JB):
                    dve.tensor_tensor(gg[:, n], gg[:, n], cb[:, n], ALU.mult).then_inc(hg_ready, 1)
                for n in range(JB):
                    dve.wait_ge(hgh_ready, JB * l + n + 1)
                    dve.wait_ge(hg_ready, JB * l + n + 1)
                    dve.tensor_tensor(hgl[:, n], gg[:, n], hgh[:, n].bitcast(F32), ALU.subtract)\
                       .then_inc(hgl_ready, 1)
                for n in range(KT):
                    add_gated(0, "ya", n, mg_part)
                dve.wait_ge(mg_part, KT * (l + 1))

                def merged_lo(n):
                    dve.wait_ge(mgh_ready, KT * l + n + 1)
                    dve.wait_ge(mg_ready, KT * l + n + 1)
                    dve.tensor_tensor(mgl[:, n], mg[:, n], mgh[:, n].bitcast(F32), ALU.subtract)\
                       .then_inc(mgl_ready, 1)

                for n in range(KT):
                    add_gated(1, "yb", n, mg_ready)
                    if n:
                        merged_lo(n - 1)
                merged_lo(KT - 1)
                if l == 0:
                    dve.wait_ge(x_in, 16 * len(TOK))
                residual(l, "mix")
                dve.wait_ge(kv_out, 32 * (l + 1))
                dve.wait_ge(h_out, 16 * (l + 1))
                normalise(2 * l, x)
                if l % 2 == 0:
                    turned_lo(l, "xt", "ln1", KT)
                    gain_bias(2 * l, x)
                    for f in range(FT):
                        dve.wait_ge(dsig_ready, f + 1)
                        frees(dve.tensor_tensor(dlin[:, f % 2], bank(l, "g", f)[:, 0:T], dsig[:, f % 2], ALU.mult),
                              l, "g", f)
                        emptied(dve, l, "g", f)
                        filled(dve, l, "u", f)
                        if f >= 2:
                            dve.wait_ge(dhl_ready, f - 1)
                        frees(dve.tensor_tensor(dh[:, f % 2], bank(l, "u", f)[:, 0:T], dlin[:, f % 2], ALU.mult),
                              l, "u", f)
                        emptied(dve, l, "u", f)
                        if f:
                            hidden_lo(f - 1)
                    hidden_lo(FT - 1)
                    residual(l, "down")
                    normalise(2 * l + 1, x)
                    turned_lo(l, "xt2", "ln2", 2 * KT)
                    gain_bias(2 * l + 1, x)

            for k in range(KT):
                filled(dve, DEPTH - 1, "xt", k)
            gain_bias(2 * DEPTH - 2, x)
            dve.memset(slot[:], -1.0).then_inc(lg_zero, 1)
            dve.wait_ge(lg_zero, 1)
            dve.wait_ge(router_in, 32)
            filled(dve, "logits")
            for t in range(3):
                ins = dve.tensor_tensor(lg[:, t, :], bank("logits")[:, NE * t:NE * t + NE], brow, ALU.add)
            frees(ins, "logits")
            emptied(dve, "logits")
            for t in range(3):
                ins = dve.max(top[:, t, :], lg[:, t, :])
            link(ins)
            for t in range(3):
                ins = dve.max_index(topi[:, t, :], top[:, t, :], lg[:, t, :])
            link(ins)
            dve.tensor_copy(topf[:], topi[:, :, 0:2]).then_inc(lg_zero, 1)
            dve.tensor_tensor(gate2[:, :, 0:1], top[:, :, 1:2], top[:, :, 0:1], ALU.subtract).then_inc(top_ready, 1)
            dve.wait_ge(lg_zero, 2)
            lanes = over(iota[:, 0:NE], 3)
            dve.tensor_tensor(m1[:], lanes, topf[:, :, 0:1].to_broadcast([P, 3, NE]), ALU.is_equal)
            link(dve.tensor_tensor(m2[:], lanes, topf[:, :, 1:2].to_broadcast([P, 3, NE]), ALU.is_equal))
            link(dve.tensor_tensor(hit[:], m1[:], m2[:], ALU.add))
            dve.memset(hit[0:DUP, 2, :], 0.0).then_inc(hit_ready, 1)
            dve.wait_ge(exp_ready, 1)
            link(dve.tensor_scalar(den[:], gate2[:, :, 1], 1.0, None, ALU.add))
            link(dve.reciprocal(gate2[:, :, 0], den[:]))
            link(dve.tensor_tensor(gate2[:, :, 1], gate2[:, :, 1], gate2[:, :, 0], ALU.mult))
            dve.tensor_tensor(m1[:], m1[:], gate2[:, :, 0:1].to_broadcast([P, 3, NE]), ALU.mult)
            link(dve.tensor_tensor(m2[:], m2[:], gate2[:, :, 1:2].to_broadcast([P, 3, NE]), ALU.mult))
            for r in range(2):
                ins = dve.tensor_tensor(gates[:, :, NE * r:NE * r + NE], m1[:], m2[:], ALU.add)
            link(ins)
            filled(dve, "pos")
            for t in range(3):
                dve.tensor_scalar(m1[:, t, :], bank("pos")[:, NE * t:NE * t + NE], 1.0, None, ALU.add)\
                   .then_inc(pos_read, 1)
            link(dve.tensor_copy(count[:], bank("pos")[:, 3 * NE:4 * NE]))
            frees(dve.reduce_max(nmax[:, 0:1], bank("pos")[:, 3 * NE:4 * NE], AX.X), "pos")
            dve.wait_ge(pos_read, 3)
            emptied(dve, "pos")
            dve.wait_ge(hit_ready, 1)
            for r in range(2):
                dve.tensor_scalar(m2[:, 0, :], count[:], float(SIZES[0] + CAP * r), None, ALU.is_gt)
                link(dve.tensor_scalar(m2[:, 1, :], count[:], float(SIZES[1] + CAP * r), None, ALU.is_gt))
                link(dve.tensor_tensor(size[:, NE * r:NE * r + NE], m2[:, 0, :], m2[:, 1, :], ALU.add))
            link(dve.tensor_scalar(nmax[:, 1:2], nmax[:, 0:1], float(CAP), float(NE), ALU.is_gt, ALU.mult))
            dve.tensor_scalar(nvi[:], nmax[:, 1:2], float(NE), None, ALU.add).then_inc(nv_ready, 1)
            for t in range(3):
                ins = dve.tensor_tensor(m1[:, t, :], m1[:, t, :], hit[:, t, :], ALU.mult)
            link(ins)
            for t in range(3):
                dve.tensor_scalar(slot[:, t, 0:NE], m1[:, t, :], -1.0, None, ALU.add)
                ins = dve.tensor_scalar(slot[:, t, NE:2 * NE], m1[:, t, :], -1.0 - CAP, None, ALU.add)
            link(ins)
            for t in range(3):
                dve.tensor_scalar(pick[:, t, :], iota[:, :], slot[:, t, 0:1], None, ALU.is_equal)\
                   .then_inc(pick_ready, 1)

            for t in range(3):
                dve.tensor_scalar(yacc[:, t, :], x[:, t, :], ALPHA, None, ALU.mult).then_inc(yacc_ready, 1)
            dve.wait_ge(yacc_ready, 3)

            def turn(i, cap):
                for f in range(FT // 2):
                    dve.wait_ge(esig_ready, i * (FT // 2) + (f + 1))
                    frees(dve.tensor_tensor(pair(elin, f % 2, cap), bank_pair("e", "g", f, cap=cap),
                                            pair(esig, f % 2, cap), ALU.mult), "e", "g", f)
                    emptied(dve, "e", "g", f, i=i)
                    filled(dve, "e", "u", f, i=i)
                    frees(dve.tensor_tensor(pair(he, f, cap), bank_pair("e", "u", f, cap=cap),
                                            pair(elin, f % 2, cap), ALU.mult), "e", "u", f)
                    if f == 0:
                        for n in range(2):
                            filled(dve, "e", "pt", n, i=i)
                            r, g, c, w = pt_place(n, cap)
                            frees(dve.tensor_copy(pg[0:r, g, c:c + w], bank("e", "pt", n)[0:r, c:c + w]),
                                  "e", "pt", n)
                        for t in range(3):
                            dve.tensor_scalar(pick[:, t, :], iota[:], slot[:, t, bass.ds(i + 1, 1)], None,
                                              ALU.is_equal).then_inc(pick_ready, 1)
                for n in range(len(Y_TILES) - BANKS, len(Y_TILES)):
                    emptied_before(dve, "e", "y", n, i=i)
                for n, (t, c, w) in enumerate(Y_TILES):
                    filled(dve, "e", "y", n, i=i)
                    frees(dve.scalar_tensor_tensor(out=yacc[:, t, c:c + w], in0=bank("e", "y", n)[:, 0:w],
                                                   scalar=gates[:, t, bass.ds(i, 1)], in1=yacc[:, t, c:c + w],
                                                   op0=ALU.mult, op1=ALU.add), "e", "y", n)

            nv = turns(dve, turn)
            for n in range(len(Y_TILES) - BANKS, len(Y_TILES)):
                emptied_before(dve, "e", "y", n, i=nv)
            normalise(2 * DEPTH - 1, yacc)
            gain_bias(2 * DEPTH - 1, yacc)

        @block.tensor
        def _(pe):
            def product(out, lhs, rhs, k, n, **kw):
                return pe.matmul(out, lhs, rhs, start=(k == 0), stop=(k == n - 1), **kw)

            def step(ins):
                ins.then_inc(mm_done, 1)

            def blocks(key, hi, lo, width, kt=KT, unit=None, turned=None):
                h, low = (v.rearrange("p (k n) -> p k n", n=P) for v in (unit or parts(pe, *key)))
                take(pe, *key)
                for k in range(kt):
                    if turned is not None:
                        pe.wait_ge(xtl_ready, turned + k + 1)
                    out = bank(*key)[:, 0:width]
                    pe.matmul(out, h[:, k], hi[:, k], start=(k == 0), stop=False)
                    pe.matmul(out, h[:, k], lo[:, k], start=False, stop=False)
                    ins = pe.matmul(out, low[:, k], hi[:, k], start=False, stop=(k == kt - 1))
                step(ins)

            def rows_of(key, k, nk, hi, lo, tiles=6):
                h, low = parts(pe, *key)
                if k == 0:
                    for n in range(tiles):
                        take(pe, key[0], key[1], n)
                for t in TURN:
                    r0 = TOK[t]
                    for c in range(2):
                        out, cs = bank(key[0], key[1], 2 * t + c), slice(512 * c, 512 * c + 512)
                        pe.matmul(out, hi[:, r0:r0 + P], h[:, cs], start=(k == 0), stop=False)
                        pe.matmul(out, hi[:, r0:r0 + P], low[:, cs], start=False, stop=False)
                        ins = pe.matmul(out, lo[:, r0:r0 + P], h[:, cs], start=False, stop=(k == nk - 1))
                    if k == nk - 1 or t == TURN[-1]:
                        step(ins)

            def turn_x(l, name, n):
                for m, t in enumerate(TURN):
                    pe.wait_ge(xn_ready, 3 * (n - 1) + m + 1)
                    for k in range(KT):
                        if m == 0:
                            take(pe, l, name, k)
                        ins = pe.transpose(bank(l, name, k)[:, TOK[t]:TOK[t] + P], x[:, t, P * k:P * k + P],
                                           ident[:])
                        if m == 2:
                            step(ins)

            pe.wait_ge(const_ready, 3)
            for l in range(DEPTH):
                for n in range(2 * JA):
                    blocks((l, "za", n), xTh, xTl, T, turned=2 * KT * l if n == 0 else None)
                for n in range(JC):
                    blocks((l, "q", n), xTh, xTl, T)
                pe.wait_ge(meml_ready, 2 * (l + 1))
                for n in range(H_C):
                    blocks((l, "k", n), memh, meml, N_MEM)
                for c in range(4):
                    h, low = parts(pe, l, "v", c)
                    for m in range(2):
                        if c == 0:
                            take(pe, l, "v", m)
                        for k in (2 * c, 2 * c + 1):
                            out, cs = bank(l, "v", m), slice(512 * (k % 2), 512 * (k % 2) + 512)
                            ms = slice(P * m, P * m + P)
                            pe.matmul(out, memh[:, k, ms], h[:, cs], start=(k == 0), stop=False)
                            pe.matmul(out, memh[:, k, ms], low[:, cs], start=False, stop=False)
                            ins = pe.matmul(out, meml[:, k, ms], h[:, cs], start=False, stop=(k == KT - 1))
                    step(ins)
                for n in range(JC):
                    emptied(pe, l, "q", n)
                    emptied(pe, l, "k", n)
                for n in range(8):
                    h, t = n // 2, n % 2
                    take(pe, l, "ps", n)
                    step(pe.matmul(bank(l, "ps", n)[:, 0:N_MEM], qT[:, h, P * t:P * t + P], kT[:, h],
                                   start=True, stop=True))
                for b in range(DEC):
                    blocks((l, "zb", b), xTh, xTl, T)
                    w = weights(pe, l, "ck", b)
                    if b % 4 == 0:
                        take(pe, l, "ss", b // 4)
                    for h in range(H_C):
                        ins = product(bank(l, "ss", b // 4)[32 * (b % 4):32 * (b % 4) + 32, 0:N_MEM],
                                      qpad[:, b, 32 * h:32 * h + 32], w[:, N_MEM * h:N_MEM * h + N_MEM], h, H_C)
                    step(ins)
                for n in range(JB):
                    blocks((l, "zg", n), xTh, xTl, T)
                for n in range(H_C + 1):
                    take(pe, l, "pt", n)
                    pe.wait_ge(probs, 10 * l + 2 * n + 2)
                    for m in range(2):
                        for t in range(2):
                            c = 2 * P * m + P * t
                            ins = pe.transpose(bank(l, "pt", n)[:, c:c + P], pp[:, 2 * n + t, P * m:P * m + P],
                                               ident[:])
                    step(ins)
                for n in range(H_C + 1):
                    emptied(pe, l, "pt", n)
                for m in range(2):
                    emptied(pe, l, "v", m)
                def attend(b):
                    w = weights(pe, l, "cv", b).rearrange("p (m c) -> p m c", m=2)
                    if b == 0:
                        for h in range(H_C):
                            take(pe, l, "o", h)
                            for m in range(2):
                                product(bank(l, "o", h)[:, 0:SEQ], vm[:, m, P * h:P * h + P],
                                        pT[:, h, N_MEM * m:N_MEM * m + SEQ], m, 2)
                    for h in range(H_C):
                        for m in range(2):
                            c = 2 * P * m + 32 * b + DSEQ * h
                            ins = product(bank(l, "o", h)[:, SEQ + DSEQ * b:SEQ + DSEQ * b + DSEQ],
                                          w[:, m, P * h:P * h + P], pT[:, H_C, c:c + DSEQ], m, 2)
                    step(ins)

                pe.wait_ge(conv_a_tap, K_A * (l + 1))
                take(pe, l, "mean", 0)
                for j in range(JA):
                    ins = product(bank(l, "mean", 0)[:, 0:T], ones[:], ca[:, j], j, JA)
                step(ins)
                for br, yk in BRANCHES:
                    for n in range(KT):
                        if br == 2:
                            attend(n)
                        blocks((l, "g", br, n), xTh, xTl, T)
                    if br == 2:
                        pe.wait_ge(dev_ready, l + 1)
                        take(pe, l, "var", 0)
                        for j in range(JA):
                            ins = product(bank(l, "var", 0)[:, 0:T], ones[:], sg[:, j], j, JA)
                        step(ins)
                    if br == 1:
                        pe.wait_ge(hgl_ready, JB * (l + 1))
                        for n in range(KT):
                            blocks((l, "yb", n), hgh, hgl, T)
                        continue
                    if br == 2:
                        for h in range(H_C):
                            emptied(pe, l, "o", h)
                    else:
                        pe.wait_ge(sal_ready, JA * (l + 1))
                    hi, lo = (oTh, oTl) if br == 2 else (sah, sal)
                    for n in range(KT):
                        if n % 2 == 0:
                            h, low = parts(pe, l, yk, n // 2)
                        half = slice(512 * (n % 2), 512 * (n % 2) + 512)
                        blocks((l, yk, n), hi, lo, T, kt=4, unit=(h[:, half], low[:, half]))
                    if br == 2:
                        pe.wait_ge(conv_b_done, 4 * (l + 1))
                        for n in range(2 * JB):
                            if n % JB == 0:
                                w = weights(pe, l, "rg", n // JB)
                            take(pe, l, "rg", n)
                            j = n % JB
                            step(pe.matmul(bank(l, "rg", n)[:, 0:T], w[:, P * j:P * j + P], cb[:, j],
                                           start=True, stop=True))
                for k in range(KT):
                    pe.wait_ge(mgl_ready, KT * l + k + 1)
                    rows_of((l, "mix", k), k, KT, mgh[:, k], mgl[:, k])
                turn_x(l, "xt", 2 * l + 1)
                if l % 2 == 0:
                    for f in range(0, FT, 2):
                        for w in "gu":
                            for n in (f, f + 1):
                                blocks((l, w, n), xTh, xTl, T, turned=KT if (w, n) == ("g", 0) else None)
                    for f in range(FT):
                        pe.wait_ge(dhl_ready, f + 1)
                        rows_of((l, "down", f), f, FT, hTh[:, f], hTl[:, f])
                    turn_x(l, "xt2", 2 * l + 2)
            pe.wait_ge(router_in, 32)
            take(pe, "router")
            for k in range(KT):
                emptied(pe, DEPTH - 1, "xt", k)
                ins = product(bank("router")[0:NE, 0:T], wr[:, k], xT[:, k], k, KT)
            step(ins)
            take(pe, "logits")
            emptied(pe, "router")
            for t, r0 in enumerate(TOK):
                ins = pe.transpose(bank("logits")[:, NE * t:NE * t + NE], lgT[0:NE, r0:r0 + P], ident[0:NE, 0:NE])
            step(ins)
            take(pe, "pos")
            pe.wait_ge(hit_ready, 1)
            for t in range(3):
                for s in range(t + 1):
                    product(bank("pos")[:, NE * t:NE * t + NE], (upper if s == t else ones)[:], hit[:, s], s, t + 1)
            for s in range(3):
                ins = product(bank("pos")[:, 3 * NE:4 * NE], ones[:], hit[:, s], s, 3)
            step(ins)

            def gather(key, i=None):
                for n in range(4):
                    take(pe, *key, n, i=i)
                    for m in range(2):
                        k = 2 * n + m
                        for t in range(3):
                            ins = product(bank(*key, n)[:, CAP * m:CAP * m + CAP], x[:, t, P * k:P * k + P],
                                          pick[:, t, :], t, 3)
                    step(ins)

            pe.wait_ge(pick_ready, 3)
            gather(("gather0",))
            for n in range(4):
                emptied(pe, "gather0", n)

            def turn(i, cap):
                for n in range(4):
                    emptied_before(pe, "e", "gather", n, i=i)
                for f in range(0, FT, 2):
                    for w in "gu":
                        take(pe, "e", w, f // 2, i=i)
                        for n in (f, f + 1):
                            u = weights(pe, "e", w, n, i=i).rearrange("p (k n) -> p k n", n=P)
                            out = bank("e", w, f // 2)[:, CAP * (n - f):CAP * (n - f) + cap]
                            for k in range(KT):
                                ins = product(out, u[:, k], xe[:, k, 0:cap], k, KT)
                            step(ins)
                    if f == 0:
                        for n in range(2):
                            r, g, c, w = pt_place(n, cap)
                            take(pe, "e", "pt", n, i=i)
                            for t in (2, 0, 1):
                                if c <= TOK[t] < c + w:
                                    ins = pe.transpose(bank("e", "pt", n)[0:r, TOK[t]:TOK[t] + P],
                                                       pick[:, t, P * g:P * g + r], ident[:])
                            step(ins)
                pe.wait_ge(pick_ready, i * 3 + 6)
                gather(("e", "gather"), i=i)
                for f in range(FT):
                    u = weights(pe, "e", "down", f, i=i)
                    if f == 0:
                        for n in range(4):
                            take(pe, "e", "down", n, i=i)
                    if f % 2 == 0:
                        emptied(pe, "e", "u", f // 2, i=i)
                    for n in range(KT):
                        ins = pe.matmul(bank("e", "down", n // 2)[:, CAP * (n % 2):CAP * (n % 2) + cap],
                                        u[:, P * n:P * n + P], he[:, f, 0:cap], start=(f == 0 and n % 2 == 0),
                                        stop=(f == FT - 1), skip_group_check=True)
                    step(ins)
                for n in range(4):
                    r, g, c, w = yt_place(n, cap)
                    take(pe, "e", "yt", n, i=i)
                    for k in range(c // P, (c + w) // P):
                        if k % 2 == 0:
                            emptied(pe, "e", "down", k // 2, i=i)
                        ins = pe.transpose(bank("e", "yt", n)[0:r, P * k - c:P * k - c + P],
                                           ye[:, k, P * g:P * g + r], ident[:])
                    step(ins)
                for n in range(2):
                    emptied(pe, "e", "pt", n, i=i)
                for n in range(4):
                    emptied(pe, "e", "yt", n, i=i)
                for n, (t, c, w) in enumerate(Y_TILES):
                    take(pe, "e", "y", n, i=i)
                    for g in range((cap + P - 1) // P):
                        r = min(cap - P * g, P)
                        ins = pe.matmul(bank("e", "y", n)[:, 0:w], pg[0:r, g, TOK[t]:TOK[t] + P],
                                        ys[0:r, g, c:c + w], start=(g == 0), stop=(P * (g + 1) >= cap))
                    step(ins)

            turns(pe, turn)

    return nc


def _blocks(w):
    k, n = w.shape
    return w.reshape(k // P, P, n // P, P).transpose(2, 1, 0, 3).reshape(n // P, P, k)


def _halves(w):
    return w.reshape(4, P, 4, 2, P).transpose(2, 1, 3, 0, 4).reshape(4, P, UNIT)


def _ffn(gate, up, down):
    import numpy as np

    g, u = (_blocks(a).reshape(FT // 2, 2, P, UNIT) for a in (gate, up))
    return np.concatenate([np.concatenate([g, u], 1).reshape(2 * FT, P, UNIT), down.reshape(FT, P, UNIT)])


def _mix_units(a, l):
    import numpy as np

    win = _blocks(a["w_in"][l])
    za = np.stack([win[ZA_U:ZA_U + JA], win[ZA_G:ZA_G + JA]], 1).reshape(2 * JA, P, UNIT)
    kv = a["w_mem_kv"][l]
    v = kv[:, D_C:].reshape(4, 2, P, D_C).transpose(0, 2, 1, 3).reshape(4, P, UNIT)
    ck = a["cache_mem_k"][l].transpose(0, 3, 2, 1).reshape(DEC, P, UNIT)
    cv = a["cache_mem_v"][l].reshape(DEC, 2, P, D_C).transpose(0, 2, 1, 3).reshape(DEC, P, UNIT)
    rg = [a[n][l].transpose(1, 0, 2).reshape(1, P, UNIT) for n in ("w_rg_a", "w_rg_x")]
    mem = a["mem_prompt"][0].T.reshape(2, 4, P, N_MEM).transpose(0, 2, 1, 3).reshape(2, P, UNIT)
    both = lambda x, y: np.stack([x, y], 1).reshape(-1, P, UNIT)
    gate = [win[ZM + KT * br:ZM + KT * br + KT] for br in range(3)]
    return np.concatenate([
        za, mem, win[ZQ:ZQ + JC], _blocks(kv[:, :D_C]), v, both(win[ZB:ZB + JB], ck), win[ZG:ZG + JB],
        both(cv, gate[2]), _halves(a["w_c_out"][l]), *rg, gate[0], _halves(a["w_a_out"][l]), gate[1],
        _blocks(a["w_b_out"][l]), a["w_mix_out"][l].reshape(KT, P, UNIT)])


def _channels(v):
    import numpy as np

    v = np.moveaxis(v, -1, 1)
    return v.reshape(DEPTH, v.shape[1] // P, P, -1).transpose(0, 2, 1, 3).reshape(DEPTH, P, -1)


def kernel(**inputs):
    import numpy as np
    import concourse.bacc as bacc
    from concourse.bass_utils import run_bass_kernel_spmd as run

    a = {k: np.asarray(v) for k, v in inputs.items()}
    x0 = np.concatenate([a["x_prompt"].reshape(SEQ, D), a["x_sample"].reshape(NSAMP, D)])
    feature = lambda v: np.ascontiguousarray(v.T.reshape(KT, P, -1).transpose(1, 0, 2))
    experts = np.concatenate([_ffn(a["w_e_gate"][0, e], a["w_e_up"][0, e], a["w_e_down"][0, e]) for e in range(NE)])
    arrays = {
        "x0": x0,
        "x0T": feature(x0),
        "chan": np.concatenate([_channels(a[n]) for n in COL if n != "lam"] + [_channels(a["lru_lambda"])], 2),
        "rows": np.stack([a["ln1_g"], a["ln1_b"], a["ln2_g"], a["ln2_b"]], 1),
        "hist": np.concatenate([_channels(a["state_conv_a"]), _channels(a["state_conv_b"]),
                                _channels(a["state_rglru"])], 2),
        "stream": np.concatenate([_mix_units(a, 0), _ffn(a["w_ff_gate"][0], a["w_ff_up"][0], a["w_ff_down"][0]),
                                  _mix_units(a, 1)]),
        "router_w": np.ascontiguousarray(a["w_router"][0].reshape(KT, P, NE).transpose(1, 0, 2)),
        "router_b": a["b_router"][0],
        "experts": np.concatenate([experts, experts[:E_SLOTS]]),
    }
    outs = {"y": (T, D), "o_a": (DEPTH, P, JA * 9 * (K_A - 1)), "o_b": (DEPTH, P, JB * 9 * (K_B - 1)),
            "o_h": (DEPTH, P, JB * 9), "o_k": (DEPTH, P, H_C, N_MEM), "o_v": (DEPTH, P, 2, D_C)}
    nc = bacc.Bacc("TRN2", target_bir_lowering=False, num_devices=1)
    args = [nc.dram_tensor(n, v.shape, F32, kind="ExternalInput").ap() for n, v in arrays.items()]
    args += [nc.dram_tensor(n, s, F32, kind="ExternalOutput").ap() for n, s in outs.items()]
    trunk(nc, *args)
    r = run(nc, [arrays], core_ids=[0]).results[0]
    ca = r["o_a"].reshape(DEPTH, P, JA, 9, K_A - 1).transpose(0, 3, 4, 2, 1).reshape(DEPTH, 9, K_A - 1, D_A)
    cb = r["o_b"].reshape(DEPTH, P, JB, 9, K_B - 1).transpose(0, 3, 4, 2, 1).reshape(DEPTH, 9, K_B - 1, D_B)
    h = r["o_h"].reshape(DEPTH, P, JB, 9).transpose(0, 3, 2, 1).reshape(DEPTH, 9, D_B)
    mk = r["o_k"].transpose(0, 3, 2, 1).reshape(DEPTH, 1, N_MEM, H_C, P)
    mv = r["o_v"].transpose(0, 2, 1, 3).reshape(DEPTH, 1, N_MEM, H_C, P)
    y = r["y"]
    return (y[:SEQ].reshape(1, SEQ, D), y[SEQ:].reshape(DEC, DSEQ, D), ca[:, :1], cb[:, :1], h[:, :1], mk, mv,
            ca[:, 1:], cb[:, 1:], h[:, 1:])
```
